# Optimizing a Trainium2 kernel written in Bass

```python
import math
import jax, jax.numpy as jnp
from jax import lax
import numpy as np

D_MODEL = 1024
BATCH = 1
SEQ = 256
DEPTH = 2
DEC_BATCH = 8
DEC_SEQ = 8
PAST_LEN = 1024
PAGE_SIZE = 128

N_EVEN = (DEPTH + 1) // 2
N_ODD = DEPTH // 2
ALPHA = (2.0 * DEPTH) ** 0.25
BETA = (8.0 * DEPTH) ** -0.25
D_FF = 2816
ROPE_BASE = 10000.0
MLA_HEADS = 8
MLA_Q_RANK = 256
MLA_KV_RANK = 128
MLA_NOPE = 64
MLA_ROPE = 32
MLA_V = 64
Q_BLOCK = 128
RET_HEADS = 4
RET_DK = 64
RET_DV = 128
RET_CHUNK = 64
GLA_HEADS = 4
GLA_DK = 64
GLA_DV = 128
GLA_GATE_RANK = 16
GLA_TAU = 16.0
GLA_CHUNK = 64
SSM_HEADS = 16
SSM_HEADDIM = 64
SSM_GROUPS = 2
SSM_DSTATE = 128
SSM_CONV = 4
SSM_CHUNK = 64
SSM_INNER = SSM_HEADS * SSM_HEADDIM
SSM_CONV_DIM = SSM_INNER + 2 * SSM_GROUPS * SSM_DSTATE

EVEN_SPLITS = (MLA_Q_RANK, MLA_KV_RANK, MLA_ROPE, RET_HEADS * RET_DK, RET_HEADS * RET_DK, RET_HEADS * RET_DV, RET_HEADS * RET_DV)
EVEN_IN = sum(EVEN_SPLITS)
EVEN_MIX = MLA_HEADS * MLA_V + RET_HEADS * RET_DV
ODD_SPLITS = (GLA_HEADS * GLA_DK, GLA_HEADS * GLA_DK, GLA_HEADS * GLA_DV, GLA_GATE_RANK, GLA_HEADS * GLA_DV, SSM_INNER, SSM_CONV_DIM, SSM_HEADS)
ODD_IN = sum(ODD_SPLITS)
ODD_MIX = GLA_HEADS * GLA_DV + SSM_INNER

kernel_name = 'hybrid_mla_retnet_gla_ssd_step'

def layer_norm(x, g, b, eps=1e-5):
    xf = x.astype(jnp.float32)
    mu = jnp.mean(xf, axis=-1, keepdims=True)
    var = jnp.mean(jnp.square(xf - mu), axis=-1, keepdims=True)
    return ((xf - mu) * lax.rsqrt(var + eps) * g.astype(jnp.float32) + b.astype(jnp.float32)).astype(x.dtype)

def rms_norm(x, g, eps=1e-6):
    xf = x.astype(jnp.float32)
    return (xf * lax.rsqrt(jnp.mean(jnp.square(xf), axis=-1, keepdims=True) + eps) * g.astype(jnp.float32)).astype(x.dtype)

def split_cols(x, sizes):
    return jnp.split(x, np.cumsum(sizes)[:-1].tolist(), axis=-1)

def rope(x, pos):
    half = x.shape[-1] // 2
    inv = ROPE_BASE ** (-jnp.arange(half, dtype=jnp.float32) / half)
    ang = pos.astype(jnp.float32)[:, None] * inv[None, :]
    cos, sin = jnp.cos(ang)[:, None, :], jnp.sin(ang)[:, None, :]
    x1 = x[..., :half].astype(jnp.float32)
    x2 = x[..., half:].astype(jnp.float32)
    return jnp.concatenate([x1 * cos - x2 * sin, x1 * sin + x2 * cos], axis=-1).astype(x.dtype)

def swiglu(h, w1, w3, w2):
    return (jax.nn.silu(h @ w1) * (h @ w3)) @ w2

def modulate(x, ada_i):
    return x * (1 + ada_i[:, 1, None]) + ada_i[:, 0, None]

def to_chunks(a, chunk):
    B, T = a.shape[:2]
    return jnp.moveaxis(a.reshape(B, T // chunk, chunk, *a.shape[2:]), 1, 0)

def chunked_scalar_decay(q, k, v, log_a, s0, chunk):
    B, T, H, K = q.shape
    V = v.shape[-1]
    f32 = jnp.float32
    causal = jnp.tril(jnp.ones((chunk, chunk), bool))

    def step(s, inp):
        qi, ki, vi, ai = inp
        seg = jnp.cumsum(ai, axis=1)
        segh = jnp.moveaxis(seg, 2, 1)
        diff = segh[..., :, None] - segh[..., None, :]
        decay = jnp.exp(jnp.where(causal, diff, -jnp.inf))
        scores = jnp.einsum('bthk,bjhk->bhtj', qi, ki) * decay
        o = jnp.einsum('bhtj,bjhv->bthv', scores, vi) + jnp.einsum('bthk,bhkv->bthv', qi * jnp.exp(seg)[..., None], s)
        tail = jnp.exp(seg[:, -1:] - seg)
        s_new = jnp.exp(seg[:, -1])[:, :, None, None] * s + jnp.einsum('bjhk,bjhv->bhkv', ki * tail[..., None], vi)
        return s_new, o

    xs = tuple(to_chunks(a.astype(f32), chunk) for a in (q, k, v, log_a))
    s_fin, o = lax.scan(step, s0.astype(f32), xs)
    return jnp.moveaxis(o, 0, 1).reshape(B, T, H, V).astype(v.dtype), s_fin

def chunked_vector_decay(q, k, v, log_a, s0, chunk):
    B, T, H, K = q.shape
    V = v.shape[-1]
    f32 = jnp.float32
    causal = jnp.tril(jnp.ones((chunk, chunk), bool))[None, :, :, None, None]

    def step(s, inp):
        qi, ki, vi, ai = inp
        seg = jnp.cumsum(ai, axis=1)
        diff = seg[:, :, None] - seg[:, None, :]
        decay = jnp.exp(jnp.where(causal, diff, -jnp.inf))
        scores = jnp.einsum('bthk,bjhk,btjhk->bhtj', qi, ki, decay)
        o = jnp.einsum('bhtj,bjhv->bthv', scores, vi) + jnp.einsum('bthk,bhkv->bthv', qi * jnp.exp(seg), s)
        tail = jnp.exp(seg[:, -1:] - seg)
        s_new = jnp.exp(seg[:, -1])[..., None] * s + jnp.einsum('bjhk,bjhv->bhkv', ki * tail, vi)
        return s_new, o

    xs = tuple(to_chunks(a.astype(f32), chunk) for a in (q, k, v, log_a))
    s_fin, o = lax.scan(step, s0.astype(f32), xs)
    return jnp.moveaxis(o, 0, 1).reshape(B, T, H, V).astype(v.dtype), s_fin

def mla_prompt(q_lat, q_rope, lat, k_rope):
    B, T, H, R = q_lat.shape
    blk = math.gcd(T, Q_BLOCK)
    nb = T // blk
    scale = (MLA_NOPE + MLA_ROPE) ** -0.5
    key_pos = jnp.arange(T)

    def one_block(args):
        ql, qr, start = args
        s = (jnp.einsum('bthr,bsr->bhts', ql, lat) + jnp.einsum('bthe,bse->bhts', qr, k_rope)).astype(jnp.float32) * scale
        q_pos = start + jnp.arange(blk)
        s = jnp.where(key_pos[None, :] <= q_pos[:, None], s, -jnp.inf)
        prob = jax.nn.softmax(s, axis=-1).astype(lat.dtype)
        return jnp.einsum('bhts,bsr->bthr', prob, lat)

    o = lax.map(one_block, (to_chunks(q_lat, blk), to_chunks(q_rope, blk), jnp.arange(nb) * blk))
    return jnp.moveaxis(o, 0, 1).reshape(B, T, H, R)

def mla_sample(q_lat, q_rope, lat, k_rope, past_lat, past_rope):
    T = q_lat.shape[1]
    P = past_lat.shape[1]
    scale = (MLA_NOPE + MLA_ROPE) ** -0.5
    s_past = jnp.einsum('bthr,bsr->bhts', q_lat, past_lat) + jnp.einsum('bthe,bse->bhts', q_rope, past_rope)
    s_new = jnp.einsum('bthr,bsr->bhts', q_lat, lat) + jnp.einsum('bthe,bse->bhts', q_rope, k_rope)
    s_new = jnp.where(jnp.tril(jnp.ones((T, T), bool)), s_new.astype(jnp.float32), -jnp.inf)
    s = jnp.concatenate([s_past.astype(jnp.float32), s_new], axis=-1) * scale
    prob = jax.nn.softmax(s, axis=-1).astype(lat.dtype)
    return jnp.einsum('bhts,bsr->bthr', prob[..., :P], past_lat) + jnp.einsum('bhts,bsr->bthr', prob[..., P:], lat)

def even_mixer(h, pos, j, p, ret_s0, past_lat, past_rope):
    B, T, _ = h.shape
    c_q, c_kv, k_rope_raw, rq, rk, rv, rg = split_cols(h @ p['w_in_even'][j], EVEN_SPLITS)
    q = (rms_norm(c_q, p['mla_q_norm'][j]) @ p['w_uq'][j]).reshape(B, T, MLA_HEADS, MLA_NOPE + MLA_ROPE)
    q_nope, q_rope = q[..., :MLA_NOPE], rope(q[..., MLA_NOPE:], pos)
    lat = rms_norm(c_kv, p['mla_kv_norm'][j])
    k_rope = rope(k_rope_raw[:, :, None, :], pos)[:, :, 0]
    q_lat = jnp.einsum('bthn,rhn->bthr', q_nope, p['w_uk'][j])
    if past_lat is None:
        o_lat = mla_prompt(q_lat, q_rope, lat, k_rope)
    else:
        o_lat = mla_sample(q_lat, q_rope, lat, k_rope, past_lat, past_rope)
    mla_out = jnp.einsum('bthr,rhv->bthv', o_lat, p['w_uv'][j]).reshape(B, T, MLA_HEADS * MLA_V)
    rq = rope(rq.reshape(B, T, RET_HEADS, RET_DK), pos)
    rk = rope(rk.reshape(B, T, RET_HEADS, RET_DK), pos) * RET_DK ** -0.5
    rv = rv.reshape(B, T, RET_HEADS, RET_DV)
    log_gamma = jnp.log1p(-jnp.exp2(-5.0 - jnp.arange(RET_HEADS, dtype=jnp.float32)))
    log_a = jnp.broadcast_to(log_gamma, (B, T, RET_HEADS))
    ro, ret_s = chunked_scalar_decay(rq, rk, rv, log_a, ret_s0, math.gcd(T, RET_CHUNK))
    ret_out = jax.nn.silu(rg) * rms_norm(ro, p['ret_norm'][j]).reshape(B, T, RET_HEADS * RET_DV)
    out = jnp.concatenate([mla_out, ret_out], axis=-1) @ p['w_out_even'][j]
    return out, lat, k_rope, ret_s

def odd_mixer(h, j, p, gla_s0, ssm_s0, conv0):
    B, T, _ = h.shape
    gq, gk, gv, g_lr, gr, z, xbc, dt_raw = split_cols(h @ p['w_in_odd'][j], ODD_SPLITS)
    gq = gq.reshape(B, T, GLA_HEADS, GLA_DK) * GLA_DK ** -0.5
    gk = gk.reshape(B, T, GLA_HEADS, GLA_DK)
    gv = gv.reshape(B, T, GLA_HEADS, GLA_DV)
    gate_pre = (g_lr @ p['gla_w_gate'][j] + p['gla_b_gate'][j]).astype(jnp.float32)
    log_a = (jax.nn.log_sigmoid(gate_pre) / GLA_TAU).reshape(B, T, GLA_HEADS, GLA_DK)
    go, gla_s = chunked_vector_decay(gq, gk, gv, log_a, gla_s0, math.gcd(T, GLA_CHUNK))
    gla_out = jax.nn.silu(gr) * rms_norm(go, p['gla_norm'][j]).reshape(B, T, GLA_HEADS * GLA_DV)
    xpad = jnp.concatenate([conv0.astype(xbc.dtype), xbc], axis=1)
    cw = p['ssm_conv_w'][j]
    conv = p['ssm_conv_b'][j] + sum(xpad[:, i:i + T] * cw[i] for i in range(SSM_CONV))
    conv_state = xpad[:, T:]
    xs, bm, cm = split_cols(jax.nn.silu(conv), (SSM_INNER, SSM_GROUPS * SSM_DSTATE, SSM_GROUPS * SSM_DSTATE))
    xs = xs.reshape(B, T, SSM_HEADS, SSM_HEADDIM)
    rep = SSM_HEADS // SSM_GROUPS
    bm = jnp.repeat(bm.reshape(B, T, SSM_GROUPS, SSM_DSTATE), rep, axis=2)
    cm = jnp.repeat(cm.reshape(B, T, SSM_GROUPS, SSM_DSTATE), rep, axis=2)
    dt = jax.nn.softplus((dt_raw + p['ssm_dt_bias'][j]).astype(jnp.float32))
    a = -jnp.exp(p['ssm_a_log'][j].astype(jnp.float32))
    y, ssm_s = chunked_scalar_decay(cm, bm, xs * dt[..., None].astype(xs.dtype), dt * a, ssm_s0, math.gcd(T, SSM_CHUNK))
    y = y + p['ssm_d'][j][:, None] * xs
    y = (y * jax.nn.silu(z.reshape(B, T, SSM_HEADS, SSM_HEADDIM))).reshape(B, T, SSM_GROUPS, SSM_INNER // SSM_GROUPS)
    y = rms_norm(y, p['ssm_norm'][j].reshape(SSM_GROUPS, SSM_INNER // SSM_GROUPS)).reshape(B, T, SSM_INNER)
    out = jnp.concatenate([gla_out, y], axis=-1) @ p['w_out_odd'][j]
    return out, gla_s, ssm_s, conv_state

def run_trunk(x, c, pos, p, ret_s0, gla_s0, ssm_s0, conv0, past_lat, past_rope, page_table):
    B, T, D = x.shape
    lat_l, rope_l, ret_l, gla_l, ssm_l, conv_l = [], [], [], [], [], []
    sc = jax.nn.silu(c)
    for l in range(DEPTH):
        ada = (sc @ p['w_ada'][l] + p['b_ada'][l]).reshape(B, 3, 3, D)
        f = swiglu(modulate(x, ada[:, 0]), p['ffn_w1'][l, 0], p['ffn_w3'][l, 0], p['ffn_w2'][l, 0])
        x = layer_norm(ALPHA * x + 0.5 * ada[:, 0, 2, None] * f, p['ln_g'][l, 0], p['ln_b'][l, 0])
        h = modulate(x, ada[:, 1])
        j = l // 2
        if l % 2 == 0:
            if past_lat is None:
                pl, pr = None, None
            else:
                pl = past_lat[j][page_table].reshape(B, -1, MLA_KV_RANK)
                pr = past_rope[j][page_table].reshape(B, -1, MLA_ROPE)
            mix, lat, kr, rs = even_mixer(h, pos, j, p, ret_s0[j], pl, pr)
            lat_l.append(lat)
            rope_l.append(kr)
            ret_l.append(rs)
        else:
            mix, gs, ss, cs = odd_mixer(h, j, p, gla_s0[j], ssm_s0[j], conv0[j])
            gla_l.append(gs)
            ssm_l.append(ss)
            conv_l.append(cs)
        x = layer_norm(ALPHA * x + ada[:, 1, 2, None] * mix, p['ln_g'][l, 1], p['ln_b'][l, 1])
        f = swiglu(modulate(x, ada[:, 2]), p['ffn_w1'][l, 1], p['ffn_w3'][l, 1], p['ffn_w2'][l, 1])
        x = layer_norm(ALPHA * x + 0.5 * ada[:, 2, 2, None] * f, p['ln_g'][l, 2], p['ln_b'][l, 2])
    return x, jnp.stack(lat_l), jnp.stack(rope_l), jnp.stack(ret_l), jnp.stack(gla_l), jnp.stack(ssm_l), jnp.stack(conv_l)

def setup_inputs(seed: int = 0) -> dict:
    key = jax.random.key(seed)
    k = jax.random.split(key, 40)
    f32 = jnp.float32
    D = D_MODEL

    def nrm(i, shape, scale):
        return jax.random.normal(k[i], shape, f32) * scale

    n_pages = PAST_LEN // PAGE_SIZE
    n_used = DEC_BATCH * n_pages
    n_pool = n_used + n_used // 4
    page_table = jax.random.permutation(k[6], n_pool)[:n_used].reshape(DEC_BATCH, n_pages).astype(jnp.int32)
    dt0 = jnp.exp(jax.random.uniform(k[32], (N_ODD, SSM_HEADS), f32, math.log(1e-3), math.log(1e-1)))
    dt_bias = dt0 + jnp.log(-jnp.expm1(-dt0))
    a_log = jnp.log(jax.random.uniform(k[33], (N_ODD, SSM_HEADS), f32, 1.0, 16.0))
    return {
        'x_prompt': nrm(0, (BATCH, SEQ, D), 1.0),
        'x_sample': nrm(1, (DEC_BATCH, DEC_SEQ, D), 1.0),
        'cache_mla_latent': nrm(4, (N_EVEN, n_pool, PAGE_SIZE, MLA_KV_RANK), 1.0),
        'cache_mla_krope': nrm(5, (N_EVEN, n_pool, PAGE_SIZE, MLA_ROPE), 1.0),
        'page_table': page_table,
        'state_retention': nrm(7, (N_EVEN, DEC_BATCH, RET_HEADS, RET_DK, RET_DV), 0.5),
        'state_gla': nrm(8, (N_ODD, DEC_BATCH, GLA_HEADS, GLA_DK, GLA_DV), 0.5),
        'state_ssm': nrm(9, (N_ODD, DEC_BATCH, SSM_HEADS, SSM_DSTATE, SSM_HEADDIM), 0.5),
        'state_conv': nrm(10, (N_ODD, DEC_BATCH, SSM_CONV - 1, SSM_CONV_DIM), 1.0),
        'c_prompt': nrm(2, (BATCH, D), 1.0),
        'c_sample': nrm(3, (DEC_BATCH, D), 1.0),
        'w_ada': nrm(11, (DEPTH, D, 9 * D), D ** -0.5),
        'b_ada': nrm(12, (DEPTH, 9 * D), 0.02),
        'ln_g': 1.0 + nrm(13, (DEPTH, 3, D), 0.02),
        'ln_b': nrm(14, (DEPTH, 3, D), 0.02),
        'ffn_w1': nrm(15, (DEPTH, 2, D, D_FF), D ** -0.5),
        'ffn_w3': nrm(16, (DEPTH, 2, D, D_FF), D ** -0.5),
        'ffn_w2': nrm(17, (DEPTH, 2, D_FF, D), BETA * D_FF ** -0.5),
        'w_in_even': nrm(18, (N_EVEN, D, EVEN_IN), D ** -0.5),
        'mla_q_norm': 1.0 + nrm(19, (N_EVEN, MLA_Q_RANK), 0.02),
        'w_uq': nrm(20, (N_EVEN, MLA_Q_RANK, MLA_HEADS * (MLA_NOPE + MLA_ROPE)), MLA_Q_RANK ** -0.5),
        'mla_kv_norm': 1.0 + nrm(21, (N_EVEN, MLA_KV_RANK), 0.02),
        'w_uk': nrm(22, (N_EVEN, MLA_KV_RANK, MLA_HEADS, MLA_NOPE), MLA_KV_RANK ** -0.5),
        'w_uv': nrm(23, (N_EVEN, MLA_KV_RANK, MLA_HEADS, MLA_V), MLA_KV_RANK ** -0.5),
        'ret_norm': 1.0 + nrm(24, (N_EVEN, RET_DV), 0.02),
        'w_out_even': nrm(25, (N_EVEN, EVEN_MIX, D), BETA * EVEN_MIX ** -0.5),
        'w_in_odd': nrm(26, (N_ODD, D, ODD_IN), D ** -0.5),
        'gla_w_gate': nrm(27, (N_ODD, GLA_GATE_RANK, GLA_HEADS * GLA_DK), GLA_GATE_RANK ** -0.5),
        'gla_b_gate': nrm(28, (N_ODD, GLA_HEADS * GLA_DK), 0.1),
        'gla_norm': 1.0 + nrm(29, (N_ODD, GLA_DV), 0.02),
        'ssm_conv_w': nrm(30, (N_ODD, SSM_CONV, SSM_CONV_DIM), SSM_CONV ** -0.5),
        'ssm_conv_b': nrm(31, (N_ODD, SSM_CONV_DIM), 0.02),
        'ssm_dt_bias': dt_bias,
        'ssm_a_log': a_log,
        'ssm_d': 1.0 + nrm(34, (N_ODD, SSM_HEADS), 0.02),
        'ssm_norm': 1.0 + nrm(35, (N_ODD, SSM_INNER), 0.02),
        'w_out_odd': nrm(36, (N_ODD, ODD_MIX, D), BETA * ODD_MIX ** -0.5),
    }

def reference(x_prompt, x_sample, cache_mla_latent, cache_mla_krope, page_table, state_retention, state_gla, state_ssm, state_conv, c_prompt, c_sample, w_ada, b_ada, ln_g, ln_b, ffn_w1, ffn_w3, ffn_w2, w_in_even, mla_q_norm, w_uq, mla_kv_norm, w_uk, w_uv, ret_norm, w_out_even, w_in_odd, gla_w_gate, gla_b_gate, gla_norm, ssm_conv_w, ssm_conv_b, ssm_dt_bias, ssm_a_log, ssm_d, ssm_norm, w_out_odd):
    p = {'w_ada': w_ada, 'b_ada': b_ada, 'ln_g': ln_g, 'ln_b': ln_b,
         'ffn_w1': ffn_w1, 'ffn_w3': ffn_w3, 'ffn_w2': ffn_w2,
         'w_in_even': w_in_even, 'mla_q_norm': mla_q_norm, 'w_uq': w_uq, 'mla_kv_norm': mla_kv_norm,
         'w_uk': w_uk, 'w_uv': w_uv, 'ret_norm': ret_norm, 'w_out_even': w_out_even,
         'w_in_odd': w_in_odd, 'gla_w_gate': gla_w_gate, 'gla_b_gate': gla_b_gate, 'gla_norm': gla_norm,
         'ssm_conv_w': ssm_conv_w, 'ssm_conv_b': ssm_conv_b, 'ssm_dt_bias': ssm_dt_bias,
         'ssm_a_log': ssm_a_log, 'ssm_d': ssm_d, 'ssm_norm': ssm_norm, 'w_out_odd': w_out_odd}
    f32 = jnp.float32
    bp, tp = x_prompt.shape[:2]
    past_len = page_table.shape[1] * PAGE_SIZE
    pos_p = jnp.arange(tp, dtype=jnp.int32)
    pos_s = past_len + jnp.arange(x_sample.shape[1], dtype=jnp.int32)
    ret0 = jnp.zeros((N_EVEN, bp, RET_HEADS, RET_DK, RET_DV), f32)
    gla0 = jnp.zeros((N_ODD, bp, GLA_HEADS, GLA_DK, GLA_DV), f32)
    ssm0 = jnp.zeros((N_ODD, bp, SSM_HEADS, SSM_DSTATE, SSM_HEADDIM), f32)
    conv0 = jnp.zeros((N_ODD, bp, SSM_CONV - 1, SSM_CONV_DIM), x_prompt.dtype)
    y_prompt, lat_p, krope_p, ret_p, gla_p, ssm_p, conv_p = run_trunk(
        x_prompt, c_prompt, pos_p, p, ret0, gla0, ssm0, conv0, None, None, None)
    y_sample, lat_s, krope_s, ret_s, gla_s, ssm_s, conv_s = run_trunk(
        x_sample, c_sample, pos_s, p, state_retention, state_gla, state_ssm, state_conv,
        cache_mla_latent, cache_mla_krope, page_table)
    return (y_prompt, y_sample, lat_p, lat_s, krope_p, krope_s, ret_p, ret_s, gla_p, gla_s, ssm_p, ssm_s, conv_p, conv_s)


_drawn_inputs = setup_inputs


def setup_inputs(seed=0):
    import zlib

    import numpy as np

    out = dict(_drawn_inputs(seed))
    spreads = {}
    factors = {'cache_mla_latent': 5.4,
     'cache_mla_krope': 8.0,
     'mla_q_norm': 8.0,
     'mla_kv_norm': 2.777,
     'ret_norm': 23.02,
     'gla_norm': 53.091,
     'ssm_d': 41.582,
     'ssm_norm': 32.418,
     'ssm_conv_b': 2.678}
    for name, (base, spread) in spreads.items():
        noise = np.random.default_rng([zlib.crc32(name.encode()), seed]).standard_normal(out[name].shape)
        drawn = base * np.exp(spread * noise) if base else spread * noise
        out[name] = __import__('jax').numpy.asarray(drawn.astype(out[name].dtype))
    for name, factor in factors.items():
        out[name] = (out[name] * factor).astype(out[name].dtype)
    return out
```

```python
from contextlib import ExitStack

import concourse.bass as bass
from concourse import mybir
import numpy as np

F32 = mybir.dt.float32
F32R = mybir.dt.float32r
U32 = mybir.dt.uint32
I32 = mybir.dt.int32
ALU = mybir.AluOpType
ACT = mybir.ActivationFunctionType
AX_X = mybir.AxisListType.X

P = 128
D = 1024
KD = D // P
TP, NSEQ, TS = 256, 8, 8
T = TP + NSEQ * TS
NC = 1 + NSEQ
FF = 2816
KF = FF // P
DEPTH = 2
NBLK = 3 * DEPTH
ALPHA = (2.0 * DEPTH) ** 0.25
LN_EPS = 1e-5 / ALPHA ** 2

RING = 3
ARENA = 27300
SLOT = 4096
N_ADA = 3 * D // 512
N_UP = KF // 2
N_DOWN = KD
N_FFN = N_UP + N_DOWN
UNIT = SLOT // 2
N_IN = {1: 4, 4: 8}
N_OUT = {1: 2, 4: 4}
MIXERS = (1, 4)
N_PAST = {1: 8, 4: 0}

N_STORES = 2 + 1

OUT_TILE0 = {1: 0, 4: KD - N_OUT[1]}

ADA0, BODY0 = [], []
_n = 0
for _i in range(NBLK):
    ADA0.append(_n)
    _n += N_ADA
    BODY0.append(_n)
    _n += N_IN[_i] + N_PAST[_i] + N_OUT[_i] if _i in MIXERS else N_UP + N_DOWN
N_SLOTS = _n
OUT0 = {i: BODY0[i] + N_IN[i] + N_PAST[i] for i in MIXERS}
PAST0 = BODY0[MIXERS[0]] + N_IN[MIXERS[0]]

BANK_DOWN = (4, 5, 6)
BANKS_IN = (1, 2, 4, 5)
BANK_MEAN, BANK_MSQ, BANK_ADA = 7, 3, 0
BANK_RAW = (1, 2)
WIDE = 96


HM, RANK, NOPE, ROPE, VM = 8, 128, 64, 32, 64
QRANK = 256
HR, DKR, DVR = 4, 64, 128
PAGE, NPAGES = 128, 8
PAST = PAGE * NPAGES
ATT_SCALE = (NOPE + ROPE) ** -0.5
RMS_EPS = 1e-6
NTOK = 3
NS = NSEQ * TS
TOK = ((0, P), (P, P), (TP, NS))
GAMMA = 1.0 - np.exp2(-5.0 - np.arange(HR))
MASKED = -1e30


def packed(widths):
    at, out = 0, {}
    for name, width in widths:
        out[name] = (at, width)
        at += width
    return out, at


EVEN_CONSTS, N_EVEN_CONSTS = packed([
    ("w_uq", 2 * HM * (NOPE + ROPE)), ("w_uk", HM // 2 * RANK), ("w_uv", HM * VM),
    ("q_norm", 2), ("kv_norm", 1), ("ret_norm", 1),
    ("cos_m", T), ("sin_m", T), ("cos_r", T), ("sin_r", T), ("swap_m", P), ("swap_r", P), ("place", 2 * P),
    ("mask_p", 3 * P), ("mask_s", NSEQ // 2 * NS), ("decay_p", HR * 3 * P), ("decay_s", HR * NS),
    ("tail", NTOK * HR), ("lead", HR * TS), ("rows", 4)])


def even_constants():
    f = np.float32
    out = {}
    pos = np.concatenate([np.arange(TP), PAST + np.tile(np.arange(TS), NSEQ)]).astype(f)

    def rotary(width, copies):
        half = width // 2
        inv = (f(10000.0) ** (-np.arange(half, dtype=f) / f(half))).astype(f)
        ang = (pos[None, :] * inv[:, None]).astype(f)
        cos, sin = np.cos(ang).astype(f), np.sin(ang).astype(f)
        return np.tile(np.concatenate([cos, cos]), (copies, 1)), np.tile(np.concatenate([-sin, sin]), (copies, 1))
    out["cos_m"], out["sin_m"] = rotary(ROPE, P // ROPE)
    out["cos_r"], out["sin_r"] = rotary(DKR, P // DKR)
    i = np.arange(P)

    def swap(width):
        m = np.zeros((P, P), f)
        m[i, i // width * width + (i % width + width // 2) % width] = 1.0
        return m
    out["swap_m"], out["swap_r"] = swap(ROPE), swap(DKR)
    place = np.zeros((P, 2, P), f)
    place[i % ROPE, 0, i] = 1.0
    place[(i % ROPE + ROPE // 2) % ROPE, 1, i] = 1.0
    out["place"] = place.reshape(P, -1)
    later = np.where(i[None, :] > i[:, None], f(MASKED), f(0))
    out["mask_p"] = np.concatenate([later, np.zeros((P, P), f), later], 1)
    row_seq, row_t = i // 64, i % TS
    col = np.arange(NS)
    mask_s = np.full((P, NSEQ // 2, NS), MASKED, f)
    for p in range(NSEQ // 2):
        seen = (col[None, :] // TS == 2 * p + row_seq[:, None]) & (col[None, :] % TS <= row_t[:, None])
        mask_s[:, p][seen] = 0.0
    out["mask_s"] = mask_s.reshape(P, -1)
    step = i[None, :] - i[:, None]
    decay_p = np.zeros((P, HR, 3, P))
    decay_s = np.zeros((P, HR, NS))
    tail = np.zeros((P, NTOK, HR))
    lead = np.zeros((P, HR, TS))
    same = (col[:, None] // TS == col[None, :] // TS) & (col[:, None] <= col[None, :])
    for h in range(HR):
        g = GAMMA[h]
        diag = np.where(step >= 0, g ** np.maximum(step, 0), 0.0)
        decay_p[:, h, 0] = decay_p[:, h, 2] = diag
        decay_p[:, h, 1] = g ** (step + P)
        decay_s[:NS, h] = np.where(same, g ** np.maximum(col[None, :] - col[:, None], 0), 0.0)
        tail[:, 0, h], tail[:, 1, h] = g ** (TP - 1 - i), g ** (P - 1 - i)
        tail[:NS, 2, h] = g ** (TS - 1 - col % TS)
        lead[64 * (h % 2):64 * (h % 2) + 64, h] = g ** (1 + np.arange(TS))
    out["decay_p"], out["decay_s"] = decay_p.reshape(P, -1), decay_s.reshape(P, -1)
    out["tail"], out["lead"] = tail.reshape(P, -1), lead.reshape(P, -1)
    out["rows"] = (i[:, None] // ROPE == np.arange(4)[None, :])
    return {k: v.astype(f) for k, v in out.items()}


GATE_RANK, TAU = 16, 16.0
HS, HDIM, GROUPS, DSTATE, CONV = 16, 64, 2, 128, 4
INNER = HS * HDIM
NXS, NXC = INNER // P, (INNER + 2 * GROUPS * DSTATE) // P
WP = CONV - 1 + TP
WS = CONV - 1 + TS
PADDED = WP + NSEQ * WS
CONV_OUT = PADDED - (CONV - 1)
HALVES = (64, 32, 16, 8, 4, 2, 1, 0)
ODD_CONSTS, N_ODD_CONSTS = packed([
    ("w_small", KD * 2 * GATE_RANK), ("w_gate", HR * DKR), ("b_gate", 2), ("gla_norm", 1),
    ("conv_w", CONV * NXC), ("conv_b", NXC), ("dt_bias", HS), ("a_log", HS), ("d_skip", NXS), ("ssm_norm", NXS),
    ("restart", T), ("levels", len(HALVES) * P), ("upto", P), ("upto_s", NS), ("after", P), ("after_s", NS),
    ("head_rows", 2)])


def odd_constants():
    i = np.arange(P)
    out = {}
    restart = np.ones((P, T))
    restart[:, [0, P, *range(TP, T, TS)]] = 0.0
    out["restart"] = restart
    levels = np.zeros((P, len(HALVES), P))
    for n, half in enumerate(HALVES):
        if half:
            b = i // (2 * half)
            levels[:, n] = (b[:, None] == b[None, :]) & (i[:, None] % (2 * half) < half) & (i[None, :] % (2 * half) >= half)
        else:
            levels[:, n] = np.eye(P)
    out["levels"] = levels
    out["upto"] = i[:, None] <= i[None, :]
    out["after"] = i[:, None] > i[None, :]
    same = i[:, None] // TS == i[None, :NS] // TS
    out["upto_s"] = (i[:, None] <= i[None, :NS]) & same
    out["after_s"] = (i[:, None] > i[None, :NS]) & same
    out["head_rows"] = i[:, None] // DKR == np.arange(2)[None, :]
    return {k: v.astype(np.float32) for k, v in out.items()}


def param_columns():
    at, out = 0, {}
    for name, width in (("ln_g", NBLK * KD), ("ln_b", NBLK * KD), ("b_ada", NBLK * 24), ("c", KD * NC)):
        out[name] = (at, width)
        at += width
    return out, at


def ffn_index(i):
    return [j for j in range(NBLK) if j not in MIXERS].index(i)


def build(nc, d):
    ctx = ExitStack()
    with ctx:
        def sb(name, shape, dt=F32):
            return ctx.enter_context(nc.sbuf_tensor(name, shape, dt))

        def sem(name):
            return ctx.enter_context(nc.semaphore(name))

        ring = sb("ring", [P, RING, SLOT])
        x = sb("x", [P, KD, T])
        y = sb("y", [P, KD, T])
        sq = sb("sq", [P, 3, T])
        ysum = sb("ysum", [P, T])
        sqsum = sb("sqsum", [P, T])
        mean2 = sb("mean2", [P, T])
        var = sb("var", [P, T])
        rstd = sb("rstd", [P, T])
        silu_g = sb("silu_g", [P, 2, T])
        gated = sb("gated", [P, 3, NSEQ, TS])
        cols, n_params = param_columns()
        params = sb("params", [P, n_params])
        sc = sb("sc", [P, KD, 32])
        ada_raw = sb("ada_raw", [P, 2, 512])
        add_turn = sb("add_turn", [P, WIDE])
        ada = sb("ada", [P, 24, NC])
        modA = sb("modA", [P, KD, NC])
        modB = sb("modB", [P, KD, NC])
        gate = sb("gate", [P, KD, NC])
        ones_d = sb("ones_d", [P, P])
        eps_rms = sb("eps_rms", [P, 1])
        ident = sb("ident", [P, P])
        sample_of = sb("sample_of", [P, NSEQ])
        pages = sb("pages", [1, NSEQ * NPAGES], I32)
        stat = sb("stat", [P, 4, 2])
        with nc.sbuf_tensor("h", [P, KD, T], F32) as h, nc.sbuf_tensor("arena", [P, ARENA], F32) as arena:
            pass
        ps = [ctx.enter_context(nc.psum_tensor(f"ps{b}", [P, 512], F32)) for b in range(8)]

        def param(name, *shape):
            at, width = cols[name]
            v = params[:, at:at + width]
            return v.rearrange("p (a b) -> p a b", b=shape[-1]) if shape else v

        ln_g, ln_b = param("ln_g", KD), param("ln_b", KD)
        b_ada, cT = param("b_ada", 24), param("c", NC)
        hidden = arena[:, 0:KF * T].rearrange("p (f t) -> p f t", t=T)
        h_lo = sb("h_lo", [P, KD, T], F32R)
        hidden_lo = sb("hidden_lo", [P, KF, T], F32R)
        hidden_hi = sb("hidden_hi", [P, KF, T], F32R)
        w_hi = sb("w_hi", [P, 2, UNIT], F32R)
        w_lo = sb("w_lo", [P, 2, UNIT], F32R)
        h_hi = sb("h_hi", [P, KD, T], F32R)
        assert 2 * KF * T + 4 * UNIT + KD * T <= ARENA
        taken = [0]

        def lay(*shape, at=None, of=None):
            n = int(np.prod(shape))
            start = taken[0] if at is None else at
            if at is None:
                taken[0] += n
                assert taken[0] <= ARENA, taken
            v = (arena if of is None else of)[:, start:start + n]
            names = "abcd"[:len(shape)]
            if len(shape) == 1:
                return v
            return v.rearrange(f"p ({' '.join(names)}) -> p {' '.join(names)}", **dict(zip(names[1:], shape[1:])))

        y_flat = y[:].rearrange("p k t -> p (k t)")
        h_flat = h[:].rearrange("p k t -> p (k t)")

        cq = lay(2, T)
        ckv = lay(T)
        kr = lay(T)
        rq = lay(2, T)
        rk = lay(2, T)
        vn = lay(NTOK, HR * DVR)
        sgr = lay(HR, T)
        qn = lay(HM // 2, T)
        kr_rot = lay(T)
        q_ls = lay(NSEQ, HM * TS, at=0)
        q_rs = lay(NSEQ, HM * TS, at=NSEQ * HM * TS)
        prob = lay(2, 3 * P, at=4 * T)
        prob_t = lay(2, 3 * P, at=4 * T + 6 * P)
        prob_s = lay(PAST + NS, at=4 * T + 12 * P)
        prob_st = lay(NPAGES + 1, P, at=4 * T + 12 * P + PAST + NS)
        assert 12 * P + PAST + NS + (NPAGES + 1) * P <= (2 + 2 + 4) * T + NTOK * HR * DVR
        taken[0] = KF * T
        even_c = lay(N_EVEN_CONSTS)
        state_r = lay(NSEQ, HR // 2, DVR)
        mix = lay(KD, T)
        lat = lay(T)
        qr = lay(2, T)
        kr4 = lay(4, T)
        lat_n = lay(NTOK, RANK)
        ktail = lay(NTOK, HR * DKR, of=y_flat, at=0)
        scores = lay(2, 3 * P + NS, of=y_flat, at=NTOK * HR * DKR)
        q_lead = lay(HR, NS, of=y_flat, at=NTOK * HR * DKR + 2 * (3 * P + NS))
        vmask = lay(NSEQ, DVR, of=h_flat, at=0)
        ro = lay(HR, T, of=h_flat, at=NSEQ * DVR)
        state_p = lay(HR // 2, DVR, of=h_flat, at=NSEQ * DVR + HR * T)
        q_lat = lay(HM, T, of=y_flat, at=0)
        o_lat = lay(HM, T, of=h_flat, at=0)
        ro_sq = [sq[:, 0, :], sq[:, 1, :], sq[:, 2, :], mean2[:]]
        ro_r = [silu_g[:, 0, :], silu_g[:, 1, :], var[:], rstd[:]]

        def even(name, *shape):
            at, width = EVEN_CONSTS[name]
            v = even_c[:, at:at + width]
            return v.rearrange("p (a b) -> p a b", b=shape[-1]) if shape else v

        w_uq, w_uk, w_uv = even("w_uq", HM * (NOPE + ROPE)), even("w_uk", RANK), even("w_uv")
        decay_p, decay_s = even("decay_p", 3 * P), even("decay_s", NS)
        place, mask_s, tail_c, lead_c = even("place", P), even("mask_s", NS), even("tail", HR), even("lead", TS)

        taken[0] = 0
        gla0 = 0
        gq = lay(2, T)
        gk = lay(2, T)
        gv = lay(NTOK, HR * DVR)
        gr = lay(HR, T)
        glr = lay(T)
        seg = lay(2, T)
        s_pair = lay(2, 4, P)
        s_samp = lay(2, 2, NS)
        q_exp = lay(HR, P + NS)
        gktail = lay(NTOK, HR * DKR)
        st1 = lay(HR // 2, DVR)
        st2 = lay(HR // 2, DVR)
        gla_end = taken[0]
        assert gla_end >= KF * T
        odd_c = lay(N_ODD_CONSTS)
        state_g = lay(NSEQ, HR // 2, DVR)
        hist = lay(NXC, NSEQ, CONV - 1)
        zs = lay(NXS, T)
        xpad = lay(NXC, PADDED)
        mix3 = lay(NXC, T)
        conv_state = lay(NXC, NC, CONV - 1)
        dtx, dt, dtu, dts, dtp, ua = (lay(NTOK, HS) for _ in range(6))
        e_a = lay(HS)
        tails = lay(HS)
        dec_p = lay(HS)
        dec_s = lay(NSEQ, HS)
        gla, ge, qe, ke = (lay(2, T, of=y_flat, at=2 * T * j) for j in range(4))
        gvmask = lay(NSEQ, DVR, of=h_flat, at=0)
        go = lay(HR, T, of=h_flat, at=NSEQ * DVR)
        xc = lay(NXC, T, at=0)
        xdt = lay(NTOK, INNER, at=NXC * T)
        ssm1 = lay(INNER, at=NXC * T + NTOK * INNER)
        acc = [lay(CONV_OUT, at=NXC * T + NTOK * INNER + INNER), lay(CONV_OUT, of=y_flat, at=HS * P)]
        assert NXC * T + NTOK * INNER + INNER + CONV_OUT <= gla_end
        xdt_tail = lay(INNER, of=state_g.rearrange("p a b c -> p (a b c)"), at=0)
        bn = lay(NTOK, GROUPS * DSTATE, of=state_g.rearrange("p a b c -> p (a b c)"), at=INNER)
        c_exp = lay(HS, P, of=y_flat, at=0)
        ssm = lay(2, INNER, of=h_flat, at=0)
        gm = lay(GROUPS, P, of=h_flat, at=2 * INNER)
        xpad_flat = xpad.rearrange("p a b -> p (a b)")
        att = lay(HS, P, of=xpad_flat, at=0)
        steps = lay(HS, P, of=xpad_flat, at=HS * P)
        b_masked = lay(NSEQ, GROUPS * DSTATE, of=xpad_flat, at=HS * P)

        def odd(name, *shape):
            at, width = ODD_CONSTS[name]
            v = odd_c[:, at:at + width]
            return v.rearrange("p (a b) -> p a b", b=shape[-1]) if shape else v

        def sized(v, t):
            if t < 2:
                return v
            return v.rearrange("p a t -> p (a t)")[:, 0:HS * NS].rearrange("p (a t) -> p a t", t=NS)

        def steps_of(t):
            return sized(steps, t)

        def att_of(t):
            return sized(att, t)

        c_exp_s = sized(c_exp, 2)
        ysq = xdt.rearrange("p a b -> p (a b)")[:, 0:NXS * T].rearrange("p (a t) -> p a t", t=T)
        DECAYS = (0, 4, 12)

        w_small, levels, conv_w = odd("w_small", 2 * GATE_RANK), odd("levels", P), odd("conv_w", NXC)

        landed = [sem(f"landed{r}") for r in range(RING)]
        w_done = sem("w_done")
        s_load = sem("s_load")
        s_const = sem("s_const")
        sc_clear = sem("sc_clear")
        sc_ready = sem("sc_ready")
        raw_copied = sem("raw_copied")
        ada_turned = sem("ada_turned")
        prep_done = sem("prep_done")
        mod_prompt = sem("mod_prompt")
        mod_sample = sem("mod_sample")
        unit_first = sem("unit_first")
        w_hi_done = sem("w_hi_done")
        w_lo_done = sem("w_lo_done")
        h_hi_done = sem("h_hi_done")
        h_lo_done = sem("h_lo_done")
        hid_hi_done = sem("hid_hi_done")
        hid_lo_done = sem("hid_lo_done")
        silu_done = sem("silu_done")
        hid_done = sem("hid_done")
        gated_done = sem("gated_done")
        y_done = sem("y_done")
        sq_done = sem("sq_done")
        sums_clear = sem("sums_clear")
        sumy_done = sem("sumy_done")
        sumq_done = sem("sumq_done")
        stats_ready = sem("stats_ready")
        mean2_done = sem("mean2_done")
        var_done = sem("var_done")
        rstd_done = sem("rstd_done")
        xhat_done = sem("xhat_done")
        xnew_done = sem("xnew_done")
        out_tile = sem("out_tile")
        named = {}

        def ev(name):
            if name not in named:
                named[name] = sem(name)
            return named[name]

        def rows64(h):
            return slice(64 * (h % 2), 64 * (h % 2) + 64)

        dve_chain = sem("dve_chain")
        act_chain = sem("act_chain")
        s_out = sem("s_out")

        def samples(ap):
            if len(ap.shape) == 3:
                return ap[:, :, TP:T].rearrange("p k (b t) -> p k b t", t=TS)
            return ap[:, TP:T].rearrange("p (b t) -> p b t", t=TS)

        def spread(ap, n):
            return ap.unsqueeze(len(ap.shape)).to_broadcast([*ap.shape, n])

        def slots(eng, count, body, straight=False):
            rest = count if straight else count % RING
            for s in range(rest):
                body(s, 0)
            if rest < count:
                with eng.Fori(0, (count - rest) // RING) as i:
                    for s in range(rest, rest + RING):
                        body(s, i)

        def wait_landed(pe, n, i=0):
            past = len([m for m in range(PAST0, min(n + 1, PAST0 + NSEQ)) if m % RING == n % RING])
            pe.wait_ge(landed[n % RING], 16 * (n // RING + 1 + past * (NPAGES - 1)) + i * 16)

        def unit_of(n, j, up):
            if up:
                return ring[:, n % RING, :].rearrange("p (g k n) -> p g k n", g=2, n=2 * P)[:, :, :, j * P:(j + 1) * P]
            return ring[:, n % RING, j * (KF // 2) * P:(j + 1) * (KF // 2) * P]

        def split_of(w, j, up):
            if up:
                return w[:, j, :].rearrange("p (g k n) -> p g k n", g=2, n=P)
            return w[:, j, 0:(KF // 2) * P]

        def units_before(i, up, s, j):
            return 2 * (N_FFN * ffn_index(i) + (0 if up else N_UP) + s) + j

        def past_of(b):
            return ring[:, (PAST0 + b) % RING, 0:NPAGES * 3 * PAGE].rearrange("p (j n) -> p j n", n=3 * PAGE)

        block = ctx.enter_context(nc.Block())

        @block.sync
        def _(sp):
            sp.dma_start(params[:], d["params"]).then_inc(s_load, 16)
            sp.dma_start(add_turn[:], d["add_turn"]).then_inc(s_load, 16)

            def stream(n0, src, first, count):
                width = src.shape[2]

                def one(s, i):
                    n = n0 + s
                    if n >= RING:
                        sp.wait_ge(w_done, n - RING + 1 + i * RING)
                    sp.dma_start(ring[:, n % RING, 0:width], src[bass.ds(first + s + i * RING, 1)]
                                 .rearrange("a p n -> (a p) n")).then_inc(landed[n % RING], 16)
                slots(sp, count, one, straight=n0 < RING)

            def load_past():
                for b in range(NSEQ):
                    n = PAST0 + b
                    sp.wait_ge(w_done, n - RING + 1)
                    with sp.Fori(0, NPAGES) as j:
                        page = sp.value_load(pages[0:1, bass.ds(j + b * NPAGES, 1)],
                                             min_val=0, max_val=d["cache"].shape[0] - 1)
                        sp.dma_start(past_of(b)[:, bass.ds(j, 1), :].rearrange("p a n -> p (a n)"),
                                     d["cache"][bass.ds(page, 1)].rearrange("a p n -> (a p) n"))\
                          .then_inc(landed[n % RING], 16)

            for i in range(NBLK):
                stream(ADA0[i], d["w_ada"], N_ADA * i, N_ADA)
                if i == 0:
                    sp.dma_start(x[:], d["xT"]).then_inc(s_load, 16)
                if i == MIXERS[0]:
                    stream(BODY0[i], d["w_in_even"], 0, N_IN[i])
                    sp.wait_ge(ev("pages_landed"), 16)
                    load_past()
                    stream(OUT0[i], d["w_out_even"], 0, N_OUT[i])
                if i == MIXERS[1]:
                    stream(BODY0[i], d["w_in_odd"], 0, N_IN[i])
                    stream(OUT0[i], d["w_out_odd"], 0, RING)
                    sp.wait_ge(ev("gla_done"), 1)
                    for b in range(NSEQ):
                        if b >= 2:
                            sp.wait_ge(ev("ssm_stored%d" % (b % 2)), 16 * (b // 2))
                        sp.dma_start(ssm[:, b % 2, :], d["state_ssm"][b]).then_inc(ev("ssm_landed%d" % (b % 2)), 16)
                    stream(OUT0[i] + RING, d["w_out_odd"], RING, N_OUT[i] - RING)
                if i in MIXERS:
                    continue
                stream(BODY0[i], d["w_up"], N_UP * ffn_index(i), N_UP)
                if i == 0:
                    sp.dma_start(ident[:], d["ident"]).then_inc(ev("even_landed"), 16)
                    sp.dma_start(sample_of[:], d["sample_of"]).then_inc(ev("even_landed"), 16)
                    sp.dma_start(pages[:], d["pages"]).then_inc(ev("pages_landed"), 16)
                stream(BODY0[i] + N_UP, d["w_down"], N_DOWN * ffn_index(i), N_DOWN)
            sp.wait_ge(xnew_done, KD * NBLK)
            sp.dma_start(d["yT"], x[:]).then_inc(s_out, 16)
            sp.wait_ge(s_out, 16 * N_STORES)

        @block.tensor
        def _(pe):
            def turn(i, s):
                pe.wait_ge(raw_copied, N_ADA * i + s + 1)
                for m in range(4):
                    last = nc.tensor.matmul(ps[BANK_ADA][:, (4 * s + m) * NC:(4 * s + m) * NC + WIDE],
                                            ada_raw[:, s % 2, m * P:(m + 1) * P], add_turn[:],
                                            start=True, stop=True)
                last.then_inc(ada_turned, 1)

            def conditioning(i):
                n0 = ADA0[i]
                for s in range(N_ADA):
                    wait_landed(pe, n0 + s)
                    if N_ADA * i + s >= 2:
                        pe.wait_ge(raw_copied, N_ADA * i + s - 1)
                    w = ring[:, (n0 + s) % RING, :].rearrange("p (k n) -> p k n", n=512)
                    for k in range(KD):
                        j = k % 4
                        last = nc.tensor.matmul(ps[BANK_RAW[s % 2]][32 * j:32 * j + 32, :], sc[:, k, :],
                                                w[:, k, :], start=(k < 4), stop=(k >= 4))
                    last.then_inc(w_done, 1)
                    if s:
                        turn(i, s - 1)
                turn(i, N_ADA - 1)

            def ffn(i):
                n0, f0, d0 = BODY0[i], KF * ffn_index(i), KD * i

                def product(out, pairs, first, last):
                    for k, (w, v) in enumerate(pairs):
                        for part, (a, b) in enumerate(((0, 0), (1, 0), (0, 1))):
                            ins = nc.tensor.matmul(out, w[a], v[b], start=first and k + part == 0,
                                                   stop=last and k == len(pairs) - 1 and part == 2)
                    return ins

                def up(s, it):
                    for j in range(2):
                        pe.wait_ge(w_lo_done, units_before(i, True, s, j) + 1 + it * (2 * RING))
                        if f0 + 2 * s + j >= 2:
                            pe.wait_ge(hid_done, f0 + 2 * s + j - 1 + it * (2 * RING))
                        hi, lo = split_of(w_hi, j, True), split_of(w_lo, j, True)
                        for g in range(2):
                            for k in range(KD):
                                if s == j == g == 0:
                                    pe.wait_ge(h_lo_done, KD * ffn_index(i) + k + 1)
                                last = product(ps[2 * j + g][:, 0:T], [((hi[:, g, k, :], lo[:, g, k, :]),
                                                                        (h_hi[:, k, :], h_lo[:, k, :]))],
                                               k == 0, k == KD - 1)
                        last.then_inc(unit_first if j == 0 else w_done, 1)
                slots(pe, N_UP, up)

                def down(s, it):
                    if d0 + s >= RING:
                        pe.wait_ge(y_done, d0 + s - RING + 1 + it * RING)
                    for j in range(2):
                        pe.wait_ge(w_lo_done, units_before(i, False, s, j) + 1 + it * (2 * RING))
                        if s == 0:
                            pe.wait_ge(hid_lo_done, f0 + (j + 1) * (KF // 2))
                        hi, lo = (split_of(w, j, False).rearrange("p (f n) -> p f n", n=P) for w in (w_hi, w_lo))
                        last = product(ps[BANK_DOWN[s % RING]][:, 0:T],
                                       [((hi[:, f, :], lo[:, f, :]),
                                         (hidden_hi[:, j * (KF // 2) + f, :], hidden_lo[:, j * (KF // 2) + f, :]))
                                        for f in range(KF // 2)], j == 0, j == 1)
                        last.then_inc(unit_first if j == 0 else w_done, 1)
                slots(pe, N_DOWN, down, straight=i == 0)

            def stats(i):
                if i == 0:
                    pe.wait_ge(s_const, 1)
                pe.wait_ge(sumy_done, KD * (i + 1))
                pe.wait_ge(sumq_done, KD * (i + 1))
                nc.tensor.matmul(ps[BANK_MEAN][:, 0:T], ones_d[:], ysum[:], start=True, stop=True)
                nc.tensor.matmul(ps[BANK_MSQ][:, 0:T], ones_d[:], sqsum[:], start=True, stop=True)\
                  .then_inc(stats_ready, 1)

            def project(i, slot, banks, groups, halfway=None):
                n = BODY0[i] + slot
                wait_landed(pe, n)
                w = ring[:, n % RING, :].rearrange("p (k n) -> p k n", n=512)
                for g, (bank, what) in enumerate(zip(banks, groups)):
                    if g == 2 and halfway:
                        halfway()
                    for k in range(KD):
                        if isinstance(what, slice):
                            size = what.stop - what.start
                            last = nc.tensor.matmul(ps[bank][0:size, 0:T], w[:, k, what], h[:, k, :],
                                                    start=(k == 0), stop=(k == KD - 1))
                        else:
                            t0, size = TOK[what]
                            last = nc.tensor.matmul(ps[bank][0:size, :], h[:, k, t0:t0 + size], w[:, k, :],
                                                    start=(k == 0), stop=(k == KD - 1))
                last.then_inc(w_done, 1)

            def out_project(i, tiles, depth, parts):
                for k in range(KD):
                    n = OUT0[i] + k // tiles
                    wait_landed(pe, n)
                    if k >= RING:
                        pe.wait_ge(y_done, KD * i + k - RING + 1)
                    w = ring[:, n % RING, 0:depth * tiles * P].rearrange("p (k n) -> p k n", n=tiles * P)
                    for f in range(depth):
                        last = nc.tensor.matmul(ps[BANK_DOWN[k % RING]][:, 0:T],
                                                w[:, f, (k % tiles) * P:(k % tiles + 1) * P], parts[:, f, :],
                                                start=(f == 0), stop=(f == depth - 1))
                    last.then_inc(w_done if k % tiles == tiles - 1 else out_tile, 1)

            def tiles_of(n):
                return [slice(m * P, (m + 1) * P) for m in range(n)]

            def group(out, pairs):
                for k, (lhs, rhs) in enumerate(pairs):
                    last = nc.tensor.matmul(out, lhs, rhs, start=(k == 0), stop=(k == len(pairs) - 1))
                return last

            def even_mixer(i):
                pe.wait_ge(mod_prompt, KD * (i + 1))
                pe.wait_ge(mod_sample, i + 1)
                project(i, 0, (1, 2, 4, 5), [*tiles_of(3), slice(3 * P, 3 * P + ROPE)])
                project(i, 1, (6, 7, 0, 3), tiles_of(4))
                pe.wait_ge(ev("even_in"), 1)
                project(i, 2, (1, 2, 4), range(NTOK))
                pe.wait_ge(ev("even_in"), 2)
                project(i, 3, (5, 6, 7, 0), tiles_of(4))
                pe.wait_ge(ev("latent_sq"), 1)
                pe.wait_ge(ev("even_in"), 3)
                group(ps[3][:, 0:T], [(ones_d[:], sq[:, 0, :]), (ones_d[:], sq[:, 1, :])])
                group(ps[1][:, 0:T], [(ones_d[:], sq[:, 2, :])]).then_inc(ev("latent_ms"), 1)
                pe.wait_ge(ev("even_landed"), 64)
                pe.wait_ge(ev("latents"), 1)
                pe.wait_ge(ev("even_in"), 4)
                for m, bank in enumerate((2, 4, 5, 6, 7, 0)):
                    last = group(ps[bank][:, 0:T], [(w_uq[:, k, m * P:(m + 1) * P], cq[:, k, :]) for k in range(2)])
                last.then_inc(ev("queries"), 1)
                for m in range(2):
                    group(ps[1 if m == 0 else 3][:, 0:T], [(even("swap_r"), rq[:, m, :])])
                pe.wait_ge(ev("queries_copied"), 1)
                for m in range(2):
                    last = group(ps[2 + 2 * m][:, 0:T], [(even("swap_r"), rk[:, m, :])])
                last.then_inc(ev("swapped_r"), 1)
                for m in range(2):
                    group(ps[5 + m][:, 0:T], [(even("swap_m"), qr[:, m, :])])
                for m, bank in enumerate((7, 0)):
                    last = group(ps[bank][:, 0:T], [(place[0:ROPE, m, :], kr[0:ROPE, :])])
                last.then_inc(ev("swapped_m"), 1)

                retention_like(rq, rk, "ret")

                pe.wait_ge(ev("ret_done"), 1)
                for t, (t0, size) in enumerate(TOK):
                    last = nc.tensor.transpose(ps[1][0:size, t * P:t * P + RANK], lat[:, t0:t0 + size], ident[:])
                last.then_inc(ev("lat_turned"), 1)
                for a in range(HM):
                    if a >= 4:
                        pe.wait_ge(ev("q_lat_copied"), a - 3)
                    group(ps[2 + a % 4][:, 0:T], [(w_uk[rows64(a), a // 2, :], qn[rows64(a), a // 2, :])])\
                        .then_inc(ev("q_lat_made"), 1)
                pe.wait_ge(ev("q_lat_copied"), HM)
                pe.wait_ge(ev("rotated_m"), 1)

                def prompt_scores(a):
                    if a >= 2:
                        pe.wait_ge(ev("prompt_masked"), a - 1)
                    bank = ps[2 + a % 2]
                    for tb in range(2):
                        keys = slice(0, P * (tb + 1))
                        q = slice(tb * P, (tb + 1) * P)
                        last = group(bank[:, tb * P:tb * P + P * (tb + 1)],
                                     [(q_lat[:, a, q], lat[:, keys]), (qr[:, a // 4, q], kr4[:, a % 4, keys])])
                    last.then_inc(ev("prompt_scores"), 1)

                def prompt_values(a):
                    pe.wait_ge(ev("prompt_norm"), a + 1)
                    if a >= 2:
                        pe.wait_ge(ev("prompt_turned_copied"), a - 1)
                    for m in range(3):
                        last = nc.tensor.transpose(ps[4 + a % 2][:, m * P:(m + 1) * P],
                                                   prob[:, a % 2, m * P:(m + 1) * P], ident[:])
                    last.then_inc(ev("prompt_turned"), 1)
                    pe.wait_ge(ev("prompt_turned_copied"), a + 1)
                    pe.wait_ge(ev("lat_copied"), 1)
                    if a >= 2:
                        pe.wait_ge(ev("prompt_o_copied"), a - 1)
                    bank = ps[6 + a % 2]
                    pt = [prob_t[:, a % 2, m * P:(m + 1) * P] for m in range(3)]
                    group(bank[:, 0:P], [(lat_n[:, 0, :], pt[0])])
                    group(bank[:, P:2 * P], [(lat_n[:, 0, :], pt[1]), (lat_n[:, 1, :], pt[2])])\
                        .then_inc(ev("prompt_o"), 1)

                prompt_scores(0)
                for a in range(HM):
                    if a + 1 < HM:
                        prompt_scores(a + 1)
                    prompt_values(a)

                pe.wait_ge(ev("prompt_o_copied"), HM)
                pe.wait_ge(ev("sample_q"), 1)

                def sample_scores(p, b):
                    wait_landed(pe, PAST0 + 2 * p + b)
                    ql, qro, past = q_ls[:, 2 * p + b, :], q_rs[0:64, 2 * p + b, :], past_of(2 * p + b)
                    for half in range(2):
                        pg = slice(4 * half, 4 * half + 4)
                        group(ps[2 + half][rows64(b), :], [(ql, past[:, pg, 0:PAGE]),
                                                           (qro, past[0:64, pg, 2 * PAGE:3 * PAGE])])
                    return group(ps[4][rows64(b), 0:NS], [(ql, lat[:, TP:T]), (qro, kr4[0:64, 0, TP:T])])

                sample_scores(0, 0)
                for p in range(NSEQ // 2):
                    sample_scores(p, 1).then_inc(ev("sample_scores"), 1)
                    if p + 1 < NSEQ // 2:
                        pe.wait_ge(ev("sample_masked"), p + 1)
                        sample_scores(p + 1, 0)
                    pe.wait_ge(ev("sample_norm"), p + 1)
                    for j in range(NPAGES):
                        nc.tensor.transpose(ps[5 + j // 4][:, (j % 4) * P:(j % 4 + 1) * P],
                                            prob_s[:, j * P:(j + 1) * P], ident[:])
                    nc.tensor.transpose(ps[7][0:NS, 0:P], prob_s[:, PAST:PAST + NS], ident[:])\
                      .then_inc(ev("sample_turned"), 1)
                    pe.wait_ge(ev("sample_turned_copied"), p + 1)
                    for b in range(2):
                        q, past = rows64(b), past_of(2 * p + b)
                        group(ps[0][:, q], [(past[:, j, PAGE:2 * PAGE], prob_st[:, j, q]) for j in range(NPAGES)]
                              + [(lat_n[0:NS, 2, :], prob_st[0:NS, NPAGES, q])]).then_inc(w_done, 1)
                pe.wait_ge(ev("sample_o_copied"), NSEQ // 2)
                for a in range(HM):
                    last = group(ps[1 + a // 2][rows64(a), 0:T], [(w_uv[:, a * VM:(a + 1) * VM], o_lat[:, a, :])])
                last.then_inc(ev("values"), 1)
                pe.wait_ge(ev("values_copied"), 1)
                out_project(i, KD // N_OUT[i], KD, mix)

            def retention_like(q, k, name):
                pe.wait_ge(ev("rotated_r"), 1)
                for t, (t0, size) in enumerate(TOK):
                    for m in range(2):
                        last = nc.tensor.transpose(ps[1 + t][0:size, m * P:(m + 1) * P], k[:, m, t0:t0 + size], ident[:])
                last.then_inc(ev("ret_k_turned"), 1)
                pe.wait_ge(ev("rotated_m"), 1)

                def head_scores(a):
                    if a >= 2:
                        pe.wait_ge(ev("ret_decayed"), a - 1)
                    r, m, bank = rows64(a), a // 2, ps[4 + a % 2]
                    group(bank[:, 0:TP], [(k[r, m, 0:P], q[r, m, 0:TP])])
                    group(bank[:, TP:TP + P], [(k[r, m, P:TP], q[r, m, P:TP])])
                    group(bank[0:NS, 3 * P:3 * P + NS], [(k[r, m, TP:T], q[r, m, TP:T])]).then_inc(ev("ret_scores"), 1)

                def head_values(a):
                    pe.wait_ge(ev("ret_decayed"), a + 1)
                    if a >= 2:
                        pe.wait_ge(ev("ret_o_copied"), a - 1)
                    r, m, bank = rows64(a), a // 2, ps[6 + a % 2]
                    s, v = scores[:, a % 2, :], slice(a * DVR, (a + 1) * DVR)
                    nc.tensor.matmul(bank[:, 0:TP], vn[:, 0, v], s[:, 0:TP], start=True, stop=False)
                    nc.tensor.matmul(bank[:, P:TP], vn[:, 1, v], s[:, TP:TP + P], start=False, stop=True)
                    nc.tensor.matmul(bank[:, TP:T], vn[0:NS, 2, v], s[0:NS, 3 * P:3 * P + NS], start=True, stop=True)
                    for b in range(NSEQ):
                        last = nc.tensor.matmul(bank[:, TP + b * TS:TP + (b + 1) * TS], state_r[:, b, m, :],
                                                q_lead[:, a, b * TS:(b + 1) * TS], start=False, stop=True,
                                                skip_group_check=True)
                    last.then_inc(ev("ret_o"), 1)

                pe.wait_ge(ev("ret_k_tail"), 1)
                head_scores(0)
                for a in range(HR):
                    if a + 1 < HR:
                        head_scores(a + 1)
                    head_values(a)
                for a in range(HR):
                    v = slice(a * DVR, (a + 1) * DVR)
                    last = group(ps[0][rows64(a), (a // 2) * DVR:(a // 2 + 1) * DVR],
                                 [(ktail[:, t, a * DKR:(a + 1) * DKR], vn[:, t, v]) for t in range(2)])
                last.then_inc(ev("ret_state"), 1)
                pe.wait_ge(ev("ret_decayed"), HR)
                pe.wait_ge(ev("ret_o_copied"), HR)
                for a in range(HR):
                    last = group(ps[1 + a][:, 0:T], [(ones_d[:], ro_sq[a])])
                last.then_inc(ev("ret_ms"), 1)
                sample_states("ret", ktail, vmask)

            def sample_states(name, kt, masked):
                for a in range(HR):
                    pe.wait_ge(ev(f"{name}_v_masked"), a + 1)
                    if a:
                        pe.wait_ge(ev(f"{name}_state_new"), a)
                    for half in range(2):
                        last = group(ps[5 + half][rows64(a), :],
                                     [(kt[0:NS, 2, a * DKR:(a + 1) * DKR], masked[0:NS, 4 * half:4 * half + 4, :])])
                    last.then_inc(ev(f"{name}_state_add"), 1)

            def odd_mixer(i):
                pe.wait_ge(mod_prompt, KD * (i + 1))
                pe.wait_ge(mod_sample, i + 1)
                project(i, 0, BANKS_IN, tiles_of(4))
                project(i, 1, (6, 7, 0), range(NTOK))
                pe.wait_ge(ev("odd_in"), 1)
                project(i, 2, (3, 1, 2, 4), tiles_of(4))
                pe.wait_ge(ev("odd_landed"), 48)
                group(ps[5][0:GATE_RANK, 0:T], [(w_small[:, k, 0:GATE_RANK], h[:, k, :]) for k in range(KD)])
                pe.wait_ge(ev("odd_in"), 2)
                for t, (t0, size) in enumerate(TOK):
                    last = group(ps[6][0:size, t * HS:(t + 1) * HS],
                                 [(h[:, k, t0:t0 + size], w_small[:, k, GATE_RANK:]) for k in range(KD)])
                last.then_inc(ev("small_made"), 1)
                pe.wait_ge(ev("small_copied"), 1)
                for m, bank in enumerate((7, 0)):
                    last = group(ps[bank][:, 0:T], [(odd("w_gate")[0:GATE_RANK, m * P:(m + 1) * P], glr[0:GATE_RANK, :])])
                last.then_inc(ev("gate_made"), 1)
                pe.wait_ge(ev("odd_in"), 3)

                def level(n):
                    pe.wait_ge(ev("level_qk"), n + 1)
                    if n:
                        pe.wait_ge(ev("level_picked"), n)
                    q, k = (qe, ke) if HALVES[n] else (gq, gk)
                    for a in range(HR):
                        r, m = rows64(a), a // 2
                        for c in range(2):
                            t = slice(c * P, (c + 1) * P)
                            last = group(ps[6 + a % 2][:, (2 * m + c) * P:(2 * m + c + 1) * P], [(k[r, m, t], q[r, m, t])])
                        if HALVES[n] < TS:
                            last = group(ps[3 * (a % 2)][0:NS, m * NS:(m + 1) * NS], [(k[r, m, TP:T], q[r, m, TP:T])])
                    last.then_inc(ev("level_made"), 1)

                for s in range(5):
                    if s:
                        pe.wait_ge(ev("odd_in"), 3 + s)
                    project(i, 3 + s, BANKS_IN, tiles_of(4), (lambda: level(2 * s)) if s < 4 else None)
                    if s < 4:
                        level(2 * s + 1)

                pe.wait_ge(ev("gla_tail"), 1)
                pe.wait_ge(ev("odd_in"), 8)
                for t, (t0, size) in enumerate(TOK):
                    for m in range(2):
                        last = nc.tensor.transpose(ps[(1, 2, 4)[t]][0:size, m * P:(m + 1) * P], ke[:, m, t0:t0 + size], ident[:])
                last.then_inc(ev("gla_k_turned"), 1)
                pe.wait_ge(ev("gla_k_copied"), 1)
                pe.wait_ge(ev("level_picked"), len(HALVES))
                for t in range(2):
                    for a in range(HR):
                        last = group(ps[3 * t][rows64(a), (a // 2) * DVR:(a // 2 + 1) * DVR],
                                     [(gktail[:, t, a * DKR:(a + 1) * DKR], gv[:, t, a * DVR:(a + 1) * DVR])])
                last.then_inc(ev("gla_state"), 1)
                pe.wait_ge(ev("gla_state1"), 1)
                for a in range(HR):
                    if a >= 2:
                        pe.wait_ge(ev("gla_o_copied"), a - 1)
                    m, bank, v = a // 2, ps[6 + a % 2], slice(a * DVR, (a + 1) * DVR)
                    group(bank[:, 0:P], [(gv[:, 0, v], s_pair[:, a % 2, 2 * m, :])])
                    group(bank[:, P:TP], [(gv[:, 1, v], s_pair[:, a % 2, 2 * m + 1, :]), (st1[:, m, :], q_exp[:, a, 0:P])])
                    group(bank[:, TP:T], [(gv[0:NS, 2, v], s_samp[0:NS, a % 2, m, :])])
                    for b in range(NSEQ):
                        last = nc.tensor.matmul(bank[:, TP + b * TS:TP + (b + 1) * TS], state_g[:, b, m, :],
                                                q_exp[:, a, P + b * TS:P + (b + 1) * TS], start=False, stop=True,
                                                skip_group_check=True)
                    last.then_inc(ev("gla_o"), 1)
                pe.wait_ge(ev("gla_o_copied"), HR)
                for a in range(HR):
                    last = group(ps[(1, 2, 4, 7)[a]][:, 0:T], [(ones_d[:], ro_sq[a])])
                last.then_inc(ev("gla_ms"), 1)
                sample_states("gla", gktail, gvmask)

                pe.wait_ge(ev("conv_done"), NXC)
                pe.wait_ge(ev("gla_done"), 1)
                for t, (t0, size) in enumerate(TOK):
                    if t:
                        pe.wait_ge(ev("xs_copied"), t)
                    for f in range(NXS + GROUPS):
                        last = nc.tensor.transpose(ps[(1, 2, 4)[f // 4]][0:size, (f % 4) * P:(f % 4 + 1) * P],
                                                   xc[:, f, t0:t0 + size], ident[:])
                    last.then_inc(ev("xs_turned"), 1)
                pe.wait_ge(ev("xs_copied"), NTOK)
                for t, (t0, size) in enumerate(TOK):
                    heads = 512 // size
                    after = odd("after")[0:size, 0:size]
                    pe.wait_ge(ev("steps"), t + 1)
                    for q in range(HS // heads):
                        if q >= 2:
                            pe.wait_ge(ev("decay_copied"), DECAYS[t] + q - 1)
                        group(ps[5 + q % 2][0:size, :], [(after, steps_of(t)[0:size, q * heads:(q + 1) * heads, :])])\
                            .then_inc(ev("decay_made"), 1)
                    if t:
                        for q in range(HS // heads):
                            n = HS // heads + q
                            pe.wait_ge(ev("decay_copied"), DECAYS[t] + n - 1)
                            group(ps[5 + n % 2][:, :], [(ones_d[0:size, :], steps_of(t)[0:size, q * heads:(q + 1) * heads, :])])\
                                .then_inc(ev("decay_made"), 1)
                    for g in range(GROUPS):
                        group(ps[7][0:size, g * size:(g + 1) * size],
                              [(xc[:, NXS + g, t0:t0 + size], xc[:, NXS + GROUPS + g, t0:t0 + size])])
                    group(ps[0][0:size, 0:HS], [(after if t < 2 else odd("after_s")[0:NS, :], ua[0:size, t, :])])
                    group(ps[0][:, HS:2 * HS], [(ones_d[0:size, :], ua[0:size, t, :])]).then_inc(ev("bc_made"), 1)
                    pe.wait_ge(ev("att_ready"), t + 1)
                    if t:
                        pe.wait_ge(ev("y_kept"), t)
                    for a in range(HS):
                        out = ps[1 + a // 8][rows64(a), (a // 2 % 4) * size:(a // 2 % 4 + 1) * size]
                        pairs = [(xdt[0:size, t, a * HDIM:(a + 1) * HDIM], att_of(t)[0:size, a, :])]
                        if t == 1:
                            pairs.append((ssm1[:, a * HDIM:(a + 1) * HDIM], c_exp[:, a, :]))
                        last = group(out, pairs)
                    last.then_inc(ev("ssd_y"), 1)
                    if t < 2:
                        pe.wait_ge(ev("tail_ready"), t + 1)
                        if t:
                            pe.wait_ge(ev("ssm1_kept"), 1)
                        for g in range(GROUPS):
                            last = group(ps[3 + g][:, :], [(bn[:, t, g * DSTATE:(g + 1) * DSTATE],
                                                            xdt_tail[:, g * 512:(g + 1) * 512])])
                        last.then_inc(ev("ssm_add"), 1)
                pe.wait_ge(ev("tail_ready"), NTOK)
                pe.wait_ge(ev("ssm1_kept"), 2)
                pe.wait_ge(ev("b_masked"), 1)
                for b in range(NSEQ):
                    pe.wait_ge(ev("ssm_landed%d" % (b % 2)), 16 * (b // 2 + 1))
                    for a in range(HS):
                        t8 = slice(b * TS, (b + 1) * TS)
                        last = group(ps[7][rows64(a), (a // 2) * NS + b * TS:(a // 2) * NS + (b + 1) * TS],
                                     [(ssm[:, b % 2, a * HDIM:(a + 1) * HDIM], c_exp_s[:, a, t8])])
                    if b:
                        pe.wait_ge(ev("ssm_new"), b)
                    for g in range(GROUPS):
                        last = group(ps[3 + g][:, :], [(b_masked[0:NS, b, g * DSTATE:(g + 1) * DSTATE],
                                                        xdt_tail[0:NS, g * 512:(g + 1) * 512])])
                    last.then_inc(ev("ssm_add_s"), 1)
                pe.wait_ge(ev("gated_sq"), 1)
                for g in range(GROUPS):
                    last = group(ps[1 + g][:, 0:T], [(ones_d[:], ysq[:, 4 * g + f, :]) for f in range(4)])
                last.then_inc(ev("ssd_ms"), 1)
                pe.wait_ge(ev("mix3_ready"), 1)
                out_project(i, KD // N_OUT[i], NXC, mix3)

            pe.wait_ge(sc_ready, 1)
            pe.wait_ge(s_load, 32)
            conditioning(0)
            for i in range(NBLK):
                if i == MIXERS[0]:
                    even_mixer(i)
                elif i == MIXERS[1]:
                    odd_mixer(i)
                else:
                    ffn(i)
                stats(i)
                if i + 1 < NBLK:
                    conditioning(i + 1)

        @block.scalar
        def _(act):
            links = [0]

            def chain(ins):
                links[0] += 1
                ins.then_inc(act_chain, 1)
                act.wait_ge(act_chain, links[0])

            def copy_raw(i, s):
                act.wait_ge(w_done, ADA0[i] + s + 1)
                if N_ADA * i + s >= 2:
                    act.wait_ge(ada_turned, N_ADA * i + s - 1)
                nc.scalar.activation(ada_raw[:, s % 2, :], ps[BANK_RAW[s % 2]][:], ACT.Copy).then_inc(raw_copied, 1)

            def modulate(i):
                src = y if i else x
                act.wait_ge(prep_done, i + 1)
                if i == 0:
                    act.wait_ge(s_load, 48)
                for k in range(KD):
                    nc.scalar.activation(h[:, k, 0:TP], src[:, k, 0:TP], ACT.Identity, bias=modB[:, k, 0:1],
                                         scale=modA[:, k, 0:1]).then_inc(mod_prompt, 1)
                    if i not in MIXERS:
                        nc.scalar.activation(h_hi[:, k, 0:TP], src[:, k, 0:TP], ACT.Identity, bias=modB[:, k, 0:1],
                                             scale=modA[:, k, 0:1]).then_inc(h_hi_done, 1)

            def round_unit(i, up, s, j, it=0):
                n = BODY0[i] + (0 if up else N_UP) + s
                before = units_before(i, up, s, j)
                wait_landed(act, n, it)
                if before >= 2:
                    if j == 0:
                        act.wait_ge(unit_first, before // 2 + it * RING)
                    else:
                        act.wait_ge(w_done, n + it * RING)
                nc.scalar.activation(split_of(w_hi, j, up), unit_of(n, j, up), ACT.Copy).then_inc(w_hi_done, 1)

            def square(i, s, it):
                act.wait_ge(y_done, KD * i + s + 1 + it * RING)
                if KD * i + s >= RING:
                    act.wait_ge(sumq_done, KD * i + s - RING + 1 + it * RING)
                nc.scalar.activation(sq[:, s % RING, :], y[:, bass.ds(s + it * RING, 1), :]
                                     .rearrange("p a t -> p (a t)"), ACT.Square).then_inc(sq_done, 1)

            def ffn(i):
                n0, f0 = BODY0[i], KF * ffn_index(i)

                def silu(s, j, it):
                    if j == 0:
                        act.wait_ge(unit_first, N_FFN * ffn_index(i) + s + 1 + it * RING)
                    else:
                        act.wait_ge(w_done, n0 + s + 1 + it * RING)
                    if f0 + 2 * s + j >= 2:
                        act.wait_ge(hid_done, f0 + 2 * s + j - 1 + it * (2 * RING))
                    nc.scalar.activation(silu_g[:, j, :], ps[2 * j][:, 0:T], ACT.Silu).then_inc(silu_done, 1)

                def round_hidden(s, j, it):
                    act.wait_ge(hid_done, f0 + 2 * s + j + 1 + it * (2 * RING))
                    at = bass.ds(2 * s + j + it * (2 * RING), 1)
                    nc.scalar.activation(hidden_hi[:, at, :].rearrange("p a t -> p (a t)"),
                                         hidden[:, at, :].rearrange("p a t -> p (a t)"), ACT.Copy).then_inc(hid_hi_done, 1)

                def up(s, it):
                    for j in range(2):
                        if s:
                            silu(s - 1, j, it)
                        if s or j:
                            round_unit(i, True, s, j, it)
                        if s:
                            round_hidden(s - 1, j, it)
                slots(act, N_UP, up)

                def down(s, it):
                    for j in range(2):
                        if s == 0:
                            silu(N_UP - 1, j, 0)
                        round_unit(i, False, s, j, it)
                        if s == 0:
                            round_hidden(N_UP - 1, j, 0)
                    if s:
                        square(i, s - 1, it)
                slots(act, N_DOWN, down, straight=i == 0)
                square(i, N_DOWN - 1, 0)
                if i + 1 == MIXERS[0]:
                    act.dma_start(even_c[:], d["even_consts"]).then_inc(ev("even_landed"), 16)
                    act.dma_start(state_r[:], d["state_r"]).then_inc(ev("even_landed"), 16)
                if i + 1 == MIXERS[1]:
                    act.dma_start(odd_c[:], d["odd_consts"]).then_inc(ev("odd_landed"), 16)
                    act.dma_start(state_g[:], d["state_g"]).then_inc(ev("odd_landed"), 16)
                    act.dma_start(hist[:], d["conv_hist"]).then_inc(ev("odd_landed"), 16)

            def norm(i):
                act.wait_ge(stats_ready, i + 1)
                nc.scalar.activation(mean2[:], ps[BANK_MEAN][:, 0:T], ACT.Square).then_inc(mean2_done, 1)
                if i + 1 < NBLK:
                    copy_raw(i + 1, 0)
                act.wait_ge(var_done, i + 1)
                chain(nc.scalar.activation(rstd[:], var[:], ACT.Ln))
                nc.scalar.activation(rstd[:], rstd[:], ACT.Exp, scale=-0.5).then_inc(rstd_done, 1)
                if i + 1 < NBLK:
                    for s in range(1, N_ADA):
                        copy_raw(i + 1, s)

            def copy(out, bank, scale=1.0):
                return nc.scalar.activation(out, bank, ACT.Copy, scale=scale)

            def even_mixer(i):
                n = BODY0[i]
                act.wait_ge(w_done, n + 1)
                copy(cq[:, 0, :], ps[1][:, 0:T])
                copy(cq[:, 1, :], ps[2][:, 0:T])
                copy(ckv[:], ps[4][:, 0:T])
                copy(kr[0:ROPE, :], ps[5][0:ROPE, 0:T]).then_inc(ev("even_in"), 1)
                act.wait_ge(w_done, n + 2)
                copy(rq[:, 0, :], ps[6][:, 0:T])
                copy(rq[:, 1, :], ps[7][:, 0:T])
                copy(rk[:, 0, :], ps[0][:, 0:T], DKR ** -0.5)
                copy(rk[:, 1, :], ps[3][:, 0:T], DKR ** -0.5).then_inc(ev("even_in"), 1)
                act.wait_ge(w_done, n + 3)
                for t, (_, size) in enumerate(TOK):
                    last = copy(vn[0:size, t, :], ps[(1, 2, 4)[t]][0:size, :])
                last.then_inc(ev("even_in"), 1)
                act.wait_ge(w_done, n + 4)
                for m, bank in enumerate((5, 6, 7, 0)):
                    last = nc.scalar.activation(sgr[:, m, :], ps[bank][:, 0:T], ACT.Silu)
                last.then_inc(ev("even_in"), 1)
                act.wait_ge(ev("latent_ms"), 1)
                act.wait_ge(ev("rms_eps"), 1)
                nc.scalar.activation(var[:], ps[3][:, 0:T], ACT.Ln, bias=eps_rms[:], scale=D / QRANK)
                chain(nc.scalar.activation(rstd[:], ps[1][:, 0:T], ACT.Ln, bias=eps_rms[:], scale=D / RANK))
                nc.scalar.activation(var[:], var[:], ACT.Exp, scale=-0.5)
                nc.scalar.activation(rstd[:], rstd[:], ACT.Exp, scale=-0.5).then_inc(ev("latent_r"), 1)
                act.wait_ge(ev("queries"), 1)
                for m, bank in enumerate((2, 4, 5, 6)):
                    copy(qn[:, m, :], ps[bank][:, 0:T])
                copy(qr[:, 0, :], ps[7][:, 0:T])
                copy(qr[:, 1, :], ps[0][:, 0:T]).then_inc(ev("queries_copied"), 1)

                for a in range(HR):
                    act.wait_ge(ev("ret_o"), a + 1)
                    copy(ro[:, a, :], ps[6 + a % 2][:, 0:T])
                    nc.scalar.activation(ro_sq[a], ps[6 + a % 2][:, 0:T], ACT.Square).then_inc(ev("ret_o_copied"), 1)
                act.wait_ge(ev("ret_ms"), 1)
                for a in range(HR):
                    last = nc.scalar.activation(ro_r[a], ps[1 + a][:, 0:T], ACT.Ln, bias=eps_rms[:], scale=D / DVR)
                chain(last)
                for a in range(HR):
                    last = nc.scalar.activation(ro_r[a], ro_r[a], ACT.Exp, scale=-0.5)
                last.then_inc(ev("ret_r"), 1)
                act.wait_ge(ev("ret_state_out"), 1)
                act.dma_start(d["out_ret_p"], state_p[:]).then_inc(ev("ret_p_stored"), 16)

                act.wait_ge(ev("lat_turned"), 1)
                copy(lat_n[:, 0:2, :], ps[1][:, 0:2 * P].rearrange("p (a n) -> p a n", n=P))
                copy(lat_n[0:NS, 2, :], ps[1][0:NS, 2 * P:3 * P]).then_inc(ev("lat_copied"), 1)
                for a in range(HM):
                    act.wait_ge(ev("q_lat_made"), a + 1)
                    copy(q_lat[:, a, :], ps[2 + a % 4][:, 0:T]).then_inc(ev("q_lat_copied"), 1)

                def prompt_exp(a):
                    act.wait_ge(ev("prompt_max"), a + 1)
                    pr, u = prob[:, a % 2, :], a % 2
                    nc.scalar.activation(pr[:, 0:P], pr[:, 0:P], ACT.Exp, bias=stat[:, u, 0:1],
                                         accum_out=stat[:, 2 + u, 0:1])
                    nc.scalar.activation(pr[:, P:3 * P], pr[:, P:3 * P], ACT.Exp, bias=stat[:, u, 1:2],
                                         accum_out=stat[:, 2 + u, 1:2]).then_inc(ev("prompt_exp"), 1)

                prompt_exp(0)
                act.wait_ge(ev("ret_p_stored"), 16)
                for a in range(HM):
                    if a + 1 < HM:
                        prompt_exp(a + 1)
                    act.wait_ge(ev("prompt_turned"), a + 1)
                    copy(prob_t[:, a % 2, :], ps[4 + a % 2][:, 0:3 * P]).then_inc(ev("prompt_turned_copied"), 1)
                    act.wait_ge(ev("prompt_o"), a + 1)
                    copy(o_lat[:, a, 0:TP], ps[6 + a % 2][:, 0:TP]).then_inc(ev("prompt_o_copied"), 1)

                for p in range(NSEQ // 2):
                    act.wait_ge(ev("sample_scores"), p + 1)
                    copy(prob_s[:, 0:512], ps[2][:], ATT_SCALE)
                    copy(prob_s[:, 512:1024], ps[3][:], ATT_SCALE).then_inc(ev("sample_copied"), 1)
                    act.wait_ge(ev("sample_max"), p + 1)
                    nc.scalar.activation(prob_s[:], prob_s[:], ACT.Exp, bias=stat[:, 0, 0:1],
                                         accum_out=stat[:, 2, 0:1]).then_inc(ev("sample_exp"), 1)
                    act.wait_ge(ev("sample_turned"), p + 1)
                    copy(prob_st[:, 0:4, :], ps[5][:].rearrange("p (a n) -> p a n", n=P))
                    copy(prob_st[:, 4:8, :], ps[6][:].rearrange("p (a n) -> p a n", n=P))
                    copy(prob_st[0:NS, 8, :], ps[7][0:NS, 0:P]).then_inc(ev("sample_turned_copied"), 1)
                    act.wait_ge(w_done, PAST0 + 2 * p + 2)
                    for b in range(2):
                        t0 = TP + (2 * p + b) * TS
                        last = copy(o_lat[:, :, t0:t0 + TS],
                                    ps[0][:, rows64(b)].rearrange("p (a t) -> p a t", t=TS))
                    last.then_inc(ev("sample_o_copied"), 1)

                act.wait_ge(ev("values"), 1)
                for m in range(4):
                    last = copy(mix[:, m, :], ps[1 + m][:, 0:T])
                last.then_inc(ev("values_copied"), 1)
                act.dma_start(d["out_lat"], lat[:]).then_inc(ev("even_stored"), 16)
                act.wait_ge(ev("rotated_m"), 1)
                act.dma_start(d["out_krope"], kr_rot[0:ROPE, :]).then_inc(ev("even_stored"), 16)
                act.wait_ge(ev("ret_state_new"), HR)
                act.dma_start(d["out_ret_s"], state_r[:]).then_inc(ev("even_stored"), 16)
                for k in range(KD):
                    square(i, k, 0)

            def odd_mixer(i):
                n = BODY0[i]

                def arrived(slot):
                    act.wait_ge(w_done, n + slot + 1)

                arrived(0)
                for m in range(2):
                    copy(gq[:, m, :], ps[BANKS_IN[m]][:, 0:T], DKR ** -0.5)
                for m in range(2):
                    last = copy(gk[:, m, :], ps[BANKS_IN[2 + m]][:, 0:T])
                last.then_inc(ev("odd_in"), 1)
                arrived(1)
                for t, (_, size) in enumerate(TOK):
                    last = copy(gv[0:size, t, :], ps[(6, 7, 0)[t]][0:size, :])
                last.then_inc(ev("odd_in"), 1)
                arrived(2)
                for m, bank in enumerate((3, 1, 2, 4)):
                    last = nc.scalar.activation(gr[:, m, :], ps[bank][:, 0:T], ACT.Silu)
                last.then_inc(ev("odd_in"), 1)
                act.wait_ge(ev("small_made"), 1)
                act.wait_ge(ev("dt_clear"), 1)
                copy(dtx[:, 0:2, :], ps[6][:, 0:2 * HS].rearrange("p (a b) -> p a b", b=HS))
                copy(dtx[0:NS, 2, :], ps[6][0:NS, 2 * HS:3 * HS])
                copy(glr[0:GATE_RANK, :], ps[5][0:GATE_RANK, 0:T]).then_inc(ev("small_copied"), 1)
                act.wait_ge(ev("gate_made"), 1)
                act.wait_ge(xnew_done, KD * i)
                for m, bank in enumerate((7, 0)):
                    last = nc.scalar.activation(gla[:, m, :], ps[bank][:, 0:T], ACT.Identity,
                                                bias=odd("b_gate")[:, m:m + 1])
                chain(last)
                chain(nc.scalar.activation(ge[:], gla[:], ACT.Abs))
                chain(nc.scalar.activation(ge[:], ge[:], ACT.Exp, scale=-1.0))
                nc.scalar.activation(ge[:], ge[:], ACT.Ln, bias=1.0).then_inc(ev("gate_log"), 1)
                act.wait_ge(ev("dt_biased"), 1)
                nc.scalar.activation(e_a[:], odd("a_log"), ACT.Exp)
                chain(nc.scalar.activation(dtu[:], dtx[:], ACT.Abs))
                nc.scalar.activation(dtu[:], dtu[:], ACT.Exp, scale=-1.0).then_inc(ev("dt_exp"), 1)

                def level(k):
                    w = TP if HALVES[k] >= TS else T
                    act.wait_ge(ev("level_diff"), k + 1)
                    chain(nc.scalar.activation(ge[:, :, 0:w], ge[:, :, 0:w], ACT.Abs))
                    nc.scalar.activation(ge[:, :, 0:w], ge[:, :, 0:w], ACT.Exp, scale=-1.0 / TAU)\
                      .then_inc(ev("level_exp"), 1)

                for s in range(5):
                    for k in (2 * s, 2 * s + 1):
                        if k < len(HALVES) and HALVES[k]:
                            level(k)
                    arrived(3 + s)
                    for m in range(4):
                        bank = ps[BANKS_IN[m]]
                        if s < 2:
                            last = nc.scalar.activation(zs[:, 4 * s + m, :], bank[:, 0:T], ACT.Silu)
                        else:
                            f = 4 * (s - 2) + m
                            copy(xpad[:, f, CONV - 1:WP], bank[:, 0:TP])
                            last = copy(xpad[:, f, WP:].rearrange("p (b t) -> p b t", t=WS)[:, :, CONV - 1:],
                                        bank[:, TP:T].rearrange("p (b t) -> p b t", t=TS))
                    last.then_inc(ev("odd_in"), 1)
                act.wait_ge(ev("level_picked"), len(HALVES))
                chain(nc.scalar.activation(qe[:], seg[:], ACT.Exp, scale=1.0 / TAU))
                act.wait_ge(ev("tail_diff"), 1)
                nc.scalar.activation(ge[:], ge[:], ACT.Exp, scale=1.0 / TAU).then_inc(ev("gla_exps"), 1)
                act.wait_ge(ev("gla_k_turned"), 1)
                for t, (_, size) in enumerate(TOK):
                    last = copy(gktail[0:size, t, :], ps[(1, 2, 4)[t]][0:size, 0:HR * DKR])
                last.then_inc(ev("gla_k_copied"), 1)
                for a in range(HR):
                    act.wait_ge(ev("gla_o"), a + 1)
                    copy(go[:, a, :], ps[6 + a % 2][:, 0:T])
                    nc.scalar.activation(ro_sq[a], ps[6 + a % 2][:, 0:T], ACT.Square).then_inc(ev("gla_o_copied"), 1)
                act.wait_ge(ev("gla_ms"), 1)
                for a in range(HR):
                    last = nc.scalar.activation(ro_r[a], ps[(1, 2, 4, 7)[a]][:, 0:T], ACT.Ln, bias=eps_rms[:], scale=D / DVR)
                chain(last)
                for a in range(HR):
                    last = nc.scalar.activation(ro_r[a], ro_r[a], ACT.Exp, scale=-0.5)
                last.then_inc(ev("gla_r"), 1)
                act.wait_ge(ev("gla_state2"), 1)
                act.dma_start(d["out_gla_p"], st2[:]).then_inc(ev("gla_stored"), 16)
                act.wait_ge(ev("gla_state_new"), HR)
                act.dma_start(d["out_gla_s"], state_g[:]).then_inc(ev("gla_stored"), 16)
                act.wait_ge(ev("conv_state"), 1)
                act.dma_start(d["out_conv"], conv_state[:]).then_inc(s_out, 16)

                act.wait_ge(ev("gla_done"), 1)
                act.wait_ge(ev("gla_stored"), 32)

                def conv_first(f):
                    if f >= 2:
                        act.wait_ge(ev("conv_done"), f - 1)
                    nc.scalar.activation(acc[f % 2], xpad[:, f, 0:CONV_OUT], ACT.Identity,
                                         bias=odd("conv_b")[:, f:f + 1], scale=conv_w[:, 0, f:f + 1])\
                      .then_inc(ev("conv_first"), 1)
                conv_first(0)
                conv_first(1)
                for f in range(NXC):
                    act.wait_ge(ev("conv_added"), f + 1)
                    nc.scalar.activation(xc[:, f, 0:TP], acc[f % 2][:, 0:TP], ACT.Silu)
                    for_samples = acc[f % 2][:, WP:CONV_OUT]
                    head = for_samples[:, 0:(NSEQ - 1) * WS].rearrange("p (b t) -> p b t", t=WS)[:, :, 0:TS]
                    nc.scalar.activation(xc[:, f, TP:T - TS].rearrange("p (b t) -> p b t", t=TS), head, ACT.Silu)
                    nc.scalar.activation(xc[:, f, T - TS:T], for_samples[:, (NSEQ - 1) * WS:], ACT.Silu)\
                      .then_inc(ev("conv_done"), 1)
                    if f + 2 < NXC:
                        conv_first(f + 2)

                for t, (_, size) in enumerate(TOK):
                    act.wait_ge(ev("xs_turned"), t + 1)
                    copy(bn[0:size, t, :], ps[4][0:size, 0:GROUPS * DSTATE]).then_inc(ev("bn_copied"), 1)
                for t, (_, size) in enumerate(TOK):
                    heads = 512 // size
                    for q in range(HS // heads):
                        act.wait_ge(ev("decay_made"), DECAYS[t] + q + 1)
                        if t and q == 0:
                            act.wait_ge(ev("ssd_y"), t)
                        nc.scalar.activation(att_of(t)[0:size, q * heads:(q + 1) * heads, :],
                                             ps[5 + q % 2][0:size, :].rearrange("p (a n) -> p a n", n=size), ACT.Exp)\
                          .then_inc(ev("decay_copied"), 1)
                    if t:
                        for q in range(HS // heads):
                            k = HS // heads + q
                            act.wait_ge(ev("decay_made"), DECAYS[t] + k + 1)
                            nc.scalar.activation(sized(c_exp, t)[:, q * heads:(q + 1) * heads, :],
                                                 ps[5 + k % 2][:].rearrange("p (a n) -> p a n", n=size), ACT.Exp,
                                                 scale=float(D)).then_inc(ev("decay_copied"), 1)
                    act.wait_ge(ev("bc_made"), t + 1)
                    if t:
                        act.wait_ge(ev("tail_ready"), t)
                        act.wait_ge(ev("ssm1_kept"), t)
                    nc.scalar.activation(tails[0:size, :], ps[0][0:size, 0:HS], ACT.Exp)
                    nc.scalar.activation(dec_p[:], ps[0][:, HS:2 * HS], ACT.Exp, scale=float(D)).then_inc(ev("tails"), 1)
                act.wait_ge(ev("ssm1_kept"), 2)
                act.dma_start(d["out_ssm_p"], ssm1[:]).then_inc(s_out, 16)
                for b in range(NSEQ):
                    act.wait_ge(ev("ssm_new"), b + 1)
                    act.dma_start(d["out_ssm_s"][b], ssm[:, b % 2, :])\
                       .then_inc(ev("ssm_stored%d" % (b % 2)), 16)
                act.wait_ge(ev("ssd_ms"), 1)
                for g in range(GROUPS):
                    last = nc.scalar.activation(ro_r[g], ps[1 + g][:, 0:T], ACT.Ln, bias=eps_rms[:], scale=float(D) / 512)
                chain(last)
                for g in range(GROUPS):
                    last = nc.scalar.activation(ro_r[g], ro_r[g], ACT.Exp, scale=-0.5)
                last.then_inc(ev("ssd_r"), 1)
                for b in range(2):
                    act.wait_ge(ev("ssm_stored%d" % b), 16 * NSEQ // 2)
                for k in range(KD):
                    square(i, k, 0)

            act.wait_ge(s_load, 32)
            act.wait_ge(sc_clear, 1)
            nc.scalar.activation(sc[:, :, 0:NC], cT, ACT.Silu).then_inc(sc_ready, 1)
            for s in range(N_ADA):
                copy_raw(0, s)
            round_unit(0, True, 0, 0)
            modulate(0)
            for i in range(NBLK):
                if i == MIXERS[0]:
                    even_mixer(i)
                elif i == MIXERS[1]:
                    odd_mixer(i)
                else:
                    ffn(i)
                norm(i)
                if i in MIXERS:
                    if i == MIXERS[0]:
                        act.wait_ge(ev("even_stored"), 16 * 3)
                    else:
                        act.wait_ge(s_out, 16 * 2)
                if i + 1 < NBLK:
                    if i + 1 not in MIXERS:
                        round_unit(i + 1, True, 0, 0)
                    modulate(i + 1)

        @block.gpsimd
        def _(pool):
            nc.gpsimd.memset(sc[:], 0.0).then_inc(sc_clear, 1)
            nc.gpsimd.memset(ones_d[:], 1.0 / D).then_inc(s_const, 1)
            nc.gpsimd.memset(eps_rms[:], RMS_EPS).then_inc(ev("rms_eps"), 1)
            pool.wait_ge(ev("rms_eps"), 1)
            for i in range(NBLK):
                if i == MIXERS[0]:
                    pool.wait_ge(ev("even_in"), 3)
                    pool.wait_ge(w_done, BODY0[i] + N_IN[i])
                    pool.wait_ge(ev("even_landed"), 64)
                    for a in range(HR):
                        if a:
                            pool.wait_ge(ev("ret_state_add"), a)
                        v = vn[0:NS, 2, a * DVR:(a + 1) * DVR]
                        nc.gpsimd.tensor_tensor(vmask[0:NS], v.unsqueeze(1).to_broadcast([NS, NSEQ, DVR]),
                                                spread(sample_of[0:NS, :], DVR), ALU.mult)\
                          .then_inc(ev("ret_v_masked"), 1)
                if i == MIXERS[1]:
                    pool.wait_ge(ev("odd_in"), 2)
                    pool.wait_ge(w_done, BODY0[i] + N_IN[i])
                    for a in range(HR):
                        if a:
                            pool.wait_ge(ev("gla_state_add"), a)
                        v = gv[0:NS, 2, a * DVR:(a + 1) * DVR]
                        nc.gpsimd.tensor_tensor(gvmask[0:NS], v.unsqueeze(1).to_broadcast([NS, NSEQ, DVR]),
                                                spread(sample_of[0:NS, :], DVR), ALU.mult)\
                          .then_inc(ev("gla_v_masked"), 1)
                if i:
                    pool.wait_ge(stats_ready, i)
                nc.gpsimd.memset(ysum[:], 0.0).then_inc(sums_clear, 1)
                nc.gpsimd.memset(sqsum[:], 0.0).then_inc(sums_clear, 1)
                pool.wait_ge(sums_clear, 2 * (i + 1))
                for k in range(KD):
                    pool.wait_ge(y_done, KD * i + k + 1)
                    if KD * i + k:
                        pool.wait_ge(sumy_done, KD * i + k)
                    nc.gpsimd.tensor_tensor(ysum[:], ysum[:], y[:, k, :], ALU.add).then_inc(sumy_done, 1)
                    pool.wait_ge(sq_done, KD * i + k + 1)
                    if KD * i + k:
                        pool.wait_ge(sumq_done, KD * i + k)
                    nc.gpsimd.tensor_tensor(sqsum[:], sqsum[:], sq[:, k % RING, :], ALU.add).then_inc(sumq_done, 1)
                for k in range(KD):
                    pool.wait_ge(xhat_done, KD * i + k + 1)
                    nc.gpsimd.tensor_scalar(x[:, k, :], y[:, k, :], ln_g[:, i, k:k + 1], ln_b[:, i, k:k + 1],
                                            ALU.mult, ALU.add).then_inc(xnew_done, 1)

        @block.vector
        def _(dve):
            links = [0]

            def link(ins):
                links[0] += 1
                ins.then_inc(dve_chain, 1)
                dve.wait_ge(dve_chain, links[0])

            def prepare(i):
                dve.wait_ge(ada_turned, N_ADA * (i + 1))
                a = ps[BANK_ADA][:, 0:24 * NC].rearrange("p (m c) -> p m c", c=NC)
                link(nc.vector.tensor_tensor(ada[:], a, spread(b_ada[:, i, :], NC), ALU.add))
                shift, scale, gt = ada[:, 0:KD, :], ada[:, KD:2 * KD, :], ada[:, 2 * KD:3 * KD, :]
                if i:
                    g, b = spread(ln_g[:, i - 1, :], NC), spread(ln_b[:, i - 1, :], NC)
                    link(nc.vector.tensor_scalar(scale, scale, 1.0, None, ALU.add))
                    nc.vector.tensor_tensor(modA[:], scale, g, ALU.mult)
                    link(nc.vector.tensor_tensor(modB[:], scale, b, ALU.mult))
                    link(nc.vector.tensor_tensor(modB[:], modB[:], shift, ALU.add))
                else:
                    nc.vector.tensor_scalar(modA[:], scale, 1.0, None, ALU.add)
                    link(nc.vector.tensor_copy(modB[:], shift))
                coef = (1.0 if i in MIXERS else 0.5) / ALPHA
                nc.vector.tensor_scalar(gate[:], gt, coef, None, ALU.mult).then_inc(prep_done, 1)
                dve.wait_ge(prep_done, i + 1)
                src = y if i else x
                if i == 0:
                    dve.wait_ge(s_load, 48)
                link(nc.vector.tensor_tensor(samples(h), samples(src), spread(modA[:, :, 1:NC], TS), ALU.mult))
                nc.vector.tensor_tensor(samples(h), samples(h), spread(modB[:, :, 1:NC], TS), ALU.add)\
                  .then_inc(mod_sample, 1)
                if i in MIXERS:
                    return
                dve.wait_ge(mod_sample, i + 1)
                link(nc.vector.tensor_copy(samples(h_hi), samples(h)))
                rest_of_unit(i, True, 0, 0)
                for k in range(KD):
                    dve.wait_ge(h_hi_done, KD * ffn_index(i) + k + 1)
                    nc.vector.tensor_tensor(h_lo[:, k, :], h[:, k, :], h_hi[:, k, :].bitcast(F32), ALU.subtract)\
                      .then_inc(h_lo_done, 1)

            def rest_of_unit(i, up, s, j, it=0):
                n = BODY0[i] + (0 if up else N_UP) + s
                dve.wait_ge(w_hi_done, units_before(i, up, s, j) + 1 + it * (2 * RING))
                nc.vector.tensor_tensor(split_of(w_lo, j, up), unit_of(n, j, up), split_of(w_hi, j, up).bitcast(F32),
                                        ALU.subtract).then_inc(w_lo_done, 1)

            def residual(i, s, it):
                f = ps[BANK_DOWN[s % RING]]
                at = bass.ds(s + it * RING, 1)
                g = gate[:, at, :].rearrange("p a c -> p (a c)")
                xt = x[:, at, :].rearrange("p a t -> p (a t)")
                yt = y[:, at, :].rearrange("p a t -> p (a t)")
                nc.vector.scalar_tensor_tensor(out=yt[:, 0:TP], in0=f[:, 0:TP], scalar=g[:, 0:1],
                                               in1=xt[:, 0:TP], op0=ALU.mult, op1=ALU.add)
                nc.vector.tensor_tensor(gated[:, s % RING], samples(f[:, 0:T]), spread(g[:, 1:NC], TS), ALU.mult)\
                  .then_inc(gated_done, 1)
                dve.wait_ge(gated_done, KD * i + s + 1 + it * RING)
                nc.vector.tensor_tensor(samples(yt), gated[:, s % RING], samples(xt), ALU.add).then_inc(y_done, 1)

            def ffn(i):
                n0, f0 = BODY0[i], KF * ffn_index(i)

                def multiply(s, j, it):
                    dve.wait_ge(silu_done, f0 + 2 * s + j + 1 + it * (2 * RING))
                    nc.vector.tensor_tensor(hidden[:, bass.ds(2 * s + j + it * (2 * RING), 1), :]
                                            .rearrange("p a t -> p (a t)"),
                                            silu_g[:, j, :], ps[2 * j + 1][:, 0:T], ALU.mult).then_inc(hid_done, 1)

                def rest_of_hidden(s, j, it):
                    dve.wait_ge(hid_hi_done, f0 + 2 * s + j + 1 + it * (2 * RING))
                    at = bass.ds(2 * s + j + it * (2 * RING), 1)
                    part = [v[:, at, :].rearrange("p a t -> p (a t)") for v in (hidden, hidden_hi, hidden_lo)]
                    nc.vector.tensor_tensor(part[2], part[0], part[1].bitcast(F32), ALU.subtract).then_inc(hid_lo_done, 1)

                def up(s, it):
                    for j in range(2):
                        if s:
                            multiply(s - 1, j, it)
                        if s or j:
                            rest_of_unit(i, True, s, j, it)
                        if s:
                            rest_of_hidden(s - 1, j, it)
                slots(dve, N_UP, up)

                def down(s, it):
                    for j in range(2):
                        if s == 0:
                            multiply(N_UP - 1, j, 0)
                        elif j:
                            dve.wait_ge(w_done, n0 + N_UP + s + it * RING)
                            residual(i, s - 1, it)
                        elif s == 1 and i:
                            dve.wait_ge(xnew_done, KD * i)
                        rest_of_unit(i, False, s, j, it)
                        if s == 0:
                            rest_of_hidden(N_UP - 1, j, 0)
                slots(dve, N_DOWN, down)
                dve.wait_ge(w_done, n0 + N_FFN)
                residual(i, N_DOWN - 1, 0)

            def norm(i):
                mean, msq = ps[BANK_MEAN][:, 0:T], ps[BANK_MSQ][:, 0:T]
                dve.wait_ge(mean2_done, i + 1)
                nc.vector.scalar_tensor_tensor(out=var[:], in0=msq, scalar=LN_EPS, in1=mean2[:],
                                               op0=ALU.add, op1=ALU.subtract).then_inc(var_done, 1)
                link(nc.vector.tensor_tensor(y[:], y[:], mean.unsqueeze(1).to_broadcast([P, KD, T]), ALU.subtract))
                dve.wait_ge(rstd_done, i + 1)
                for k in range(KD):
                    nc.vector.tensor_tensor(y[:, k, :], y[:, k, :], rstd[:], ALU.mult).then_inc(xhat_done, 1)
                dve.wait_ge(xhat_done, KD * (i + 1))

            def rotate(z, banks, cos, sin, signal):
                link(nc.vector.tensor_tensor(z[:], z[:], cos.unsqueeze(1).to_broadcast([P, 2, T]), ALU.mult))
                for m in range(2):
                    last = nc.vector.tensor_tensor(silu_g[:, m, :], ps[banks[m]][:, 0:T], sin, ALU.mult)
                link(last)
                last = nc.vector.tensor_tensor(z[:], z[:], silu_g[:], ALU.add)
                if signal:
                    last.then_inc(ev(signal), 1)
                else:
                    link(last)

            def even_mixer(i):
                dve.wait_ge(ev("even_in"), 1)
                nc.vector.tensor_tensor(sq[:, 0:2, :], cq[:], cq[:], ALU.mult)
                nc.vector.tensor_tensor(sq[:, 2, :], ckv[:], ckv[:], ALU.mult).then_inc(ev("latent_sq"), 1)
                dve.wait_ge(ev("even_landed"), 64)
                dve.wait_ge(ev("latent_r"), 1)
                q_norm = even("q_norm")
                for m in range(2):
                    nc.vector.scalar_tensor_tensor(out=cq[:, m, :], in0=cq[:, m, :], scalar=q_norm[:, m:m + 1],
                                                   in1=var[:], op0=ALU.mult, op1=ALU.mult)
                nc.vector.scalar_tensor_tensor(out=lat[:], in0=ckv[:], scalar=even("kv_norm"), in1=rstd[:],
                                               op0=ALU.mult, op1=ALU.mult).then_inc(ev("latents"), 1)
                dve.wait_ge(ev("swapped_r"), 1)
                rotate(rq, (1, 3), even("cos_r"), even("sin_r"), None)
                rotate(rk, (2, 4), even("cos_r"), even("sin_r"), "rotated_r")
                dve.wait_ge(xnew_done, KD * i)
                dve.wait_ge(ev("rotated_r"), 1)
                for a in range(HR):
                    last = nc.vector.tensor_tensor(q_lead[:, a, :].rearrange("p (b t) -> p b t", t=TS), samples(rq[:, a // 2, :]),
                                                   lead_c[:, a, :].unsqueeze(1).to_broadcast([P, NSEQ, TS]), ALU.mult)
                link(last)
                dve.wait_ge(ev("swapped_m"), 1)
                rotate(qr, (5, 6), even("cos_m"), even("sin_m"), None)
                nc.vector.tensor_tensor(silu_g[:, 0, :], ps[7][:, 0:T], even("cos_m"), ALU.mult)
                link(nc.vector.tensor_tensor(silu_g[:, 1, :], ps[0][:, 0:T], even("sin_m"), ALU.mult))
                link(nc.vector.tensor_tensor(kr_rot[:], silu_g[:, 0, :], silu_g[:, 1, :], ALU.add))
                for m in range(4):
                    last = nc.vector.tensor_scalar(kr4[:, m, :], kr_rot[:], even("rows")[:, m:m + 1], None, ALU.mult)
                last.then_inc(ev("rotated_m"), 1)

                dve.wait_ge(ev("ret_k_turned"), 1)
                for t, (_, size) in enumerate(TOK):
                    last = nc.vector.tensor_tensor(ktail[0:size, t, :].rearrange("p (a k) -> p a k", k=DKR),
                                                   ps[1 + t][0:size, 0:HR * DKR].rearrange("p (a k) -> p a k", k=DKR),
                                                   spread(tail_c[0:size, t, :], DKR), ALU.mult)
                last.then_inc(ev("ret_k_tail"), 1)
                for a in range(HR):
                    dve.wait_ge(ev("ret_scores"), a + 1)
                    if a >= 2:
                        dve.wait_ge(ev("ret_o"), a - 1)
                    nc.vector.tensor_tensor(scores[:, a % 2, 0:3 * P], ps[4 + a % 2][:, 0:3 * P], decay_p[:, a, :], ALU.mult)
                    nc.vector.tensor_tensor(scores[0:NS, a % 2, 3 * P:], ps[4 + a % 2][0:NS, 3 * P:3 * P + NS],
                                            decay_s[0:NS, a, :], ALU.mult).then_inc(ev("ret_decayed"), 1)
                dve.wait_ge(ev("ret_state"), 1)
                nc.vector.tensor_copy(state_p[:].rearrange("p a n -> p (a n)"), ps[0][:, 0:2 * DVR])\
                  .then_inc(ev("ret_state_out"), 1)
                for a in range(HR):
                    dve.wait_ge(ev("ret_state_add"), a + 1)
                    for half in range(2):
                        st = state_r[rows64(a), 4 * half:4 * half + 4, a // 2, :]
                        last = nc.vector.scalar_tensor_tensor(
                            out=st, in0=st, scalar=float(GAMMA[a] ** TS),
                            in1=ps[5 + half][rows64(a), :].rearrange("p (b n) -> p b n", n=DVR),
                            op0=ALU.mult, op1=ALU.add)
                    last.then_inc(ev("ret_state_new"), 1)
                dve.wait_ge(ev("ret_r"), 1)
                for a in range(HR):
                    link(nc.vector.scalar_tensor_tensor(out=ro[:, a, :], in0=ro[:, a, :], scalar=even("ret_norm"),
                                                        in1=ro_r[a], op0=ALU.mult, op1=ALU.mult))
                nc.vector.tensor_tensor(mix[:, 4:8, :], ro[:], sgr[:], ALU.mult).then_inc(ev("ret_done"), 1)

                def prompt_max(a):
                    dve.wait_ge(ev("prompt_scores"), a + 1)
                    if a >= 2:
                        dve.wait_ge(ev("prompt_turned"), a - 1)
                    pr, u = prob[:, a % 2, :], a % 2
                    nc.vector.scalar_tensor_tensor(out=pr, in0=ps[2 + a % 2][:, 0:3 * P], scalar=ATT_SCALE,
                                                   in1=even("mask_p"), op0=ALU.mult, op1=ALU.add)\
                      .then_inc(ev("prompt_masked"), 1)
                    dve.wait_ge(ev("prompt_masked"), a + 1)
                    nc.vector.tensor_reduce(stat[:, u, 0:1], pr[:, 0:P], AX_X, ALU.max)
                    link(nc.vector.tensor_reduce(stat[:, u, 1:2], pr[:, P:3 * P], AX_X, ALU.max))
                    nc.vector.tensor_scalar(stat[:, u, :], stat[:, u, :], -1.0, None, ALU.mult)\
                      .then_inc(ev("prompt_max"), 1)

                def prompt_norm(a):
                    dve.wait_ge(ev("prompt_exp"), a + 1)
                    pr, u = prob[:, a % 2, :], a % 2
                    link(nc.vector.reciprocal(stat[:, 2 + u, :], stat[:, 2 + u, :]))
                    nc.vector.tensor_scalar(pr[:, 0:P], pr[:, 0:P], stat[:, 2 + u, 0:1], None, ALU.mult)
                    nc.vector.tensor_scalar(pr[:, P:3 * P], pr[:, P:3 * P], stat[:, 2 + u, 1:2], None, ALU.mult)\
                      .then_inc(ev("prompt_norm"), 1)

                prompt_max(0)
                for a in range(HM):
                    if a + 1 < HM:
                        prompt_max(a + 1)
                    prompt_norm(a)

                dve.wait_ge(ev("q_lat_copied"), HM)
                nc.vector.tensor_copy(q_ls[:].rearrange("p b (a t) -> p b a t", t=TS),
                                      q_lat[:, :, TP:T].rearrange("p a (b t) -> p b a t", t=TS))
                nc.vector.memset(q_rs[32:64], 0.0)
                for a in range(HM):
                    last = nc.vector.tensor_copy(
                        q_rs[0:ROPE].rearrange("p b (a t) -> p b a t", t=TS)[:, :, a, :],
                        qr[ROPE * (a % 4):ROPE * (a % 4 + 1), a // 4, TP:T].rearrange("p (b t) -> p b t", t=TS))
                last.then_inc(ev("sample_q"), 1)
                for p in range(NSEQ // 2):
                    dve.wait_ge(ev("sample_scores"), p + 1)
                    dve.wait_ge(ev("sample_copied"), p + 1)
                    nc.vector.scalar_tensor_tensor(out=prob_s[:, PAST:PAST + NS], in0=ps[4][:, 0:NS], scalar=ATT_SCALE,
                                                   in1=mask_s[:, p, :], op0=ALU.mult, op1=ALU.add)\
                      .then_inc(ev("sample_masked"), 1)
                    dve.wait_ge(ev("sample_masked"), p + 1)
                    link(nc.vector.tensor_reduce(stat[:, 0, 0:1], prob_s[:], AX_X, ALU.max))
                    nc.vector.tensor_scalar(stat[:, 0, 0:1], stat[:, 0, 0:1], -1.0, None, ALU.mult)\
                      .then_inc(ev("sample_max"), 1)
                    dve.wait_ge(ev("sample_exp"), p + 1)
                    link(nc.vector.reciprocal(stat[:, 2, 0:1], stat[:, 2, 0:1]))
                    nc.vector.tensor_scalar(prob_s[:], prob_s[:], stat[:, 2, 0:1], None, ALU.mult)\
                      .then_inc(ev("sample_norm"), 1)
                out_residual(i)

            def odd_mixer(i):
                dve.wait_ge(ev("odd_landed"), 48)
                nc.vector.memset(dtx[:], 0.0).then_inc(ev("dt_clear"), 1)
                nc.vector.memset(xpad[:, :, 0:CONV - 1], 0.0)
                nc.vector.tensor_copy(xpad[:, :, WP:].rearrange("p f (b t) -> p f b t", t=WS)[:, :, :, 0:CONV - 1], hist[:])
                nc.vector.memset(s_pair[:], 0.0)
                link(nc.vector.memset(s_samp[:], 0.0))
                dve.wait_ge(ev("small_copied"), 1)
                nc.vector.tensor_tensor(dtx[:], dtx[:], odd("dt_bias").unsqueeze(1).to_broadcast([P, NTOK, HS]), ALU.add)\
                  .then_inc(ev("dt_biased"), 1)
                dve.wait_ge(ev("dt_exp"), 1)
                link(nc.vector.tensor_scalar(dts[:], dtu[:], 2.0, None, ALU.add))
                link(nc.vector.reciprocal(dts[:], dts[:]))
                link(nc.vector.tensor_tensor(dts[:], dts[:], dtu[:], ALU.mult))
                link(nc.vector.tensor_tensor(dtu[:], dts[:], dts[:], ALU.mult))
                link(nc.vector.tensor_scalar(dtp[:], dtu[:], 1.0 / 15, None, ALU.mult))
                for k in (13, 11, 9, 7, 5, 3):
                    link(nc.vector.scalar_tensor_tensor(out=dtp[:], in0=dtp[:], scalar=1.0 / k, in1=dtu[:],
                                                        op0=ALU.add, op1=ALU.mult))
                link(nc.vector.scalar_tensor_tensor(out=dtp[:], in0=dtp[:], scalar=1.0, in1=dts[:],
                                                    op0=ALU.add, op1=ALU.mult))
                link(nc.vector.tensor_scalar(dtx[:], dtx[:], 0.0, None, ALU.max))
                link(nc.vector.scalar_tensor_tensor(out=dt[:], in0=dtp[:], scalar=2.0, in1=dtx[:],
                                                    op0=ALU.mult, op1=ALU.add))
                link(nc.vector.scalar_tensor_tensor(out=ua[:], in0=dt[:], scalar=-1.0,
                                                    in1=e_a[:].unsqueeze(1).to_broadcast([P, NTOK, HS]),
                                                    op0=ALU.mult, op1=ALU.mult))
                dve.wait_ge(ev("gate_log"), 1)
                link(nc.vector.scalar_tensor_tensor(out=gla[:], in0=gla[:], scalar=0.0, in1=ge[:],
                                                    op0=ALU.min, op1=ALU.subtract))
                for m in range(2):
                    last = nc.vector.tensor_tensor_scan(seg[:, m, :], odd("restart"), gla[:, m, :], 0.0, ALU.mult, ALU.add)
                link(last)

                def level_diff(k):
                    half = HALVES[k]
                    w = TP if half >= TS else T
                    v = seg[:, :, 0:w].rearrange("p m (n l) -> p m n l", l=2 * half)
                    nc.vector.tensor_tensor(ge[:, :, 0:w].rearrange("p m (n l) -> p m n l", l=2 * half), v,
                                            v[:, :, :, half - 1:half].to_broadcast([P, 2, w // (2 * half), 2 * half]),
                                            ALU.subtract).then_inc(ev("level_diff"), 1)

                def level_qk(k):
                    if k:
                        dve.wait_ge(ev("level_made"), k)
                    w = TP if HALVES[k] >= TS else T
                    dve.wait_ge(ev("level_exp"), k + 1)
                    nc.vector.tensor_tensor(qe[:, :, 0:w], gq[:, :, 0:w], ge[:, :, 0:w], ALU.mult)
                    nc.vector.tensor_tensor(ke[:, :, 0:w], gk[:, :, 0:w], ge[:, :, 0:w], ALU.mult)\
                      .then_inc(ev("level_qk"), 1)

                level_diff(0)
                level_qk(0)
                for k, half in enumerate(HALVES):
                    if k + 1 < len(HALVES) and HALVES[k + 1]:
                        dve.wait_ge(ev("level_qk"), k + 1)
                        level_diff(k + 1)
                        level_qk(k + 1)
                    elif half:
                        dve.wait_ge(ev("level_made"), k + 1)
                        nc.vector.memset(q_exp[:], 0.0).then_inc(ev("level_qk"), 1)
                    dve.wait_ge(ev("level_made"), k + 1)
                    pick = levels[:, k, :].bitcast(U32)
                    for e in range(2):
                        last = nc.vector.copy_predicated(s_pair[:, e], pick.unsqueeze(1).to_broadcast([P, 4, P]),
                                                         ps[6 + e][:].rearrange("p (a n) -> p a n", n=P))
                    if half < TS:
                        pick = levels[0:NS, k, 0:NS].bitcast(U32)
                        for e in range(2):
                            last = nc.vector.copy_predicated(s_samp[0:NS, e], pick.unsqueeze(1).to_broadcast([NS, 2, NS]),
                                                             ps[3 * e][0:NS, 0:2 * NS].rearrange("p (a n) -> p a n", n=NS))
                    last.then_inc(ev("level_picked"), 1)
                dve.wait_ge(ev("level_picked"), len(HALVES))
                for w0, w1, n in ((0, TP, P), (TP, T, TS)):
                    v = seg[:, :, w0:w1].rearrange("p m (n l) -> p m n l", l=n)
                    last = nc.vector.tensor_tensor(ge[:, :, w0:w1].rearrange("p m (n l) -> p m n l", l=n),
                                                   v[:, :, :, n - 1:n].to_broadcast([P, 2, (w1 - w0) // n, n]), v, ALU.subtract)
                last.then_inc(ev("tail_diff"), 1)
                dve.wait_ge(ev("gla_exps"), 1)
                nc.vector.tensor_tensor(ke[:], gk[:], ge[:], ALU.mult).then_inc(ev("gla_tail"), 1)
                for a in range(HR):
                    r, m = rows64(a), a // 2
                    last = nc.vector.tensor_tensor(q_exp[r, a, :], gq[r, m, P:T], qe[r, m, P:T], ALU.mult)
                dve.wait_ge(ev("gla_state"), 1)
                nc.vector.tensor_copy(st1[:].rearrange("p a n -> p (a n)"), ps[0][:, 0:2 * DVR]).then_inc(ev("gla_state1"), 1)
                dve.wait_ge(ev("gla_state1"), 1)
                for m in range(2):
                    last = nc.vector.scalar_tensor_tensor(out=st2[:, m, :], in0=st1[:, m, :], scalar=qe[:, m, TP - 1:TP],
                                                          in1=ps[3][:, m * DVR:(m + 1) * DVR], op0=ALU.mult, op1=ALU.add)
                last.then_inc(ev("gla_state2"), 1)
                dve.wait_ge(ev("gla_o"), HR)
                ends = qe[:, :, TP:T].rearrange("p m (b t) -> p b m t", t=TS)[:, :, :, TS - 1:TS]
                link(nc.vector.tensor_tensor(state_g[:], state_g[:], ends.to_broadcast([P, NSEQ, 2, DVR]), ALU.mult))
                for a in range(HR):
                    dve.wait_ge(ev("gla_state_add"), a + 1)
                    for half in range(2):
                        st = state_g[rows64(a), 4 * half:4 * half + 4, a // 2, :]
                        last = nc.vector.tensor_tensor(st, st, ps[5 + half][rows64(a), :].rearrange("p (b n) -> p b n", n=DVR),
                                                       ALU.add)
                    last.then_inc(ev("gla_state_new"), 1)
                dve.wait_ge(ev("gla_r"), 1)
                for a in range(HR):
                    last = nc.vector.scalar_tensor_tensor(out=go[:, a, :], in0=go[:, a, :], scalar=odd("gla_norm"),
                                                          in1=ro_r[a], op0=ALU.mult, op1=ALU.mult)
                link(last)
                dve.wait_ge(ev("odd_in"), 8)
                nc.vector.tensor_copy(conv_state[:, :, 0, :], xpad[:, :, WP - CONV + 1:WP])
                nc.vector.tensor_copy(conv_state[:, :, 1:NC, :],
                                      xpad[:, :, WP:].rearrange("p f (b t) -> p f b t", t=WS)[:, :, :, TS:WS])\
                  .then_inc(ev("conv_state"), 1)
                nc.vector.tensor_tensor(mix3[:, 0:4, :], go[:], gr[:], ALU.mult).then_inc(ev("gla_done"), 1)

                for f in range(NXC):
                    dve.wait_ge(ev("conv_first"), f + 1)
                    for k in range(1, CONV):
                        last = nc.vector.scalar_tensor_tensor(out=acc[f % 2], in0=xpad[:, f, k:k + CONV_OUT],
                                                              scalar=conv_w[:, k, f:f + 1], in1=acc[f % 2],
                                                              op0=ALU.mult, op1=ALU.add)
                        if k < CONV - 1:
                            link(last)
                    last.then_inc(ev("conv_added"), 1)
                for t, (_, size) in enumerate(TOK):
                    dve.wait_ge(ev("xs_turned"), t + 1)
                    dve.wait_ge(ev("bn_copied"), t + 1)
                    for g in range(GROUPS):
                        last = nc.vector.tensor_tensor(
                            xdt[0:size, t, g * 512:(g + 1) * 512].rearrange("p (a n) -> p a n", n=HDIM),
                            ps[1 + g][0:size, :].rearrange("p (a n) -> p a n", n=HDIM),
                            spread(dt[0:size, t, g * 8:(g + 1) * 8], HDIM), ALU.mult)
                    last.then_inc(ev("xs_copied"), 1)
                for t, (t0, size) in enumerate(TOK):
                    upto = odd("upto") if t < 2 else odd("upto_s")[0:NS, :]
                    if t:
                        dve.wait_ge(ev("decay_made"), DECAYS[t])
                    else:
                        dve.wait_ge(ev("conv_done"), NXC)
                    nc.vector.tensor_tensor(steps_of(t)[0:size], spread(ua[0:size, t, :], size),
                                            upto.unsqueeze(1).to_broadcast([size, HS, size]), ALU.mult)\
                      .then_inc(ev("steps"), 1)
                    dve.wait_ge(ev("bc_made"), t + 1)
                    link(nc.vector.tensor_tensor(gm[0:size, :, 0:size],
                                                 ps[7][0:size, 0:2 * size].rearrange("p (a n) -> p a n", n=size),
                                                 upto.unsqueeze(1).to_broadcast([size, 2, size]), ALU.mult))
                    dve.wait_ge(ev("tails"), t + 1)
                    if t == 2:
                        link(nc.vector.tensor_copy(dec_s[:].rearrange("p b a -> p a b"),
                                                   c_exp_s.rearrange("p a (b t) -> p a b t", t=TS)[:, :, :, TS - 1]))
                    for g in range(GROUPS):
                        hs = slice(8 * g, 8 * g + 8)
                        last = nc.vector.tensor_tensor(att_of(t)[0:size, hs, :], att_of(t)[0:size, hs, :],
                                                       gm[0:size, g, 0:size].unsqueeze(1).to_broadcast([size, 8, size]), ALU.mult)
                        if t:
                            ce = sized(c_exp, t)[:, hs, :]
                            last = nc.vector.tensor_tensor(ce, ce, xc[:, NXS + GROUPS + g, t0:t0 + size].unsqueeze(1)
                                                           .to_broadcast([P, 8, size]), ALU.mult)
                    last.then_inc(ev("att_ready"), 1)
                    if t:
                        dve.wait_ge(ev("ssm_add"), t)
                    nc.vector.tensor_tensor(xdt_tail[0:size, :].rearrange("p (a n) -> p a n", n=HDIM),
                                            xdt[0:size, t, :].rearrange("p (a n) -> p a n", n=HDIM),
                                            spread(tails[0:size, :], HDIM), ALU.mult).then_inc(ev("tail_ready"), 1)
                    dve.wait_ge(ev("ssd_y"), t + 1)
                    for f in range(NXS):
                        last = nc.vector.scalar_tensor_tensor(
                            out=xc[:, f, t0:t0 + size], in0=xc[:, f, t0:t0 + size], scalar=odd("d_skip")[:, f:f + 1],
                            in1=ps[1 + f // 4][:, (f % 4) * size:(f % 4 + 1) * size], op0=ALU.mult, op1=ALU.add)
                    last.then_inc(ev("y_kept"), 1)
                    if t < 2:
                        dve.wait_ge(ev("ssm_add"), t + 1)
                        if t:
                            link(nc.vector.tensor_tensor(ssm1[:].rearrange("p (a n) -> p a n", n=HDIM),
                                                         ssm1[:].rearrange("p (a n) -> p a n", n=HDIM),
                                                         spread(dec_p[:], HDIM), ALU.mult))
                        for g in range(GROUPS):
                            part = ssm1[:, g * 512:(g + 1) * 512]
                            if t:
                                last = nc.vector.tensor_tensor(part, part, ps[3 + g][:], ALU.add)
                            else:
                                last = nc.vector.tensor_copy(part, ps[3 + g][:])
                        last.then_inc(ev("ssm1_kept"), 1)
                nc.vector.tensor_tensor(b_masked[0:NS], bn[0:NS, 2, :].unsqueeze(1).to_broadcast([NS, NSEQ, GROUPS * DSTATE]),
                                        spread(sample_of[0:NS, :], GROUPS * DSTATE), ALU.mult).then_inc(ev("b_masked"), 1)
                for b in range(NSEQ):
                    dve.wait_ge(ev("ssm_add_s"), b + 1)
                    st = ssm[:, b % 2, :]
                    link(nc.vector.tensor_tensor(st.rearrange("p (a n) -> p a n", n=HDIM),
                                                 st.rearrange("p (a n) -> p a n", n=HDIM),
                                                 spread(dec_s[:, b, :], HDIM), ALU.mult))
                    for g in range(GROUPS):
                        last = nc.vector.tensor_tensor(st[:, g * 512:(g + 1) * 512], st[:, g * 512:(g + 1) * 512],
                                                       ps[3 + g][:], ALU.add)
                    last.then_inc(ev("ssm_new"), 1)
                dve.wait_ge(ev("y_kept"), NTOK)
                link(nc.vector.tensor_tensor(xc[:, 0:NXS, TP:T], xc[:, 0:NXS, TP:T],
                                             ps[7][:].rearrange("p (f n) -> p f n", n=NS), ALU.add))
                link(nc.vector.tensor_tensor(xc[:, 0:NXS, :], xc[:, 0:NXS, :], zs[:], ALU.mult))
                nc.vector.tensor_tensor(ysq[:], xc[:, 0:NXS, :], xc[:, 0:NXS, :], ALU.mult).then_inc(ev("gated_sq"), 1)
                dve.wait_ge(ev("ssd_r"), 1)
                for f in range(NXS):
                    last = nc.vector.scalar_tensor_tensor(out=mix3[:, 4 + f, :], in0=xc[:, f, :],
                                                          scalar=odd("ssm_norm")[:, f:f + 1], in1=ro_r[f // 4],
                                                          op0=ALU.mult, op1=ALU.mult)
                last.then_inc(ev("mix3_ready"), 1)
                out_residual(i)

            def out_residual(i):
                tiles = KD // N_OUT[i]
                dve.wait_ge(xnew_done, KD * i)
                for k in range(KD):
                    if k % tiles == tiles - 1:
                        dve.wait_ge(w_done, OUT0[i] + k // tiles + 1)
                    else:
                        dve.wait_ge(out_tile, OUT_TILE0[i] + k // tiles * (tiles - 1) + k % tiles + 1)
                    residual(i, k, 0)

            dve.wait_ge(s_load, 32)
            prepare(0)
            for i in range(NBLK):
                if i == MIXERS[0]:
                    even_mixer(i)
                elif i == MIXERS[1]:
                    odd_mixer(i)
                else:
                    ffn(i)
                norm(i)
                if i + 1 < NBLK:
                    prepare(i + 1)


def kernel(**inputs):
    import numpy as _np
    import concourse.bacc as _bacc
    from concourse import mybir as _mybir
    from concourse.bass_utils import run_bass_kernel_spmd as _run

    a = {k: _np.asarray(v) for k, v in inputs.items()}

    def slots_of(w, width):
        *lead, k, n = w.shape
        w = w.reshape(-1, k // P, P, n // width, width)
        return _np.ascontiguousarray(w.transpose(0, 3, 2, 1, 4)).reshape(-1, P, k // P * width)

    def features(w):
        w = w.reshape(*w.shape[:-1], w.shape[-1] // P, P)
        return _np.moveaxis(w, -1, 0).reshape(P, -1)

    tokens = _np.concatenate([a["x_prompt"].reshape(TP, D), a["x_sample"].reshape(NSEQ * TS, D)])
    cond = _np.concatenate([a["c_prompt"], a["c_sample"]])
    up = _np.stack([slots_of(a["ffn_w1"].reshape(4, D, FF), 2 * P), slots_of(a["ffn_w3"].reshape(4, D, FF), 2 * P)], 2)
    arrays = {
        "xT": tokens.T.reshape(KD, P, T).transpose(1, 0, 2),
        "params": _np.concatenate([features(a["ln_g"].reshape(NBLK, D)), features(a["ln_b"].reshape(NBLK, D)),
                                   features(a["b_ada"].reshape(NBLK, 3 * D)),
                                   cond.T.reshape(KD, P, NC).transpose(1, 0, 2).reshape(P, -1)], 1),
        "w_ada": slots_of(a["w_ada"], 512),
        "w_up": up.reshape(-1, P, SLOT),
        "w_down": slots_of(a["ffn_w2"].reshape(4, FF, D), P),
    }
    add_turn = _np.zeros((P, WIDE), _np.float32)
    for c in range(NC):
        add_turn[c::32, c] = 1.0
    arrays["add_turn"] = add_turn
    uq = a["w_uq"][0].reshape(QRANK, HM, NOPE + ROPE)
    uq = _np.concatenate([uq[:, :, :NOPE].reshape(QRANK, -1), uq[:, :, NOPE:].reshape(QRANK, -1)], 1)
    given = even_constants()
    given["w_uq"] = uq.reshape(2, P, -1).transpose(1, 0, 2)
    given["w_uk"] = a["w_uk"][0].reshape(RANK, HM // 2, 2 * NOPE).transpose(2, 1, 0)
    given["w_uv"] = a["w_uv"][0].reshape(RANK, HM * VM)
    given["q_norm"], given["kv_norm"] = features(a["mla_q_norm"][0]), features(a["mla_kv_norm"][0])
    given["ret_norm"] = features(a["ret_norm"][0])
    arrays["even_consts"] = _np.concatenate([given[k].reshape(P, -1) for k in EVEN_CONSTS], 1)
    w = a["w_in_even"][0]
    w = _np.concatenate([w[:, :416], w[:, 320:416], w[:, 416:]], 1)
    arrays["w_in_even"] = slots_of(w, 512)
    arrays["w_out_even"] = slots_of(a["w_out_even"][0], 512)
    lat = a["cache_mla_latent"][0]
    rope = a["cache_mla_krope"][0].transpose(0, 2, 1)
    rope = _np.concatenate([rope, _np.zeros((rope.shape[0], P - ROPE, PAGE), rope.dtype)], 1)
    arrays["cache"] = _np.concatenate([lat.transpose(0, 2, 1), lat, rope], 2)
    arrays["pages"] = a["page_table"].reshape(1, -1)
    arrays["ident"] = _np.eye(P, dtype=_np.float32)
    arrays["sample_of"] = (_np.arange(P)[:, None] // TS == _np.arange(NSEQ)[None, :]).astype(_np.float32)

    def state(s):
        return s.reshape(NSEQ, 2, 2, DKR, DVR).transpose(2, 3, 0, 1, 4).reshape(P, NSEQ, 2, DVR)

    def state_back(s):
        s = s.reshape(2, DKR, -1, 2, DVR)
        return s.transpose(2, 3, 0, 1, 4).reshape(1, -1, HR, DKR, DVR)
    arrays["state_r"] = state(a["state_retention"][0])
    given = odd_constants()
    w = a["w_in_odd"][0]
    low, rest, dts = w[:, 1024:1040], _np.concatenate([w[:, :1024], w[:, 1040:4112]], 1), w[:, 4112:]
    arrays["w_in_odd"] = slots_of(rest, 512)
    arrays["w_out_odd"] = slots_of(a["w_out_odd"][0], 2 * P)
    given["w_small"] = _np.concatenate([low, dts], 1).reshape(KD, P, 2 * GATE_RANK).transpose(1, 0, 2)
    given["w_gate"] = _np.concatenate([a["gla_w_gate"][0], _np.zeros((P - GATE_RANK, HR * DKR), _np.float32)])
    given["b_gate"], given["gla_norm"] = features(a["gla_b_gate"][0]), features(a["gla_norm"][0])
    given["conv_w"], given["conv_b"] = features(a["ssm_conv_w"][0]), features(a["ssm_conv_b"][0])
    given["dt_bias"] = _np.broadcast_to(a["ssm_dt_bias"][0], (P, HS))
    given["a_log"] = _np.broadcast_to(a["ssm_a_log"][0], (P, HS))
    given["d_skip"] = features(_np.repeat(a["ssm_d"][0], HDIM))
    given["ssm_norm"] = features(a["ssm_norm"][0])
    arrays["odd_consts"] = _np.concatenate([given[k].reshape(P, -1) for k in ODD_CONSTS], 1)
    arrays["state_g"] = state(a["state_gla"][0])
    arrays["state_ssm"] = a["state_ssm"][0].transpose(0, 2, 1, 3).reshape(NSEQ, DSTATE, INNER)
    arrays["conv_hist"] = a["state_conv"][0].reshape(NSEQ, CONV - 1, NXC, P).transpose(3, 2, 0, 1)
    outs = {"out_gla_p": (P, HR // 2, DVR), "out_gla_s": (P, NSEQ, HR // 2, DVR), "out_ssm_p": (P, INNER),
            "out_ssm_s": (NSEQ, P, INNER), "out_conv": (P, NXC, NC, CONV - 1), "out_lat": (P, T), "out_krope": (ROPE, T), "out_ret_p": (P, HR // 2, DVR),
            "out_ret_s": (P, NSEQ, HR // 2, DVR), "yT": (P, KD, T)}
    nc = _bacc.Bacc("TRN2", target_bir_lowering=False, num_devices=1)
    arrays = {k: _np.ascontiguousarray(v) for k, v in arrays.items()}
    dram = {k: nc.dram_tensor(f"dram_{k}", v.shape, _mybir.dt.from_np(v.dtype), kind="ExternalInput").ap()
            for k, v in arrays.items()}
    for k, shape in outs.items():
        dram[k] = nc.dram_tensor(f"dram_{k}", shape, F32, kind="ExternalOutput").ap()
    build(nc, dram)
    r = _run(nc, [{f"dram_{k}": v for k, v in arrays.items()}], core_ids=[0]).results[0]
    def tokens_back(v):
        v = v.T
        return v[:TP][None], v[TP:].reshape(NSEQ, TS, -1)

    y_p, y_s = tokens_back(r["dram_yT"].transpose(1, 0, 2).reshape(D, T))
    lat_p, lat_s = tokens_back(r["dram_out_lat"])
    kr_p, kr_s = tokens_back(r["dram_out_krope"])
    conv = r["dram_out_conv"].transpose(2, 3, 1, 0).reshape(1, NC, CONV - 1, NXC * P)
    ssm_p = r["dram_out_ssm_p"].reshape(1, 1, DSTATE, HS, HDIM).transpose(0, 1, 3, 2, 4)
    ssm_s = r["dram_out_ssm_s"].reshape(1, NSEQ, DSTATE, HS, HDIM).transpose(0, 1, 3, 2, 4)
    return (y_p, y_s, lat_p[None], lat_s[None], kr_p[None], kr_s[None],
            state_back(r["dram_out_ret_p"]), state_back(r["dram_out_ret_s"]),
            state_back(r["dram_out_gla_p"]), state_back(r["dram_out_gla_s"]), ssm_p, ssm_s, conv[:, :1], conv[:, 1:])
```

```python
from contextlib import ExitStack

import concourse.bass as bass
from concourse import mybir
import numpy as np

F32 = mybir.dt.float32
F32R = mybir.dt.float32r
U32 = mybir.dt.uint32
I32 = mybir.dt.int32
ALU = mybir.AluOpType
ACT = mybir.ActivationFunctionType
AX_X = mybir.AxisListType.X

P = 128
D = 1024
KD = D // P
TP, NSEQ, TS = 256, 8, 8
T = TP + NSEQ * TS
NC = 1 + NSEQ
FF = 2816
KF = FF // P
DEPTH = 2
NBLK = 3 * DEPTH
ALPHA = (2.0 * DEPTH) ** 0.25
LN_EPS = 1e-5 / ALPHA ** 2

RING = 3
ARENA = 27300
SLOT = 4096
N_ADA = 3 * D // 512
N_UP = KF // 2
N_DOWN = KD
N_FFN = N_UP + N_DOWN
UNIT = SLOT // 2
N_IN = {1: 4, 4: 8}
N_OUT = {1: 2, 4: 4}
MIXERS = (1, 4)
PER_STATE = 4
N_PAST = {1: 8, 4: 2}

N_STORES = 2 + 1

OUT_TILE0 = {1: 0, 4: KD - N_OUT[1]}

N_EARLY = 4
ADA, BODY0, OUT0 = [list(range(N_ADA))], [], {}
_n = N_ADA
for _i in range(NBLK):
    _next = _i + 1 < NBLK
    BODY0.append(_n)
    if _i in MIXERS:
        _n += N_IN[_i] + N_PAST[_i]
        _ada = list(range(_n, _n + N_EARLY))
        OUT0[_i] = _n + N_EARLY
        _n = OUT0[_i] + N_OUT[_i]
    else:
        _down = _n + N_UP + 2
        _ada = [_n + 1, _n + 3, _down + 1, _down + 3]
        _n += N_FFN + (N_EARLY if _next else 0)
    if _next:
        ADA.append(_ada + [_n, _n + 1])
        _n += N_ADA - N_EARLY
N_SLOTS = _n
PAST0 = BODY0[MIXERS[0]] + N_IN[MIXERS[0]]
STATE0 = BODY0[MIXERS[1]] + N_IN[MIXERS[1]]

BANK_DOWN = (4, 5, 6)
BANKS_IN = (1, 2, 4, 5)
BANK_MEAN, BANK_MSQ, BANK_ADA = 2, 3, 7
WIDE = 96


HM, RANK, NOPE, ROPE, VM = 8, 128, 64, 32, 64
QRANK = 256
HR, DKR, DVR = 4, 64, 128
PAGE, NPAGES = 128, 8
PAST = PAGE * NPAGES
ATT_SCALE = (NOPE + ROPE) ** -0.5
RMS_EPS = 1e-6
NTOK = 3
NS = NSEQ * TS
TOK = ((0, P), (P, P), (TP, NS))
GAMMA = 1.0 - np.exp2(-5.0 - np.arange(HR))
MASKED = -1e30


def packed(widths):
    at, out = 0, {}
    for name, width in widths:
        out[name] = (at, width)
        at += width
    return out, at


EVEN_CONSTS, N_EVEN_CONSTS = packed([
    ("w_uq", 2 * HM * (NOPE + ROPE)), ("w_uk", HM // 2 * RANK), ("w_uv", HM * VM),
    ("q_norm", 2), ("kv_norm", 1), ("ret_norm", 1),
    ("cos_m", T), ("sin_m", T), ("cos_r", T), ("sin_r", T), ("swap_m", P), ("swap_r", P), ("place", 2 * P),
    ("mask_p", 3 * P), ("mask_s", NSEQ * NS), ("decay_p", HR * 3 * P), ("decay_s", HR * NS),
    ("tail", NTOK * HR), ("lead", HR * TS), ("rows", 4)])


def even_constants():
    f = np.float32
    out = {}
    pos = np.concatenate([np.arange(TP), PAST + np.tile(np.arange(TS), NSEQ)]).astype(f)

    def rotary(width, copies):
        half = width // 2
        inv = (f(10000.0) ** (-np.arange(half, dtype=f) / f(half))).astype(f)
        ang = (pos[None, :] * inv[:, None]).astype(f)
        cos, sin = np.cos(ang).astype(f), np.sin(ang).astype(f)
        return np.tile(np.concatenate([cos, cos]), (copies, 1)), np.tile(np.concatenate([-sin, sin]), (copies, 1))
    out["cos_m"], out["sin_m"] = rotary(ROPE, P // ROPE)
    out["cos_r"], out["sin_r"] = rotary(DKR, P // DKR)
    i = np.arange(P)

    def swap(width):
        m = np.zeros((P, P), f)
        m[i, i // width * width + (i % width + width // 2) % width] = 1.0
        return m
    out["swap_m"], out["swap_r"] = swap(ROPE), swap(DKR)
    place = np.zeros((P, 2, P), f)
    place[i % ROPE, 0, i] = 1.0
    place[(i % ROPE + ROPE // 2) % ROPE, 1, i] = 1.0
    out["place"] = place.reshape(P, -1)
    later = np.where(i[None, :] > i[:, None], f(MASKED), f(0))
    out["mask_p"] = np.concatenate([later, np.zeros((P, P), f), later], 1)
    row_t = i % TS
    col = np.arange(NS)
    mask_s = np.full((P, NSEQ, NS), MASKED, f)
    for b in range(NSEQ):
        mask_s[:, b][(col[None, :] // TS == b) & (col[None, :] % TS <= row_t[:, None])] = 0.0
    out["mask_s"] = mask_s.reshape(P, -1)
    step = i[None, :] - i[:, None]
    decay_p = np.zeros((P, HR, 3, P))
    decay_s = np.zeros((P, HR, NS))
    tail = np.zeros((P, NTOK, HR))
    lead = np.zeros((P, HR, TS))
    same = (col[:, None] // TS == col[None, :] // TS) & (col[:, None] <= col[None, :])
    for h in range(HR):
        g = GAMMA[h]
        diag = np.where(step >= 0, g ** np.maximum(step, 0), 0.0)
        decay_p[:, h, 0] = decay_p[:, h, 2] = diag
        decay_p[:, h, 1] = g ** (step + P)
        decay_s[:NS, h] = np.where(same, g ** np.maximum(col[None, :] - col[:, None], 0), 0.0)
        tail[:, 0, h], tail[:, 1, h] = g ** (TP - 1 - i), g ** (P - 1 - i)
        tail[:NS, 2, h] = g ** (TS - 1 - col % TS)
        lead[64 * (h % 2):64 * (h % 2) + 64, h] = g ** (1 + np.arange(TS))
    out["decay_p"], out["decay_s"] = decay_p.reshape(P, -1), decay_s.reshape(P, -1)
    out["tail"], out["lead"] = tail.reshape(P, -1), lead.reshape(P, -1)
    out["rows"] = (i[:, None] // ROPE == np.arange(4)[None, :])
    return {k: v.astype(f) for k, v in out.items()}


GATE_RANK, TAU = 16, 16.0
HS, HDIM, GROUPS, DSTATE, CONV = 16, 64, 2, 128, 4
INNER = HS * HDIM
NXS, NXC = INNER // P, (INNER + 2 * GROUPS * DSTATE) // P
WP = CONV - 1 + TP
WS = CONV - 1 + TS
PADDED = WP + NSEQ * WS
CONV_OUT = PADDED - (CONV - 1)
HALVES = (64, 32, 16, 8, 4, 2, 1, 0)
ODD_CONSTS, N_ODD_CONSTS = packed([
    ("w_small", KD * 2 * GATE_RANK), ("w_gate", HR * DKR), ("b_gate", 2), ("gla_norm", 1),
    ("conv_w", CONV * NXC), ("conv_b", NXC), ("dt_bias", HS), ("a_log", HS), ("d_skip", NXS), ("ssm_norm", NXS),
    ("restart", T), ("levels", len(HALVES) * P), ("upto", P), ("upto_s", NS), ("after", P), ("after_s", NS),
    ("head_rows", 2)])


def odd_constants():
    i = np.arange(P)
    out = {}
    restart = np.ones((P, T))
    restart[:, [0, P, *range(TP, T, TS)]] = 0.0
    out["restart"] = restart
    levels = np.zeros((P, len(HALVES), P))
    for n, half in enumerate(HALVES):
        if half:
            b = i // (2 * half)
            levels[:, n] = (b[:, None] == b[None, :]) & (i[:, None] % (2 * half) < half) & (i[None, :] % (2 * half) >= half)
        else:
            levels[:, n] = np.eye(P)
    out["levels"] = levels
    out["upto"] = i[:, None] <= i[None, :]
    out["after"] = i[:, None] > i[None, :]
    same = i[:, None] // TS == i[None, :NS] // TS
    out["upto_s"] = (i[:, None] <= i[None, :NS]) & same
    out["after_s"] = (i[:, None] > i[None, :NS]) & same
    out["head_rows"] = i[:, None] // DKR == np.arange(2)[None, :]
    return {k: v.astype(np.float32) for k, v in out.items()}


def param_columns():
    at, out = 0, {}
    for name, width in (("ln_g", NBLK * KD), ("ln_b", NBLK * KD), ("b_ada", NBLK * 24), ("c", KD * NC)):
        out[name] = (at, width)
        at += width
    return out, at


def body_slot(i, up, s):
    extra = 2 if i + 1 < NBLK else 0
    return BODY0[i] + (0 if up else N_UP + extra) + s + min(s, extra)


def done_before(i, up, s):
    n = body_slot(i, up, s)
    return n - 1 if s == 1 and i + 1 < NBLK else n


def raw_bank(i, s):
    within_up = i > 0 and i - 1 not in MIXERS and s < 2
    return (5, 6)[s] if within_up else s % 2


def ffn_index(i):
    return [j for j in range(NBLK) if j not in MIXERS].index(i)


def build(nc, d):
    ctx = ExitStack()
    with ctx:
        def sb(name, shape, dt=F32):
            return ctx.enter_context(nc.sbuf_tensor(name, shape, dt))

        def sem(name):
            return ctx.enter_context(nc.semaphore(name))

        ring = sb("ring", [P, RING, SLOT])
        x = sb("x", [P, KD, T])
        y = sb("y", [P, KD, T])
        sq = sb("sq", [P, 3, T])
        ysum = sb("ysum", [P, T])
        sqsum = sb("sqsum", [P, T])
        mean2 = sb("mean2", [P, T])
        var = sb("var", [P, T])
        rstd = sb("rstd", [P, T])
        silu_g = sb("silu_g", [P, 2, T])
        gated = sb("gated", [P, 3, NSEQ, TS])
        cols, n_params = param_columns()
        params = sb("params", [P, n_params])
        sc = sb("sc", [P, KD, 32])
        ada_raw = sb("ada_raw", [P, 2, 512])
        add_turn = sb("add_turn", [P, WIDE])
        ada = sb("ada", [P, 24, NC])
        modA = sb("modA", [P, KD, NC])
        modB = sb("modB", [P, KD, NC])
        gate = sb("gate", [P, KD, NC])
        ones_d = sb("ones_d", [P, P])
        eps_rms = sb("eps_rms", [P, 1])
        ident = sb("ident", [P, P])
        sample_of = sb("sample_of", [P, NSEQ])
        pages = sb("pages", [1, NSEQ * NPAGES], I32)
        stat = sb("stat", [P, 4, 2])
        stat_s = sb("stat_s", [P, 2, 9])
        with nc.sbuf_tensor("h", [P, KD, T], F32) as h, nc.sbuf_tensor("arena", [P, ARENA], F32) as arena:
            pass
        ps = [ctx.enter_context(nc.psum_tensor(f"ps{b}", [P, 512], F32)) for b in range(8)]

        def param(name, *shape):
            at, width = cols[name]
            v = params[:, at:at + width]
            return v.rearrange("p (a b) -> p a b", b=shape[-1]) if shape else v

        ln_g, ln_b = param("ln_g", KD), param("ln_b", KD)
        b_ada, cT = param("b_ada", 24), param("c", NC)
        hidden = arena[:, 0:KF * T].rearrange("p (f t) -> p f t", t=T)
        h_lo = sb("h_lo", [P, KD, T], F32R)
        hidden_lo = sb("hidden_lo", [P, KF, T], F32R)
        hidden_hi = sb("hidden_hi", [P, KF, T], F32R)
        w_hi = sb("w_hi", [P, 2, UNIT], F32R)
        w_lo = sb("w_lo", [P, 2, UNIT], F32R)
        h_hi = sb("h_hi", [P, KD, T], F32R)
        assert 2 * KF * T + 4 * UNIT + KD * T <= ARENA
        taken = [0]

        def lay(*shape, at=None, of=None):
            n = int(np.prod(shape))
            start = taken[0] if at is None else at
            if at is None:
                taken[0] += n
                assert taken[0] <= ARENA, taken
            v = (arena if of is None else of)[:, start:start + n]
            names = "abcd"[:len(shape)]
            if len(shape) == 1:
                return v
            return v.rearrange(f"p ({' '.join(names)}) -> p {' '.join(names)}", **dict(zip(names[1:], shape[1:])))

        y_flat = y[:].rearrange("p k t -> p (k t)")
        h_flat = h[:].rearrange("p k t -> p (k t)")

        cq = lay(2, T)
        ckv = lay(T)
        kr = lay(T)
        rq = lay(2, T)
        rk = lay(2, T)
        vn = lay(NTOK, HR * DVR)
        sgr = lay(HR, T)
        qn = lay(HM // 2, T)
        kr_rot = lay(T)
        q_ls = lay(NSEQ, HM * TS, at=0)
        q_rs = lay(NSEQ, HM * TS, at=NSEQ * HM * TS)
        prob = lay(2, 3 * P, at=4 * T)
        prob_t = lay(2, 3 * P, at=4 * T + 6 * P)
        assert 12 * P <= (2 + 2 + 4) * T + NTOK * HR * DVR
        taken[0] = KF * T
        even_c = lay(N_EVEN_CONSTS)
        state_r = lay(NSEQ, HR // 2, DVR)
        mix = lay(KD, T)
        lat = lay(T)
        qr = lay(2, T)
        kr4 = lay(4, T)
        lat_n = lay(NTOK, RANK)
        prob_s = lay(2, PAST // 2 + NS)
        inverse = lay(2, P)
        prob_st = lay(NPAGES + 2, NS)
        ktail = lay(NTOK, HR * DKR, of=y_flat, at=0)
        scores = lay(2, 3 * P + NS, of=y_flat, at=NTOK * HR * DKR)
        q_lead = lay(HR, NS, of=y_flat, at=NTOK * HR * DKR + 2 * (3 * P + NS))
        vmask = lay(NSEQ, DVR, of=h_flat, at=0)
        ro = lay(HR, T, of=h_flat, at=NSEQ * DVR)
        state_p = lay(HR // 2, DVR, of=h_flat, at=NSEQ * DVR + HR * T)
        q_lat = lay(HM, T, of=y_flat, at=0)
        o_lat = lay(HM, T, of=h_flat, at=0)
        ro_sq = [sq[:, 0, :], sq[:, 1, :], sq[:, 2, :], mean2[:]]
        ro_r = [silu_g[:, 0, :], silu_g[:, 1, :], var[:], rstd[:]]

        def even(name, *shape):
            at, width = EVEN_CONSTS[name]
            v = even_c[:, at:at + width]
            return v.rearrange("p (a b) -> p a b", b=shape[-1]) if shape else v

        w_uq, w_uk, w_uv = even("w_uq", HM * (NOPE + ROPE)), even("w_uk", RANK), even("w_uv")
        decay_p, decay_s = even("decay_p", 3 * P), even("decay_s", NS)
        place, mask_s, tail_c, lead_c = even("place", P), even("mask_s", NS), even("tail", HR), even("lead", TS)

        taken[0] = 0
        gla0 = 0
        gq = lay(2, T)
        gk = lay(2, T)
        gv = lay(NTOK, HR * DVR)
        gr = lay(HR, T)
        glr = lay(T)
        seg = lay(2, T)
        s_pair = lay(2, 4, P)
        s_samp = lay(2, 2, NS)
        q_exp = lay(HR, P + NS)
        gktail = lay(NTOK, HR * DKR)
        st1 = lay(HR // 2, DVR)
        st2 = lay(HR // 2, DVR)
        gla_end = taken[0]
        assert gla_end >= KF * T
        odd_c = lay(N_ODD_CONSTS)
        state_g = lay(NSEQ, HR // 2, DVR)
        hist = lay(NXC, NSEQ, CONV - 1)
        zs = lay(NXS, T)
        xpad = lay(NXC, PADDED)
        mix3 = lay(NXC, T)
        conv_state = lay(NXC, NC, CONV - 1)
        dtx, dt, dtu, dts, dtp, ua = (lay(NTOK, HS) for _ in range(6))
        e_a = lay(HS)
        tails = lay(HS)
        dec_p = lay(HS)
        dec_s = lay(NSEQ, HS)
        gla, ge, qe, ke = (lay(2, T, of=y_flat, at=2 * T * j) for j in range(4))
        gvmask = lay(NSEQ, DVR, of=h_flat, at=0)
        go = lay(HR, T, of=h_flat, at=NSEQ * DVR)
        xc = lay(NXC, T, at=0)
        xdt = lay(NTOK, INNER, at=NXC * T)
        ssm1 = lay(INNER, at=NXC * T + NTOK * INNER)
        acc = [lay(CONV_OUT, at=NXC * T + NTOK * INNER + INNER), lay(CONV_OUT, of=y_flat, at=HS * P)]
        assert NXC * T + NTOK * INNER + INNER + CONV_OUT <= gla_end
        xdt_tail = lay(INNER, of=state_g.rearrange("p a b c -> p (a b c)"), at=0)
        bn = lay(NTOK, GROUPS * DSTATE, of=state_g.rearrange("p a b c -> p (a b c)"), at=INNER)
        c_exp = lay(HS, P, of=y_flat, at=0)
        gm = lay(GROUPS, P, of=h_flat, at=2 * INNER)
        xpad_flat = xpad.rearrange("p a b -> p (a b)")
        att = lay(HS, P, of=xpad_flat, at=0)
        steps = lay(HS, P, of=xpad_flat, at=HS * P)
        b_masked = lay(NSEQ, GROUPS * DSTATE, of=xpad_flat, at=HS * P)

        def odd(name, *shape):
            at, width = ODD_CONSTS[name]
            v = odd_c[:, at:at + width]
            return v.rearrange("p (a b) -> p a b", b=shape[-1]) if shape else v

        def sized(v, t):
            if t < 2:
                return v
            return v.rearrange("p a t -> p (a t)")[:, 0:HS * NS].rearrange("p (a t) -> p a t", t=NS)

        def steps_of(t):
            return sized(steps, t)

        def att_of(t):
            return sized(att, t)

        c_exp_s = sized(c_exp, 2)
        ysq = xdt.rearrange("p a b -> p (a b)")[:, 0:NXS * T].rearrange("p (a t) -> p a t", t=T)
        DECAYS = (0, 4, 12)

        w_small, levels, conv_w = odd("w_small", 2 * GATE_RANK), odd("levels", P), odd("conv_w", NXC)

        landed = [sem(f"landed{r}") for r in range(RING)]
        half_landed = [sem(f"half_landed{r}") for r in range(RING)]
        w_done = sem("w_done")
        s_load = sem("s_load")
        s_const = sem("s_const")
        sc_clear = sem("sc_clear")
        sc_ready = sem("sc_ready")
        raw_copied = sem("raw_copied")
        ada_turned = sem("ada_turned")
        prep_done = sem("prep_done")
        mod_prompt = sem("mod_prompt")
        mod_sample = sem("mod_sample")
        unit_first = sem("unit_first")
        w_hi_done = sem("w_hi_done")
        w_lo_done = sem("w_lo_done")
        h_hi_done = sem("h_hi_done")
        h_lo_done = sem("h_lo_done")
        hid_hi_done = sem("hid_hi_done")
        hid_lo_done = sem("hid_lo_done")
        silu_done = sem("silu_done")
        hid_done = sem("hid_done")
        gated_done = sem("gated_done")
        y_done = sem("y_done")
        sq_done = sem("sq_done")
        sums_clear = sem("sums_clear")
        sumy_done = sem("sumy_done")
        sumq_done = sem("sumq_done")
        stats_ready = sem("stats_ready")
        mean2_done = sem("mean2_done")
        var_done = sem("var_done")
        rstd_done = sem("rstd_done")
        xhat_done = sem("xhat_done")
        xnew_done = sem("xnew_done")
        out_tile = sem("out_tile")
        named = {}

        def ev(name):
            if name not in named:
                named[name] = sem(name)
            return named[name]

        def rows64(h):
            return slice(64 * (h % 2), 64 * (h % 2) + 64)

        dve_chain = sem("dve_chain")
        act_chain = sem("act_chain")
        s_out = sem("s_out")

        def samples(ap):
            if len(ap.shape) == 3:
                return ap[:, :, TP:T].rearrange("p k (b t) -> p k b t", t=TS)
            return ap[:, TP:T].rearrange("p (b t) -> p b t", t=TS)

        def spread(ap, n):
            return ap.unsqueeze(len(ap.shape)).to_broadcast([*ap.shape, n])

        def slots(eng, count, body, straight=False):
            rest = count if straight else count % RING
            for s in range(rest):
                body(s, 0)
            if rest < count:
                with eng.Fori(0, (count - rest) // RING) as i:
                    for s in range(rest, rest + RING):
                        body(s, i)

        def wait_landed(pe, n, i=0):
            past = len([m for m in range(PAST0, min(n + 1, PAST0 + NSEQ)) if m % RING == n % RING])
            pe.wait_ge(landed[n % RING], 16 * (n // RING + 1 + past * (NPAGES // 2 - 1)) + i * 16)

        def unit_of(n, j, up):
            if up:
                return ring[:, n % RING, :].rearrange("p (g k n) -> p g k n", g=2, n=2 * P)[:, :, :, j * P:(j + 1) * P]
            return ring[:, n % RING, j * (KF // 2) * P:(j + 1) * (KF // 2) * P]

        def split_of(w, j, up):
            if up:
                return w[:, j, :].rearrange("p (g k n) -> p g k n", g=2, n=P)
            return w[:, j, 0:(KF // 2) * P]

        def units_before(i, up, s, j):
            return 2 * (N_FFN * ffn_index(i) + (0 if up else N_UP) + s) + j

        def past_of(b):
            return ring[:, (PAST0 + b) % RING, 0:NPAGES * 3 * PAGE].rearrange("p (j n) -> p j n", n=3 * PAGE)

        def ssm_of(b):
            at = b % PER_STATE * INNER
            return ring[:, (STATE0 + b // PER_STATE) % RING, at:at + INNER]

        def load_past(eng, first, signal):
            for b in range(NSEQ):
                n = PAST0 + b
                eng.wait_ge(w_done, n - RING + 1)
                with eng.Fori(first, first + NPAGES // 2) as j:
                    page = eng.value_load(pages[0:1, bass.ds(j + b * NPAGES, 1)],
                                          min_val=0, max_val=d["cache"].shape[0] - 1)
                    eng.dma_start(past_of(b)[:, bass.ds(j, 1), :].rearrange("p a n -> p (a n)"),
                                  d["cache"][bass.ds(page, 1)].rearrange("a p n -> (a p) n"))\
                       .then_inc(signal[n % RING], 16)

        block = ctx.enter_context(nc.Block())

        @block.sync
        def _(sp):
            sp.dma_start(params[:], d["params"]).then_inc(s_load, 16)
            sp.dma_start(add_turn[:], d["add_turn"]).then_inc(s_load, 16)

            def load(n, src, at, i=0):
                if n >= RING:
                    sp.wait_ge(w_done, n - RING + 1 + i * RING)
                sp.dma_start(ring[:, n % RING, 0:src.shape[2]], src[bass.ds(at + i * RING, 1)]
                             .rearrange("a p n -> (a p) n")).then_inc(landed[n % RING], 16)

            def load_ada(i, parts):
                for s in parts:
                    if i < NBLK:
                        load(ADA[i][s], d["w_ada"], N_ADA * i + s)

            def stream(n0, src, first, parts):
                for s in parts:
                    load(n0 + s, src, first + s)

            for i in range(NBLK):
                if i == 0:
                    load_ada(0, range(N_ADA))
                    sp.dma_start(x[:], d["xT"]).then_inc(s_load, 16)
                if i == MIXERS[0]:
                    stream(BODY0[i], d["w_in_even"], 0, range(N_IN[i]))
                    sp.wait_ge(ev("pages_landed"), 16)
                    load_past(sp, 0, landed)
                    load_ada(i + 1, range(N_EARLY))
                    stream(OUT0[i], d["w_out_even"], 0, range(N_OUT[i]))
                if i == MIXERS[1]:
                    stream(BODY0[i], d["w_in_odd"], 0, range(N_IN[i]))
                    stream(STATE0, d["state_ssm"], 0, range(NSEQ // PER_STATE))
                    for s in range(N_EARLY):
                        if 1 <= s <= NSEQ // PER_STATE:
                            sp.wait_ge(ev("ssm_stored%d" % (s - 1)), 16 * PER_STATE)
                        load_ada(i + 1, (s,))
                    stream(OUT0[i], d["w_out_odd"], 0, range(N_OUT[i]))
                if i in MIXERS:
                    load_ada(i + 1, range(N_EARLY, N_ADA))
                    continue

                def load_up(s, it):
                    load(body_slot(i, True, s), d["w_up"], N_UP * ffn_index(i) + s, it)
                    if s < 2:
                        load_ada(i + 1, (s,))
                slots(sp, N_UP, load_up)

                def load_down(s, it):
                    load(body_slot(i, False, s), d["w_down"], N_DOWN * ffn_index(i) + s, it)
                    if s < 2:
                        load_ada(i + 1, (2 + s,))
                if i == 0:
                    sp.dma_start(ident[:], d["ident"]).then_inc(ev("even_landed"), 16)
                    sp.dma_start(sample_of[:], d["sample_of"]).then_inc(ev("even_landed"), 16)
                    sp.dma_start(pages[:], d["pages"]).then_inc(ev("pages_landed"), 16)
                slots(sp, N_DOWN, load_down)
                load_ada(i + 1, range(N_EARLY, N_ADA))
            sp.wait_ge(xnew_done, KD * NBLK)
            sp.dma_start(d["yT"], x[:]).then_inc(s_out, 16)
            sp.wait_ge(s_out, 16 * N_STORES)

        @block.tensor
        def _(pe):
            def turn(i, s):
                pe.wait_ge(raw_copied, N_ADA * i + s + 1)
                for m in range(4):
                    last = nc.tensor.matmul(ps[BANK_ADA][:, (4 * s + m) * NC:(4 * s + m) * NC + WIDE],
                                            ada_raw[:, s % 2, m * P:(m + 1) * P], add_turn[:],
                                            start=True, stop=True)
                last.then_inc(ada_turned, 1)

            def conditioning(i, parts):
                for s in parts:
                    if i == NBLK:
                        continue
                    n = ADA[i][s]
                    wait_landed(pe, n)
                    if N_ADA * i + s >= 2:
                        pe.wait_ge(raw_copied, N_ADA * i + s - 1)
                    w = ring[:, n % RING, :].rearrange("p (k n) -> p k n", n=512)
                    for k in range(KD):
                        j = k % 4
                        last = nc.tensor.matmul(ps[raw_bank(i, s)][32 * j:32 * j + 32, :], sc[:, k, :],
                                                w[:, k, :], start=(k < 4), stop=(k >= 4))
                    last.then_inc(w_done, 1)
                    if s:
                        turn(i, s - 1)
                    if s == N_ADA - 1:
                        turn(i, s)

            def ffn(i):
                n0, f0, d0 = BODY0[i], KF * ffn_index(i), KD * i

                def product(out, pairs, first, last):
                    for k, (w, v) in enumerate(pairs):
                        for part, (a, b) in enumerate(((0, 0), (1, 0), (0, 1))):
                            ins = nc.tensor.matmul(out, w[a], v[b], start=first and k + part == 0,
                                                   stop=last and k == len(pairs) - 1 and part == 2)
                    return ins

                def up(s, it):
                    for j in range(2):
                        pe.wait_ge(w_lo_done, units_before(i, True, s, j) + 1 + it * (2 * RING))
                        if f0 + 2 * s + j >= 2:
                            pe.wait_ge(hid_done, f0 + 2 * s + j - 1 + it * (2 * RING))
                        hi, lo = split_of(w_hi, j, True), split_of(w_lo, j, True)
                        for g in range(2):
                            for k in range(KD):
                                if s == j == g == 0:
                                    pe.wait_ge(h_lo_done, KD * ffn_index(i) + k + 1)
                                last = product(ps[2 * j + g][:, 0:T], [((hi[:, g, k, :], lo[:, g, k, :]),
                                                                        (h_hi[:, k, :], h_lo[:, k, :]))],
                                               k == 0, k == KD - 1)
                        last.then_inc(unit_first if j == 0 else w_done, 1)
                    if s < 2:
                        conditioning(i + 1, (s,))
                slots(pe, N_UP, up)

                def down(s, it):
                    if d0 + s >= RING:
                        pe.wait_ge(y_done, d0 + s - RING + 1 + it * RING)
                    for j in range(2):
                        pe.wait_ge(w_lo_done, units_before(i, False, s, j) + 1 + it * (2 * RING))
                        if s == 0:
                            pe.wait_ge(hid_lo_done, f0 + (j + 1) * (KF // 2))
                        hi, lo = (split_of(w, j, False).rearrange("p (f n) -> p f n", n=P) for w in (w_hi, w_lo))
                        last = product(ps[BANK_DOWN[s % RING]][:, 0:T],
                                       [((hi[:, f, :], lo[:, f, :]),
                                         (hidden_hi[:, j * (KF // 2) + f, :], hidden_lo[:, j * (KF // 2) + f, :]))
                                        for f in range(KF // 2)], j == 0, j == 1)
                        last.then_inc(unit_first if j == 0 else w_done, 1)
                    if s < 2:
                        conditioning(i + 1, (2 + s,))
                slots(pe, N_DOWN, down, straight=i == 0)

            def stats(i):
                if i == 0:
                    pe.wait_ge(s_const, 1)
                pe.wait_ge(sumy_done, KD * (i + 1))
                pe.wait_ge(sumq_done, KD * (i + 1))
                nc.tensor.matmul(ps[BANK_MEAN][:, 0:T], ones_d[:], ysum[:], start=True, stop=True)
                nc.tensor.matmul(ps[BANK_MSQ][:, 0:T], ones_d[:], sqsum[:], start=True, stop=True)\
                  .then_inc(stats_ready, 1)

            def project(i, slot, banks, groups, halfway=None):
                n = BODY0[i] + slot
                wait_landed(pe, n)
                w = ring[:, n % RING, :].rearrange("p (k n) -> p k n", n=512)
                for g, (bank, what) in enumerate(zip(banks, groups)):
                    if g == 2 and halfway:
                        halfway()
                    for k in range(KD):
                        if isinstance(what, slice):
                            size = what.stop - what.start
                            last = nc.tensor.matmul(ps[bank][0:size, 0:T], w[:, k, what], h[:, k, :],
                                                    start=(k == 0), stop=(k == KD - 1))
                        else:
                            t0, size = TOK[what]
                            last = nc.tensor.matmul(ps[bank][0:size, :], h[:, k, t0:t0 + size], w[:, k, :],
                                                    start=(k == 0), stop=(k == KD - 1))
                last.then_inc(w_done, 1)

            def out_project(i, tiles, depth, parts):
                for k in range(KD):
                    n = OUT0[i] + k // tiles
                    wait_landed(pe, n)
                    if k >= RING:
                        pe.wait_ge(y_done, KD * i + k - RING + 1)
                    w = ring[:, n % RING, 0:depth * tiles * P].rearrange("p (k n) -> p k n", n=tiles * P)
                    for f in range(depth):
                        last = nc.tensor.matmul(ps[BANK_DOWN[k % RING]][:, 0:T],
                                                w[:, f, (k % tiles) * P:(k % tiles + 1) * P], parts[:, f, :],
                                                start=(f == 0), stop=(f == depth - 1))
                    last.then_inc(w_done if k % tiles == tiles - 1 else out_tile, 1)

            def tiles_of(n):
                return [slice(m * P, (m + 1) * P) for m in range(n)]

            def group(out, pairs):
                for k, (lhs, rhs) in enumerate(pairs):
                    last = nc.tensor.matmul(out, lhs, rhs, start=(k == 0), stop=(k == len(pairs) - 1))
                return last

            def even_mixer(i):
                pe.wait_ge(mod_prompt, KD * (i + 1))
                pe.wait_ge(mod_sample, i + 1)
                project(i, 0, (1, 2, 4, 5), [*tiles_of(3), slice(3 * P, 3 * P + ROPE)])
                project(i, 1, (6, 7, 0, 3), tiles_of(4))
                pe.wait_ge(ev("even_in"), 1)
                project(i, 2, (1, 2, 4), range(NTOK))
                pe.wait_ge(ev("even_in"), 2)
                project(i, 3, (5, 6, 7, 0), tiles_of(4))
                pe.wait_ge(ev("latent_sq"), 1)
                pe.wait_ge(ev("even_in"), 3)
                group(ps[3][:, 0:T], [(ones_d[:], sq[:, 0, :]), (ones_d[:], sq[:, 1, :])])
                group(ps[1][:, 0:T], [(ones_d[:], sq[:, 2, :])]).then_inc(ev("latent_ms"), 1)
                pe.wait_ge(ev("even_landed"), 64)
                pe.wait_ge(ev("latents"), 1)
                pe.wait_ge(ev("even_in"), 4)
                for m, bank in enumerate((2, 4, 5, 6, 7, 0)):
                    last = group(ps[bank][:, 0:T], [(w_uq[:, k, m * P:(m + 1) * P], cq[:, k, :]) for k in range(2)])
                last.then_inc(ev("queries"), 1)
                for m in range(2):
                    group(ps[1 if m == 0 else 3][:, 0:T], [(even("swap_r"), rq[:, m, :])])
                pe.wait_ge(ev("queries_copied"), 1)
                for m in range(2):
                    last = group(ps[2 + 2 * m][:, 0:T], [(even("swap_r"), rk[:, m, :])])
                last.then_inc(ev("swapped_r"), 1)
                for m in range(2):
                    group(ps[5 + m][:, 0:T], [(even("swap_m"), qr[:, m, :])])
                for m, bank in enumerate((7, 0)):
                    last = group(ps[bank][:, 0:T], [(place[0:ROPE, m, :], kr[0:ROPE, :])])
                last.then_inc(ev("swapped_m"), 1)

                retention_like(rq, rk, "ret")

                pe.wait_ge(ev("ret_done"), 1)
                for t, (t0, size) in enumerate(TOK):
                    last = nc.tensor.transpose(ps[1][0:size, t * P:t * P + RANK], lat[:, t0:t0 + size], ident[:])
                last.then_inc(ev("lat_turned"), 1)
                for a in range(HM):
                    if a >= 4:
                        pe.wait_ge(ev("q_lat_copied"), a - 3)
                    group(ps[2 + a % 4][:, 0:T], [(w_uk[rows64(a), a // 2, :], qn[rows64(a), a // 2, :])])\
                        .then_inc(ev("q_lat_made"), 1)
                pe.wait_ge(ev("q_lat_copied"), HM)
                pe.wait_ge(ev("rotated_m"), 1)

                def prompt_scores(a):
                    if a >= 2:
                        pe.wait_ge(ev("prompt_masked"), a - 1)
                    bank = ps[2 + a % 2]
                    for tb in range(2):
                        keys = slice(0, P * (tb + 1))
                        q = slice(tb * P, (tb + 1) * P)
                        last = group(bank[:, tb * P:tb * P + P * (tb + 1)],
                                     [(q_lat[:, a, q], lat[:, keys]), (qr[:, a // 4, q], kr4[:, a % 4, keys])])
                    last.then_inc(ev("prompt_scores"), 1)

                def prompt_turn(a):
                    pe.wait_ge(ev("prompt_norm"), a + 1)
                    if a >= 2:
                        pe.wait_ge(ev("prompt_turned_copied"), a - 1)
                    for m in range(3):
                        last = nc.tensor.transpose(ps[4 + a % 2][:, m * P:(m + 1) * P],
                                                   prob[:, a % 2, m * P:(m + 1) * P], ident[:])
                    last.then_inc(ev("prompt_turned"), 1)

                def prompt_values(a):
                    pe.wait_ge(ev("prompt_turned_copied"), a + 1)
                    pe.wait_ge(ev("lat_copied"), 1)
                    if a >= 2:
                        pe.wait_ge(ev("prompt_o_copied"), a - 1)
                    bank = ps[6 + a % 2]
                    pt = [prob_t[:, a % 2, m * P:(m + 1) * P] for m in range(3)]
                    group(bank[:, 0:P], [(lat_n[:, 0, :], pt[0])])
                    group(bank[:, P:2 * P], [(lat_n[:, 0, :], pt[1]), (lat_n[:, 1, :], pt[2])])\
                        .then_inc(ev("prompt_o"), 1)

                prompt_scores(0)
                prompt_scores(1)
                for a in range(HM):
                    prompt_turn(a)
                    if a + 2 < HM:
                        prompt_scores(a + 2)
                    prompt_values(a)

                pe.wait_ge(ev("prompt_o_copied"), HM)
                pe.wait_ge(ev("sample_q"), 1)
                pe.wait_ge(ev("turned_clear"), 1)

                def sample_scores(b):
                    if b >= 2:
                        pe.wait_ge(ev("sample_exp"), b - 1)
                    wait_landed(pe, PAST0 + b)
                    pe.wait_ge(half_landed[(PAST0 + b) % RING], 16 * (NPAGES // 2) * (b // RING + 1))
                    u = b % 2
                    ql, qro, past = q_ls[:, b, :], q_rs[0:64, b, :], past_of(b)
                    for rotary in range(2):
                        for half in range(2):
                            pg = slice(4 * half, 4 * half + 4)
                            lhs, rhs = (qro, past[0:64, pg, 2 * PAGE:3 * PAGE]) if rotary else (ql, past[:, pg, 0:PAGE])
                            nc.tensor.matmul(ps[2 + u][rows64(half), :], lhs, rhs, start=rotary == 0, stop=rotary == 1)
                    group(ps[1 + 6 * u][0:NS, 0:NS], [(ql, lat[:, TP:T]), (qro, kr4[0:64, 0, TP:T])])\
                        .then_inc(ev("sample_scores"), 1)

                for b in range(2):
                    sample_scores(b)
                for b in range(NSEQ):
                    pe.wait_ge(ev("sample_inverse"), b + 1)
                    u = b % 2
                    for j in range(NPAGES // 2):
                        nc.tensor.matmul(ps[6][:, j * P:(j + 1) * P], prob_s[:, u, j * P:(j + 1) * P], inverse[:, u, :],
                                         start=True, stop=True)
                    if b:
                        pe.wait_ge(ev("sample_o_copied"), b)
                    nc.tensor.matmul(ps[0][0:NS, P:2 * P], prob_s[0:NS, u, PAST // 2:], inverse[0:NS, u, :],
                                     start=True, stop=True).then_inc(ev("sample_turned"), 1)
                    pe.wait_ge(ev("sample_turned_copied"), b + 1)
                    past, flat = past_of(b), prob_st[:].rearrange("p j n -> p (j n)")
                    group(ps[0][:, 0:P], [(past[:, j // 2 + NPAGES // 2 * (j % 2), PAGE:2 * PAGE], flat[:, j * NS:j * NS + P])
                                          for j in range(NPAGES)]
                          + [(lat_n[0:NS, 2, :], flat[0:NS, NPAGES * NS:NPAGES * NS + P])]).then_inc(w_done, 1)
                    if b + 2 < NSEQ:
                        sample_scores(b + 2)
                pe.wait_ge(ev("sample_o_copied"), NSEQ)
                for a in range(HM):
                    last = group(ps[1 + a // 2][rows64(a), 0:T], [(w_uv[:, a * VM:(a + 1) * VM], o_lat[:, a, :])])
                last.then_inc(ev("values"), 1)
                pe.wait_ge(ev("values_copied"), 1)
                conditioning(i + 1, range(N_EARLY))
                out_project(i, KD // N_OUT[i], KD, mix)

            def retention_like(q, k, name):
                pe.wait_ge(ev("rotated_r"), 1)
                for t, (t0, size) in enumerate(TOK):
                    for m in range(2):
                        last = nc.tensor.transpose(ps[1 + t][0:size, m * P:(m + 1) * P], k[:, m, t0:t0 + size], ident[:])
                last.then_inc(ev("ret_k_turned"), 1)
                pe.wait_ge(ev("rotated_m"), 1)

                def head_scores(a):
                    if a >= 2:
                        pe.wait_ge(ev("ret_decayed"), a - 1)
                    r, m, bank = rows64(a), a // 2, ps[4 + a % 2]
                    group(bank[:, 0:TP], [(k[r, m, 0:P], q[r, m, 0:TP])])
                    group(bank[:, TP:TP + P], [(k[r, m, P:TP], q[r, m, P:TP])])
                    group(bank[0:NS, 3 * P:3 * P + NS], [(k[r, m, TP:T], q[r, m, TP:T])]).then_inc(ev("ret_scores"), 1)

                def head_values(a):
                    pe.wait_ge(ev("ret_decayed"), a + 1)
                    if a >= 2:
                        pe.wait_ge(ev("ret_o_copied"), a - 1)
                    r, m, bank = rows64(a), a // 2, ps[6 + a % 2]
                    s, v = scores[:, a % 2, :], slice(a * DVR, (a + 1) * DVR)
                    nc.tensor.matmul(bank[:, 0:TP], vn[:, 0, v], s[:, 0:TP], start=True, stop=False)
                    nc.tensor.matmul(bank[:, P:TP], vn[:, 1, v], s[:, TP:TP + P], start=False, stop=True)
                    nc.tensor.matmul(bank[:, TP:T], vn[0:NS, 2, v], s[0:NS, 3 * P:3 * P + NS], start=True, stop=True)
                    for b in range(NSEQ):
                        last = nc.tensor.matmul(bank[:, TP + b * TS:TP + (b + 1) * TS], state_r[:, b, m, :],
                                                q_lead[:, a, b * TS:(b + 1) * TS], start=False, stop=True,
                                                skip_group_check=True)
                    last.then_inc(ev("ret_o"), 1)

                pe.wait_ge(ev("ret_k_tail"), 1)
                head_scores(0)
                for a in range(HR):
                    if a + 1 < HR:
                        head_scores(a + 1)
                    head_values(a)
                for a in range(HR):
                    v = slice(a * DVR, (a + 1) * DVR)
                    last = group(ps[0][rows64(a), (a // 2) * DVR:(a // 2 + 1) * DVR],
                                 [(ktail[:, t, a * DKR:(a + 1) * DKR], vn[:, t, v]) for t in range(2)])
                last.then_inc(ev("ret_state"), 1)
                pe.wait_ge(ev("ret_decayed"), HR)
                pe.wait_ge(ev("ret_o_copied"), HR)
                for a in range(HR):
                    last = group(ps[1 + a][:, 0:T], [(ones_d[:], ro_sq[a])])
                last.then_inc(ev("ret_ms"), 1)
                sample_states("ret", ktail, vmask)

            def sample_states(name, kt, masked):
                for a in range(HR):
                    pe.wait_ge(ev(f"{name}_v_masked"), a + 1)
                    if a:
                        pe.wait_ge(ev(f"{name}_state_new"), a)
                    for half in range(2):
                        last = group(ps[5 + half][rows64(a), :],
                                     [(kt[0:NS, 2, a * DKR:(a + 1) * DKR], masked[0:NS, 4 * half:4 * half + 4, :])])
                    last.then_inc(ev(f"{name}_state_add"), 1)

            def odd_mixer(i):
                pe.wait_ge(mod_prompt, KD * (i + 1))
                pe.wait_ge(mod_sample, i + 1)
                project(i, 0, BANKS_IN, tiles_of(4))
                project(i, 1, (6, 7, 0), range(NTOK))
                pe.wait_ge(ev("odd_in"), 1)
                project(i, 2, (3, 1, 2, 4), tiles_of(4))
                pe.wait_ge(ev("odd_landed"), 48)
                group(ps[5][0:GATE_RANK, 0:T], [(w_small[:, k, 0:GATE_RANK], h[:, k, :]) for k in range(KD)])
                pe.wait_ge(ev("odd_in"), 2)
                for t, (t0, size) in enumerate(TOK):
                    last = group(ps[6][0:size, t * HS:(t + 1) * HS],
                                 [(h[:, k, t0:t0 + size], w_small[:, k, GATE_RANK:]) for k in range(KD)])
                last.then_inc(ev("small_made"), 1)
                pe.wait_ge(ev("small_copied"), 1)
                for m, bank in enumerate((7, 0)):
                    last = group(ps[bank][:, 0:T], [(odd("w_gate")[0:GATE_RANK, m * P:(m + 1) * P], glr[0:GATE_RANK, :])])
                last.then_inc(ev("gate_made"), 1)
                pe.wait_ge(ev("odd_in"), 3)

                def level(n):
                    pe.wait_ge(ev("level_qk"), n + 1)
                    if n:
                        pe.wait_ge(ev("level_picked"), n)
                    q, k = (qe, ke) if HALVES[n] else (gq, gk)
                    for a in range(HR):
                        r, m = rows64(a), a // 2
                        for c in range(2):
                            t = slice(c * P, (c + 1) * P)
                            last = group(ps[6 + a % 2][:, (2 * m + c) * P:(2 * m + c + 1) * P], [(k[r, m, t], q[r, m, t])])
                        if HALVES[n] < TS:
                            last = group(ps[3 * (a % 2)][0:NS, m * NS:(m + 1) * NS], [(k[r, m, TP:T], q[r, m, TP:T])])
                    last.then_inc(ev("level_made"), 1)

                for s in range(5):
                    if s:
                        pe.wait_ge(ev("odd_in"), 3 + s)
                    project(i, 3 + s, BANKS_IN, tiles_of(4), (lambda: level(2 * s)) if s < 4 else None)
                    if s < 4:
                        level(2 * s + 1)

                pe.wait_ge(ev("gla_tail"), 1)
                pe.wait_ge(ev("odd_in"), 8)
                for t, (t0, size) in enumerate(TOK):
                    for m in range(2):
                        last = nc.tensor.transpose(ps[(1, 2, 4)[t]][0:size, m * P:(m + 1) * P], ke[:, m, t0:t0 + size], ident[:])
                last.then_inc(ev("gla_k_turned"), 1)
                pe.wait_ge(ev("gla_k_copied"), 1)
                pe.wait_ge(ev("level_picked"), len(HALVES))
                for t in range(2):
                    for a in range(HR):
                        last = group(ps[3 * t][rows64(a), (a // 2) * DVR:(a // 2 + 1) * DVR],
                                     [(gktail[:, t, a * DKR:(a + 1) * DKR], gv[:, t, a * DVR:(a + 1) * DVR])])
                last.then_inc(ev("gla_state"), 1)
                pe.wait_ge(ev("gla_state1"), 1)
                for a in range(HR):
                    if a >= 2:
                        pe.wait_ge(ev("gla_o_copied"), a - 1)
                    m, bank, v = a // 2, ps[6 + a % 2], slice(a * DVR, (a + 1) * DVR)
                    group(bank[:, 0:P], [(gv[:, 0, v], s_pair[:, a % 2, 2 * m, :])])
                    group(bank[:, P:TP], [(gv[:, 1, v], s_pair[:, a % 2, 2 * m + 1, :]), (st1[:, m, :], q_exp[:, a, 0:P])])
                    group(bank[:, TP:T], [(gv[0:NS, 2, v], s_samp[0:NS, a % 2, m, :])])
                    for b in range(NSEQ):
                        last = nc.tensor.matmul(bank[:, TP + b * TS:TP + (b + 1) * TS], state_g[:, b, m, :],
                                                q_exp[:, a, P + b * TS:P + (b + 1) * TS], start=False, stop=True,
                                                skip_group_check=True)
                    last.then_inc(ev("gla_o"), 1)
                pe.wait_ge(ev("gla_o_copied"), HR)
                for a in range(HR):
                    last = group(ps[(1, 2, 4, 7)[a]][:, 0:T], [(ones_d[:], ro_sq[a])])
                last.then_inc(ev("gla_ms"), 1)
                sample_states("gla", gktail, gvmask)

                pe.wait_ge(ev("gla_done"), 1)
                for t, (t0, size) in enumerate(TOK):
                    if t:
                        pe.wait_ge(ev("xs_copied"), t)
                    for f in range(NXS + GROUPS):
                        if t == 0:
                            pe.wait_ge(ev("conv_done"), f + 1)
                        last = nc.tensor.transpose(ps[(1, 2, 4)[f // 4]][0:size, (f % 4) * P:(f % 4 + 1) * P],
                                                   xc[:, f, t0:t0 + size], ident[:])
                    last.then_inc(ev("xs_turned"), 1)
                pe.wait_ge(ev("xs_copied"), NTOK)
                pe.wait_ge(ev("conv_done"), NXC)
                for t, (t0, size) in enumerate(TOK):
                    heads = 512 // size
                    after = odd("after")[0:size, 0:size]
                    pe.wait_ge(ev("steps"), t + 1)
                    for q in range(HS // heads):
                        if q >= 2:
                            pe.wait_ge(ev("decay_copied"), DECAYS[t] + q - 1)
                        group(ps[5 + q % 2][0:size, :], [(after, steps_of(t)[0:size, q * heads:(q + 1) * heads, :])])\
                            .then_inc(ev("decay_made"), 1)
                    if t:
                        for q in range(HS // heads):
                            n = HS // heads + q
                            pe.wait_ge(ev("decay_copied"), DECAYS[t] + n - 1)
                            group(ps[5 + n % 2][:, :], [(ones_d[0:size, :], steps_of(t)[0:size, q * heads:(q + 1) * heads, :])])\
                                .then_inc(ev("decay_made"), 1)
                    for g in range(GROUPS):
                        group(ps[7][0:size, g * size:(g + 1) * size],
                              [(xc[:, NXS + g, t0:t0 + size], xc[:, NXS + GROUPS + g, t0:t0 + size])])
                    group(ps[0][0:size, 0:HS], [(after if t < 2 else odd("after_s")[0:NS, :], ua[0:size, t, :])])
                    group(ps[0][:, HS:2 * HS], [(ones_d[0:size, :], ua[0:size, t, :])]).then_inc(ev("bc_made"), 1)
                    pe.wait_ge(ev("att_ready"), t + 1)
                    if t:
                        pe.wait_ge(ev("y_kept"), t)
                    for a in range(HS):
                        out = ps[1 + a // 8][rows64(a), (a // 2 % 4) * size:(a // 2 % 4 + 1) * size]
                        pairs = [(xdt[0:size, t, a * HDIM:(a + 1) * HDIM], att_of(t)[0:size, a, :])]
                        if t == 1:
                            pairs.append((ssm1[:, a * HDIM:(a + 1) * HDIM], c_exp[:, a, :]))
                        last = group(out, pairs)
                    last.then_inc(ev("ssd_y"), 1)
                    if t < 2:
                        pe.wait_ge(ev("tail_ready"), t + 1)
                        if t:
                            pe.wait_ge(ev("ssm1_kept"), 1)
                        for g in range(GROUPS):
                            last = group(ps[3 + g][:, :], [(bn[:, t, g * DSTATE:(g + 1) * DSTATE],
                                                            xdt_tail[:, g * 512:(g + 1) * 512])])
                        last.then_inc(ev("ssm_add"), 1)
                pe.wait_ge(ev("tail_ready"), NTOK)
                pe.wait_ge(ev("ssm1_kept"), 2)
                pe.wait_ge(ev("b_masked"), 1)
                for b in range(NSEQ):
                    wait_landed(pe, STATE0 + b // PER_STATE)
                    for a in range(HS):
                        t8 = slice(b * TS, (b + 1) * TS)
                        last = group(ps[7][rows64(a), (a // 2) * NS + b * TS:(a // 2) * NS + (b + 1) * TS],
                                     [(ssm_of(b)[:, a * HDIM:(a + 1) * HDIM], c_exp_s[:, a, t8])])
                    if b % PER_STATE == PER_STATE - 1:
                        last.then_inc(w_done, 1)
                    if b >= 2:
                        pe.wait_ge(ev("ssm_new"), b - 1)
                    for g in range(GROUPS):
                        last = group(ps[3 + 2 * (b % 2) + g][:, :], [(b_masked[0:NS, b, g * DSTATE:(g + 1) * DSTATE],
                                                        xdt_tail[0:NS, g * 512:(g + 1) * 512])])
                    last.then_inc(ev("ssm_add_s"), 1)
                pe.wait_ge(ev("gated_sq"), 1)
                for g in range(GROUPS):
                    last = group(ps[1 + g][:, 0:T], [(ones_d[:], ysq[:, 4 * g + f, :]) for f in range(4)])
                last.then_inc(ev("ssd_ms"), 1)
                pe.wait_ge(ev("mix3_ready"), 1)
                conditioning(i + 1, range(N_EARLY))
                out_project(i, KD // N_OUT[i], NXC, mix3)

            pe.wait_ge(sc_ready, 1)
            pe.wait_ge(s_load, 32)
            conditioning(0, range(N_ADA))
            for i in range(NBLK):
                if i == MIXERS[0]:
                    even_mixer(i)
                elif i == MIXERS[1]:
                    odd_mixer(i)
                else:
                    ffn(i)
                stats(i)
                conditioning(i + 1, range(N_EARLY, N_ADA))

        @block.scalar
        def _(act):
            links = [0]

            def chain(ins):
                links[0] += 1
                ins.then_inc(act_chain, 1)
                act.wait_ge(act_chain, links[0])

            def copy_raw(i, s):
                if i == NBLK:
                    return
                act.wait_ge(w_done, ADA[i][s] + 1)
                if N_ADA * i + s >= 2:
                    act.wait_ge(ada_turned, N_ADA * i + s - 1)
                nc.scalar.activation(ada_raw[:, s % 2, :], ps[raw_bank(i, s)][:], ACT.Copy).then_inc(raw_copied, 1)

            def modulate(i):
                src = y if i else x
                act.wait_ge(prep_done, i + 1)
                if i == 0:
                    act.wait_ge(s_load, 48)
                for k in range(KD):
                    nc.scalar.activation(h[:, k, 0:TP], src[:, k, 0:TP], ACT.Identity, bias=modB[:, k, 0:1],
                                         scale=modA[:, k, 0:1]).then_inc(mod_prompt, 1)
                    if i not in MIXERS:
                        nc.scalar.activation(h_hi[:, k, 0:TP], src[:, k, 0:TP], ACT.Identity, bias=modB[:, k, 0:1],
                                             scale=modA[:, k, 0:1]).then_inc(h_hi_done, 1)

            def round_unit(i, up, s, j, it=0):
                n = body_slot(i, up, s)
                before = units_before(i, up, s, j)
                wait_landed(act, n, it)
                if before >= 2:
                    if j == 0:
                        act.wait_ge(unit_first, before // 2 + it * RING)
                    else:
                        act.wait_ge(w_done, done_before(i, up, s) + it * RING)
                nc.scalar.activation(split_of(w_hi, j, up), unit_of(n, j, up), ACT.Copy).then_inc(w_hi_done, 1)

            def square(i, s, it):
                act.wait_ge(y_done, KD * i + s + 1 + it * RING)
                if KD * i + s >= RING:
                    act.wait_ge(sumq_done, KD * i + s - RING + 1 + it * RING)
                nc.scalar.activation(sq[:, s % RING, :], y[:, bass.ds(s + it * RING, 1), :]
                                     .rearrange("p a t -> p (a t)"), ACT.Square).then_inc(sq_done, 1)

            def ffn(i):
                n0, f0 = BODY0[i], KF * ffn_index(i)

                def silu(up, s, j, it):
                    s0 = (s if up else N_UP) - 1
                    if j == 0:
                        act.wait_ge(unit_first, N_FFN * ffn_index(i) + s0 + 1 + it * RING)
                    else:
                        act.wait_ge(w_done, done_before(i, up, s) + it * RING)
                    if f0 + 2 * s0 + j >= 2:
                        act.wait_ge(hid_done, f0 + 2 * s0 + j - 1 + it * (2 * RING))
                    nc.scalar.activation(silu_g[:, j, :], ps[2 * j][:, 0:T], ACT.Silu).then_inc(silu_done, 1)

                def round_hidden(s, j, it):
                    act.wait_ge(hid_done, f0 + 2 * s + j + 1 + it * (2 * RING))
                    at = bass.ds(2 * s + j + it * (2 * RING), 1)
                    nc.scalar.activation(hidden_hi[:, at, :].rearrange("p a t -> p (a t)"),
                                         hidden[:, at, :].rearrange("p a t -> p (a t)"), ACT.Copy).then_inc(hid_hi_done, 1)

                def up(s, it):
                    for j in range(2):
                        if s:
                            silu(True, s, j, it)
                        if s or j:
                            round_unit(i, True, s, j, it)
                        if s:
                            round_hidden(s - 1, j, it)
                    if s == 1:
                        copy_raw(i + 1, 0)
                slots(act, N_UP, up)
                copy_raw(i + 1, 1)

                def down(s, it):
                    for j in range(2):
                        if s == 0:
                            silu(False, s, j, 0)
                        round_unit(i, False, s, j, it)
                        if s == 0:
                            round_hidden(N_UP - 1, j, 0)
                    if s:
                        square(i, s - 1, it)
                    if s == 1:
                        copy_raw(i + 1, 2)
                slots(act, N_DOWN, down, straight=i == 0)
                square(i, N_DOWN - 1, 0)
                copy_raw(i + 1, 3)
                if i + 1 == MIXERS[0]:
                    act.dma_start(even_c[:], d["even_consts"]).then_inc(ev("even_landed"), 16)
                    act.dma_start(state_r[:], d["state_r"]).then_inc(ev("even_landed"), 16)
                if i + 1 == MIXERS[1]:
                    act.dma_start(odd_c[:], d["odd_consts"]).then_inc(ev("odd_landed"), 16)
                    act.dma_start(state_g[:], d["state_g"]).then_inc(ev("odd_landed"), 16)
                    act.dma_start(hist[:], d["conv_hist"]).then_inc(ev("odd_landed"), 16)

            def norm(i):
                act.wait_ge(stats_ready, i + 1)
                nc.scalar.activation(mean2[:], ps[BANK_MEAN][:, 0:T], ACT.Square).then_inc(mean2_done, 1)
                copy_raw(i + 1, N_EARLY)
                act.wait_ge(var_done, i + 1)
                chain(nc.scalar.activation(rstd[:], var[:], ACT.Ln))
                nc.scalar.activation(rstd[:], rstd[:], ACT.Exp, scale=-0.5).then_inc(rstd_done, 1)
                copy_raw(i + 1, N_ADA - 1)

            def copy(out, bank, scale=1.0):
                return nc.scalar.activation(out, bank, ACT.Copy, scale=scale)

            def even_mixer(i):
                n = BODY0[i]
                act.wait_ge(w_done, n + 1)
                copy(cq[:, 0, :], ps[1][:, 0:T])
                copy(cq[:, 1, :], ps[2][:, 0:T])
                copy(ckv[:], ps[4][:, 0:T])
                copy(kr[0:ROPE, :], ps[5][0:ROPE, 0:T]).then_inc(ev("even_in"), 1)
                act.wait_ge(w_done, n + 2)
                copy(rq[:, 0, :], ps[6][:, 0:T])
                copy(rq[:, 1, :], ps[7][:, 0:T])
                copy(rk[:, 0, :], ps[0][:, 0:T], DKR ** -0.5)
                copy(rk[:, 1, :], ps[3][:, 0:T], DKR ** -0.5).then_inc(ev("even_in"), 1)
                act.wait_ge(w_done, n + 3)
                for t, (_, size) in enumerate(TOK):
                    last = copy(vn[0:size, t, :], ps[(1, 2, 4)[t]][0:size, :])
                last.then_inc(ev("even_in"), 1)
                act.wait_ge(w_done, n + 4)
                for m, bank in enumerate((5, 6, 7, 0)):
                    last = nc.scalar.activation(sgr[:, m, :], ps[bank][:, 0:T], ACT.Silu)
                last.then_inc(ev("even_in"), 1)
                act.wait_ge(ev("latent_ms"), 1)
                act.wait_ge(ev("rms_eps"), 1)
                nc.scalar.activation(var[:], ps[3][:, 0:T], ACT.Ln, bias=eps_rms[:], scale=D / QRANK)
                chain(nc.scalar.activation(rstd[:], ps[1][:, 0:T], ACT.Ln, bias=eps_rms[:], scale=D / RANK))
                nc.scalar.activation(var[:], var[:], ACT.Exp, scale=-0.5)
                nc.scalar.activation(rstd[:], rstd[:], ACT.Exp, scale=-0.5).then_inc(ev("latent_r"), 1)
                act.wait_ge(ev("queries"), 1)
                for m, bank in enumerate((2, 4, 5, 6)):
                    copy(qn[:, m, :], ps[bank][:, 0:T])
                copy(qr[:, 0, :], ps[7][:, 0:T])
                copy(qr[:, 1, :], ps[0][:, 0:T]).then_inc(ev("queries_copied"), 1)

                for a in range(HR):
                    act.wait_ge(ev("ret_o"), a + 1)
                    copy(ro[:, a, :], ps[6 + a % 2][:, 0:T])
                    nc.scalar.activation(ro_sq[a], ps[6 + a % 2][:, 0:T], ACT.Square).then_inc(ev("ret_o_copied"), 1)
                act.wait_ge(ev("ret_ms"), 1)
                for a in range(HR):
                    last = nc.scalar.activation(ro_r[a], ps[1 + a][:, 0:T], ACT.Ln, bias=eps_rms[:], scale=D / DVR)
                chain(last)
                for a in range(HR):
                    last = nc.scalar.activation(ro_r[a], ro_r[a], ACT.Exp, scale=-0.5)
                last.then_inc(ev("ret_r"), 1)
                act.wait_ge(ev("ret_state_out"), 1)
                act.dma_start(d["out_ret_p"], state_p[:]).then_inc(ev("ret_p_stored"), 16)

                act.wait_ge(ev("lat_turned"), 1)
                copy(lat_n[:, 0:2, :], ps[1][:, 0:2 * P].rearrange("p (a n) -> p a n", n=P))
                copy(lat_n[0:NS, 2, :], ps[1][0:NS, 2 * P:3 * P]).then_inc(ev("lat_copied"), 1)
                for a in range(HM):
                    act.wait_ge(ev("q_lat_made"), a + 1)
                    copy(q_lat[:, a, :], ps[2 + a % 4][:, 0:T]).then_inc(ev("q_lat_copied"), 1)

                def prompt_exp(a):
                    act.wait_ge(ev("prompt_max"), a + 1)
                    pr, u = prob[:, a % 2, :], a % 2
                    nc.scalar.activation(pr[:, 0:P], pr[:, 0:P], ACT.Exp, bias=stat[:, u, 0:1],
                                         accum_out=stat[:, 2 + u, 0:1])
                    nc.scalar.activation(pr[:, P:3 * P], pr[:, P:3 * P], ACT.Exp, bias=stat[:, u, 1:2],
                                         accum_out=stat[:, 2 + u, 1:2]).then_inc(ev("prompt_exp"), 1)

                prompt_exp(0)
                prompt_exp(1)
                act.wait_ge(ev("ret_p_stored"), 16)
                for a in range(HM):
                    act.wait_ge(ev("prompt_turned"), a + 1)
                    copy(prob_t[:, a % 2, :], ps[4 + a % 2][:, 0:3 * P]).then_inc(ev("prompt_turned_copied"), 1)
                    if 1 <= a < HM - 1:
                        prompt_exp(a + 1)
                    act.wait_ge(ev("prompt_o"), a + 1)
                    copy(o_lat[:, a, 0:TP], ps[6 + a % 2][:, 0:TP]).then_inc(ev("prompt_o_copied"), 1)

                def sample_exp(b):
                    act.wait_ge(ev("sample_max"), b + 1)
                    u = b % 2
                    nc.scalar.activation(prob_s[:, u, 0:PAST // 2], ps[2 + u][:], ACT.Exp, bias=stat_s[:, u, 4:5],
                                         scale=ATT_SCALE, accum_out=stat_s[:, u, 5:6])
                    new = prob_s[0:NS, u, PAST // 2:]
                    nc.scalar.activation(new, new, ACT.Exp, bias=stat_s[0:NS, u, 4:5], scale=ATT_SCALE,
                                         accum_out=stat_s[0:NS, u, 7:8]).then_inc(ev("sample_exp"), 1)

                sample_exp(0)
                sample_exp(1)
                for b in range(NSEQ):
                    act.wait_ge(ev("turned_clear"), 1)
                    act.wait_ge(ev("sample_turned"), b + 1)
                    copy(prob_st[:, 0:NPAGES, :], ps[6][:].rearrange("p (a n) -> p a n", n=NS))
                    copy(prob_st[0:NS, NPAGES, :], ps[0][0:NS, P:P + NS]).then_inc(ev("sample_turned_copied"), 1)
                    if 1 <= b < NSEQ - 1:
                        sample_exp(b + 1)
                    act.wait_ge(w_done, PAST0 + b + 1)
                    t0 = TP + b * TS
                    copy(o_lat[:, :, t0:t0 + TS], ps[0][:, 0:NS].rearrange("p (a t) -> p a t", t=TS))\
                        .then_inc(ev("sample_o_copied"), 1)

                act.wait_ge(ev("values"), 1)
                for m in range(4):
                    last = copy(mix[:, m, :], ps[1 + m][:, 0:T])
                last.then_inc(ev("values_copied"), 1)
                for s in range(N_EARLY):
                    copy_raw(i + 1, s)
                act.dma_start(d["out_lat"], lat[:]).then_inc(ev("even_stored"), 16)
                act.wait_ge(ev("rotated_m"), 1)
                act.dma_start(d["out_krope"], kr_rot[0:ROPE, :]).then_inc(ev("even_stored"), 16)
                act.wait_ge(ev("ret_state_new"), HR)
                act.dma_start(d["out_ret_s"], state_r[:]).then_inc(ev("even_stored"), 16)
                for k in range(KD):
                    square(i, k, 0)

            def odd_mixer(i):
                n = BODY0[i]

                def arrived(slot):
                    act.wait_ge(w_done, n + slot + 1)

                arrived(0)
                for m in range(2):
                    copy(gq[:, m, :], ps[BANKS_IN[m]][:, 0:T], DKR ** -0.5)
                for m in range(2):
                    last = copy(gk[:, m, :], ps[BANKS_IN[2 + m]][:, 0:T])
                last.then_inc(ev("odd_in"), 1)
                arrived(1)
                for t, (_, size) in enumerate(TOK):
                    last = copy(gv[0:size, t, :], ps[(6, 7, 0)[t]][0:size, :])
                last.then_inc(ev("odd_in"), 1)
                arrived(2)
                for m, bank in enumerate((3, 1, 2, 4)):
                    last = nc.scalar.activation(gr[:, m, :], ps[bank][:, 0:T], ACT.Silu)
                last.then_inc(ev("odd_in"), 1)
                act.wait_ge(ev("small_made"), 1)
                act.wait_ge(ev("dt_clear"), 1)
                copy(dtx[:, 0:2, :], ps[6][:, 0:2 * HS].rearrange("p (a b) -> p a b", b=HS))
                copy(dtx[0:NS, 2, :], ps[6][0:NS, 2 * HS:3 * HS])
                copy(glr[0:GATE_RANK, :], ps[5][0:GATE_RANK, 0:T]).then_inc(ev("small_copied"), 1)
                act.wait_ge(ev("gate_made"), 1)
                act.wait_ge(xnew_done, KD * i)
                for m, bank in enumerate((7, 0)):
                    last = nc.scalar.activation(gla[:, m, :], ps[bank][:, 0:T], ACT.Identity,
                                                bias=odd("b_gate")[:, m:m + 1])
                chain(last)
                chain(nc.scalar.activation(ge[:], gla[:], ACT.Abs))
                chain(nc.scalar.activation(ge[:], ge[:], ACT.Exp, scale=-1.0))
                nc.scalar.activation(ge[:], ge[:], ACT.Ln, bias=1.0).then_inc(ev("gate_log"), 1)
                act.wait_ge(ev("dt_biased"), 1)
                nc.scalar.activation(e_a[:], odd("a_log"), ACT.Exp)
                chain(nc.scalar.activation(dtu[:], dtx[:], ACT.Abs))
                nc.scalar.activation(dtu[:], dtu[:], ACT.Exp, scale=-1.0).then_inc(ev("dt_exp"), 1)

                def level(k):
                    w = TP if HALVES[k] >= TS else T
                    act.wait_ge(ev("level_diff"), k + 1)
                    chain(nc.scalar.activation(ge[:, :, 0:w], ge[:, :, 0:w], ACT.Abs))
                    nc.scalar.activation(ge[:, :, 0:w], ge[:, :, 0:w], ACT.Exp, scale=-1.0 / TAU)\
                      .then_inc(ev("level_exp"), 1)

                for s in range(5):
                    for k in (2 * s, 2 * s + 1):
                        if k < len(HALVES) and HALVES[k]:
                            level(k)
                    arrived(3 + s)
                    for m in range(4):
                        bank = ps[BANKS_IN[m]]
                        if s < 2:
                            last = nc.scalar.activation(zs[:, 4 * s + m, :], bank[:, 0:T], ACT.Silu)
                        else:
                            f = 4 * (s - 2) + m
                            copy(xpad[:, f, CONV - 1:WP], bank[:, 0:TP])
                            last = copy(xpad[:, f, WP:].rearrange("p (b t) -> p b t", t=WS)[:, :, CONV - 1:],
                                        bank[:, TP:T].rearrange("p (b t) -> p b t", t=TS))
                    last.then_inc(ev("odd_in"), 1)
                act.wait_ge(ev("level_picked"), len(HALVES))
                chain(nc.scalar.activation(qe[:], seg[:], ACT.Exp, scale=1.0 / TAU))
                act.wait_ge(ev("tail_diff"), 1)
                nc.scalar.activation(ge[:], ge[:], ACT.Exp, scale=1.0 / TAU).then_inc(ev("gla_exps"), 1)
                act.wait_ge(ev("gla_k_turned"), 1)
                for t, (_, size) in enumerate(TOK):
                    last = copy(gktail[0:size, t, :], ps[(1, 2, 4)[t]][0:size, 0:HR * DKR])
                last.then_inc(ev("gla_k_copied"), 1)
                for a in range(HR):
                    act.wait_ge(ev("gla_o"), a + 1)
                    copy(go[:, a, :], ps[6 + a % 2][:, 0:T])
                    nc.scalar.activation(ro_sq[a], ps[6 + a % 2][:, 0:T], ACT.Square).then_inc(ev("gla_o_copied"), 1)
                act.wait_ge(ev("gla_ms"), 1)
                for a in range(HR):
                    last = nc.scalar.activation(ro_r[a], ps[(1, 2, 4, 7)[a]][:, 0:T], ACT.Ln, bias=eps_rms[:], scale=D / DVR)
                chain(last)
                for a in range(HR):
                    last = nc.scalar.activation(ro_r[a], ro_r[a], ACT.Exp, scale=-0.5)
                last.then_inc(ev("gla_r"), 1)
                act.wait_ge(ev("gla_state2"), 1)
                act.dma_start(d["out_gla_p"], st2[:]).then_inc(ev("gla_stored"), 16)
                act.wait_ge(ev("gla_state_new"), HR)
                act.dma_start(d["out_gla_s"], state_g[:]).then_inc(ev("gla_stored"), 16)
                act.wait_ge(ev("conv_state"), 1)
                act.dma_start(d["out_conv"], conv_state[:]).then_inc(s_out, 16)

                act.wait_ge(ev("gla_done"), 1)
                act.wait_ge(ev("gla_stored"), 32)

                def conv_first(f):
                    if f >= 2:
                        act.wait_ge(ev("conv_done"), f - 1)
                    nc.scalar.activation(acc[f % 2], xpad[:, f, 0:CONV_OUT], ACT.Identity,
                                         bias=odd("conv_b")[:, f:f + 1], scale=conv_w[:, 0, f:f + 1])\
                      .then_inc(ev("conv_first"), 1)
                conv_first(0)
                conv_first(1)
                for f in range(NXC):
                    act.wait_ge(ev("conv_added"), f + 1)
                    nc.scalar.activation(xc[:, f, 0:TP], acc[f % 2][:, 0:TP], ACT.Silu)
                    for_samples = acc[f % 2][:, WP:CONV_OUT]
                    head = for_samples[:, 0:(NSEQ - 1) * WS].rearrange("p (b t) -> p b t", t=WS)[:, :, 0:TS]
                    nc.scalar.activation(xc[:, f, TP:T - TS].rearrange("p (b t) -> p b t", t=TS), head, ACT.Silu)
                    nc.scalar.activation(xc[:, f, T - TS:T], for_samples[:, (NSEQ - 1) * WS:], ACT.Silu)\
                      .then_inc(ev("conv_done"), 1)
                    if f + 2 < NXC:
                        conv_first(f + 2)

                for t, (_, size) in enumerate(TOK):
                    act.wait_ge(ev("xs_turned"), t + 1)
                    copy(bn[0:size, t, :], ps[4][0:size, 0:GROUPS * DSTATE]).then_inc(ev("bn_copied"), 1)
                for t, (_, size) in enumerate(TOK):
                    heads = 512 // size
                    for q in range(HS // heads):
                        act.wait_ge(ev("decay_made"), DECAYS[t] + q + 1)
                        if t and q == 0:
                            act.wait_ge(ev("ssd_y"), t)
                        nc.scalar.activation(att_of(t)[0:size, q * heads:(q + 1) * heads, :],
                                             ps[5 + q % 2][0:size, :].rearrange("p (a n) -> p a n", n=size), ACT.Exp)\
                          .then_inc(ev("decay_copied"), 1)
                    if t:
                        for q in range(HS // heads):
                            k = HS // heads + q
                            act.wait_ge(ev("decay_made"), DECAYS[t] + k + 1)
                            nc.scalar.activation(sized(c_exp, t)[:, q * heads:(q + 1) * heads, :],
                                                 ps[5 + k % 2][:].rearrange("p (a n) -> p a n", n=size), ACT.Exp,
                                                 scale=float(D)).then_inc(ev("decay_copied"), 1)
                    act.wait_ge(ev("bc_made"), t + 1)
                    if t:
                        act.wait_ge(ev("tail_ready"), t)
                        act.wait_ge(ev("ssm1_kept"), t)
                    nc.scalar.activation(tails[0:size, :], ps[0][0:size, 0:HS], ACT.Exp)
                    nc.scalar.activation(dec_p[:], ps[0][:, HS:2 * HS], ACT.Exp, scale=float(D)).then_inc(ev("tails"), 1)
                act.wait_ge(ev("ssm1_kept"), 2)
                act.dma_start(d["out_ssm_p"], ssm1[:]).then_inc(s_out, 16)
                for b in range(NSEQ):
                    act.wait_ge(ev("ssm_new"), b + 1)
                    act.dma_start(d["out_ssm_s"][b], ssm_of(b)).then_inc(ev("ssm_stored%d" % (b // PER_STATE)), 16)
                act.wait_ge(ev("ssd_ms"), 1)
                for g in range(GROUPS):
                    last = nc.scalar.activation(ro_r[g], ps[1 + g][:, 0:T], ACT.Ln, bias=eps_rms[:], scale=float(D) / 512)
                chain(last)
                for g in range(GROUPS):
                    last = nc.scalar.activation(ro_r[g], ro_r[g], ACT.Exp, scale=-0.5)
                last.then_inc(ev("ssd_r"), 1)
                for s in range(N_EARLY):
                    copy_raw(i + 1, s)
                for s in range(NSEQ // PER_STATE):
                    act.wait_ge(ev("ssm_stored%d" % s), 16 * PER_STATE)
                for k in range(KD):
                    square(i, k, 0)

            act.wait_ge(s_load, 32)
            act.wait_ge(sc_clear, 1)
            nc.scalar.activation(sc[:, :, 0:NC], cT, ACT.Silu).then_inc(sc_ready, 1)
            for s in range(N_ADA):
                copy_raw(0, s)
            round_unit(0, True, 0, 0)
            modulate(0)
            for i in range(NBLK):
                if i == MIXERS[0]:
                    even_mixer(i)
                elif i == MIXERS[1]:
                    odd_mixer(i)
                else:
                    ffn(i)
                norm(i)
                if i in MIXERS:
                    if i == MIXERS[0]:
                        act.wait_ge(ev("even_stored"), 16 * 3)
                    else:
                        act.wait_ge(s_out, 16 * 2)
                if i + 1 < NBLK:
                    if i + 1 not in MIXERS:
                        round_unit(i + 1, True, 0, 0)
                    modulate(i + 1)

        @block.gpsimd
        def _(pool):
            nc.gpsimd.memset(sc[:], 0.0).then_inc(sc_clear, 1)
            nc.gpsimd.memset(ones_d[:], 1.0 / D).then_inc(s_const, 1)
            nc.gpsimd.memset(eps_rms[:], RMS_EPS).then_inc(ev("rms_eps"), 1)
            pool.wait_ge(ev("rms_eps"), 1)
            for i in range(NBLK):
                if i == MIXERS[0]:
                    pool.wait_ge(ev("even_in"), 3)
                    pool.wait_ge(w_done, BODY0[i] + N_IN[i])
                    pool.wait_ge(ev("even_landed"), 64)
                    for a in range(HR):
                        if a:
                            pool.wait_ge(ev("ret_state_add"), a)
                        v = vn[0:NS, 2, a * DVR:(a + 1) * DVR]
                        nc.gpsimd.tensor_tensor(vmask[0:NS], v.unsqueeze(1).to_broadcast([NS, NSEQ, DVR]),
                                                spread(sample_of[0:NS, :], DVR), ALU.mult)\
                          .then_inc(ev("ret_v_masked"), 1)
                    pool.wait_ge(ev("pages_landed"), 16)
                    load_past(pool, NPAGES // 2, half_landed)
                if i == MIXERS[1]:
                    pool.wait_ge(ev("odd_in"), 2)
                    pool.wait_ge(w_done, BODY0[i] + N_IN[i])
                    for a in range(HR):
                        if a:
                            pool.wait_ge(ev("gla_state_add"), a)
                        v = gv[0:NS, 2, a * DVR:(a + 1) * DVR]
                        nc.gpsimd.tensor_tensor(gvmask[0:NS], v.unsqueeze(1).to_broadcast([NS, NSEQ, DVR]),
                                                spread(sample_of[0:NS, :], DVR), ALU.mult)\
                          .then_inc(ev("gla_v_masked"), 1)
                if i:
                    pool.wait_ge(stats_ready, i)
                nc.gpsimd.memset(ysum[:], 0.0).then_inc(sums_clear, 1)
                nc.gpsimd.memset(sqsum[:], 0.0).then_inc(sums_clear, 1)
                pool.wait_ge(sums_clear, 2 * (i + 1))
                for k in range(KD):
                    pool.wait_ge(y_done, KD * i + k + 1)
                    if KD * i + k:
                        pool.wait_ge(sumy_done, KD * i + k)
                    nc.gpsimd.tensor_tensor(ysum[:], ysum[:], y[:, k, :], ALU.add).then_inc(sumy_done, 1)
                    pool.wait_ge(sq_done, KD * i + k + 1)
                    if KD * i + k:
                        pool.wait_ge(sumq_done, KD * i + k)
                    nc.gpsimd.tensor_tensor(sqsum[:], sqsum[:], sq[:, k % RING, :], ALU.add).then_inc(sumq_done, 1)
                for k in range(KD):
                    pool.wait_ge(xhat_done, KD * i + k + 1)
                    nc.gpsimd.tensor_scalar(x[:, k, :], y[:, k, :], ln_g[:, i, k:k + 1], ln_b[:, i, k:k + 1],
                                            ALU.mult, ALU.add).then_inc(xnew_done, 1)

        @block.vector
        def _(dve):
            links = [0]

            def link(ins):
                links[0] += 1
                ins.then_inc(dve_chain, 1)
                dve.wait_ge(dve_chain, links[0])

            def prepare(i):
                dve.wait_ge(ada_turned, N_ADA * (i + 1))
                a = ps[BANK_ADA][:, 0:24 * NC].rearrange("p (m c) -> p m c", c=NC)
                link(nc.vector.tensor_tensor(ada[:], a, spread(b_ada[:, i, :], NC), ALU.add))
                shift, scale, gt = ada[:, 0:KD, :], ada[:, KD:2 * KD, :], ada[:, 2 * KD:3 * KD, :]
                if i:
                    g, b = spread(ln_g[:, i - 1, :], NC), spread(ln_b[:, i - 1, :], NC)
                    link(nc.vector.tensor_scalar(scale, scale, 1.0, None, ALU.add))
                    nc.vector.tensor_tensor(modA[:], scale, g, ALU.mult)
                    link(nc.vector.tensor_tensor(modB[:], scale, b, ALU.mult))
                    link(nc.vector.tensor_tensor(modB[:], modB[:], shift, ALU.add))
                else:
                    nc.vector.tensor_scalar(modA[:], scale, 1.0, None, ALU.add)
                    link(nc.vector.tensor_copy(modB[:], shift))
                coef = (1.0 if i in MIXERS else 0.5) / ALPHA
                nc.vector.tensor_scalar(gate[:], gt, coef, None, ALU.mult).then_inc(prep_done, 1)
                dve.wait_ge(prep_done, i + 1)
                src = y if i else x
                if i == 0:
                    dve.wait_ge(s_load, 48)
                link(nc.vector.tensor_tensor(samples(h), samples(src), spread(modA[:, :, 1:NC], TS), ALU.mult))
                nc.vector.tensor_tensor(samples(h), samples(h), spread(modB[:, :, 1:NC], TS), ALU.add)\
                  .then_inc(mod_sample, 1)
                if i in MIXERS:
                    return
                dve.wait_ge(mod_sample, i + 1)
                link(nc.vector.tensor_copy(samples(h_hi), samples(h)))
                rest_of_unit(i, True, 0, 0)
                for k in range(KD):
                    dve.wait_ge(h_hi_done, KD * ffn_index(i) + k + 1)
                    nc.vector.tensor_tensor(h_lo[:, k, :], h[:, k, :], h_hi[:, k, :].bitcast(F32), ALU.subtract)\
                      .then_inc(h_lo_done, 1)

            def rest_of_unit(i, up, s, j, it=0):
                n = body_slot(i, up, s)
                dve.wait_ge(w_hi_done, units_before(i, up, s, j) + 1 + it * (2 * RING))
                nc.vector.tensor_tensor(split_of(w_lo, j, up), unit_of(n, j, up), split_of(w_hi, j, up).bitcast(F32),
                                        ALU.subtract).then_inc(w_lo_done, 1)

            def residual(i, s, it):
                f = ps[BANK_DOWN[s % RING]]
                at = bass.ds(s + it * RING, 1)
                g = gate[:, at, :].rearrange("p a c -> p (a c)")
                xt = x[:, at, :].rearrange("p a t -> p (a t)")
                yt = y[:, at, :].rearrange("p a t -> p (a t)")
                nc.vector.scalar_tensor_tensor(out=yt[:, 0:TP], in0=f[:, 0:TP], scalar=g[:, 0:1],
                                               in1=xt[:, 0:TP], op0=ALU.mult, op1=ALU.add)
                nc.vector.tensor_tensor(gated[:, s % RING], samples(f[:, 0:T]), spread(g[:, 1:NC], TS), ALU.mult)\
                  .then_inc(gated_done, 1)
                dve.wait_ge(gated_done, KD * i + s + 1 + it * RING)
                nc.vector.tensor_tensor(samples(yt), gated[:, s % RING], samples(xt), ALU.add).then_inc(y_done, 1)

            def ffn(i):
                n0, f0 = BODY0[i], KF * ffn_index(i)

                def multiply(s, j, it):
                    dve.wait_ge(silu_done, f0 + 2 * s + j + 1 + it * (2 * RING))
                    nc.vector.tensor_tensor(hidden[:, bass.ds(2 * s + j + it * (2 * RING), 1), :]
                                            .rearrange("p a t -> p (a t)"),
                                            silu_g[:, j, :], ps[2 * j + 1][:, 0:T], ALU.mult).then_inc(hid_done, 1)

                def rest_of_hidden(s, j, it):
                    dve.wait_ge(hid_hi_done, f0 + 2 * s + j + 1 + it * (2 * RING))
                    at = bass.ds(2 * s + j + it * (2 * RING), 1)
                    part = [v[:, at, :].rearrange("p a t -> p (a t)") for v in (hidden, hidden_hi, hidden_lo)]
                    nc.vector.tensor_tensor(part[2], part[0], part[1].bitcast(F32), ALU.subtract).then_inc(hid_lo_done, 1)

                def up(s, it):
                    for j in range(2):
                        if s:
                            multiply(s - 1, j, it)
                        if s or j:
                            rest_of_unit(i, True, s, j, it)
                        if s:
                            rest_of_hidden(s - 1, j, it)
                slots(dve, N_UP, up)

                def down(s, it):
                    for j in range(2):
                        if s == 0:
                            multiply(N_UP - 1, j, 0)
                        elif j:
                            dve.wait_ge(w_done, done_before(i, False, s) + it * RING)
                            residual(i, s - 1, it)
                        elif s == 1 and i:
                            dve.wait_ge(xnew_done, KD * i)
                        rest_of_unit(i, False, s, j, it)
                        if s == 0:
                            rest_of_hidden(N_UP - 1, j, 0)
                slots(dve, N_DOWN, down)
                dve.wait_ge(w_done, body_slot(i, False, N_DOWN - 1) + 1)
                residual(i, N_DOWN - 1, 0)

            def norm(i):
                mean, msq = ps[BANK_MEAN][:, 0:T], ps[BANK_MSQ][:, 0:T]
                dve.wait_ge(mean2_done, i + 1)
                nc.vector.scalar_tensor_tensor(out=var[:], in0=msq, scalar=LN_EPS, in1=mean2[:],
                                               op0=ALU.add, op1=ALU.subtract).then_inc(var_done, 1)
                link(nc.vector.tensor_tensor(y[:], y[:], mean.unsqueeze(1).to_broadcast([P, KD, T]), ALU.subtract))
                dve.wait_ge(rstd_done, i + 1)
                for k in range(KD):
                    nc.vector.tensor_tensor(y[:, k, :], y[:, k, :], rstd[:], ALU.mult).then_inc(xhat_done, 1)
                dve.wait_ge(xhat_done, KD * (i + 1))

            def rotate(z, banks, cos, sin, signal):
                link(nc.vector.tensor_tensor(z[:], z[:], cos.unsqueeze(1).to_broadcast([P, 2, T]), ALU.mult))
                for m in range(2):
                    last = nc.vector.tensor_tensor(silu_g[:, m, :], ps[banks[m]][:, 0:T], sin, ALU.mult)
                link(last)
                last = nc.vector.tensor_tensor(z[:], z[:], silu_g[:], ALU.add)
                if signal:
                    last.then_inc(ev(signal), 1)
                else:
                    link(last)

            def even_mixer(i):
                dve.wait_ge(ev("even_in"), 1)
                nc.vector.tensor_tensor(sq[:, 0:2, :], cq[:], cq[:], ALU.mult)
                nc.vector.tensor_tensor(sq[:, 2, :], ckv[:], ckv[:], ALU.mult).then_inc(ev("latent_sq"), 1)
                dve.wait_ge(ev("even_landed"), 64)
                dve.wait_ge(ev("latent_r"), 1)
                q_norm = even("q_norm")
                for m in range(2):
                    nc.vector.scalar_tensor_tensor(out=cq[:, m, :], in0=cq[:, m, :], scalar=q_norm[:, m:m + 1],
                                                   in1=var[:], op0=ALU.mult, op1=ALU.mult)
                nc.vector.scalar_tensor_tensor(out=lat[:], in0=ckv[:], scalar=even("kv_norm"), in1=rstd[:],
                                               op0=ALU.mult, op1=ALU.mult).then_inc(ev("latents"), 1)
                dve.wait_ge(ev("swapped_r"), 1)
                rotate(rq, (1, 3), even("cos_r"), even("sin_r"), None)
                rotate(rk, (2, 4), even("cos_r"), even("sin_r"), "rotated_r")
                dve.wait_ge(xnew_done, KD * i)
                dve.wait_ge(ev("rotated_r"), 1)
                for a in range(HR):
                    last = nc.vector.tensor_tensor(q_lead[:, a, :].rearrange("p (b t) -> p b t", t=TS), samples(rq[:, a // 2, :]),
                                                   lead_c[:, a, :].unsqueeze(1).to_broadcast([P, NSEQ, TS]), ALU.mult)
                link(last)
                dve.wait_ge(ev("swapped_m"), 1)
                rotate(qr, (5, 6), even("cos_m"), even("sin_m"), None)
                nc.vector.tensor_tensor(silu_g[:, 0, :], ps[7][:, 0:T], even("cos_m"), ALU.mult)
                link(nc.vector.tensor_tensor(silu_g[:, 1, :], ps[0][:, 0:T], even("sin_m"), ALU.mult))
                link(nc.vector.tensor_tensor(kr_rot[:], silu_g[:, 0, :], silu_g[:, 1, :], ALU.add))
                for m in range(4):
                    last = nc.vector.tensor_scalar(kr4[:, m, :], kr_rot[:], even("rows")[:, m:m + 1], None, ALU.mult)
                last.then_inc(ev("rotated_m"), 1)

                dve.wait_ge(ev("ret_k_turned"), 1)
                for t, (_, size) in enumerate(TOK):
                    last = nc.vector.tensor_tensor(ktail[0:size, t, :].rearrange("p (a k) -> p a k", k=DKR),
                                                   ps[1 + t][0:size, 0:HR * DKR].rearrange("p (a k) -> p a k", k=DKR),
                                                   spread(tail_c[0:size, t, :], DKR), ALU.mult)
                last.then_inc(ev("ret_k_tail"), 1)
                for a in range(HR):
                    dve.wait_ge(ev("ret_scores"), a + 1)
                    if a >= 2:
                        dve.wait_ge(ev("ret_o"), a - 1)
                    nc.vector.tensor_tensor(scores[:, a % 2, 0:3 * P], ps[4 + a % 2][:, 0:3 * P], decay_p[:, a, :], ALU.mult)
                    nc.vector.tensor_tensor(scores[0:NS, a % 2, 3 * P:], ps[4 + a % 2][0:NS, 3 * P:3 * P + NS],
                                            decay_s[0:NS, a, :], ALU.mult).then_inc(ev("ret_decayed"), 1)
                dve.wait_ge(ev("ret_state"), 1)
                nc.vector.tensor_copy(state_p[:].rearrange("p a n -> p (a n)"), ps[0][:, 0:2 * DVR])\
                  .then_inc(ev("ret_state_out"), 1)
                for a in range(HR):
                    dve.wait_ge(ev("ret_state_add"), a + 1)
                    for half in range(2):
                        st = state_r[rows64(a), 4 * half:4 * half + 4, a // 2, :]
                        last = nc.vector.scalar_tensor_tensor(
                            out=st, in0=st, scalar=float(GAMMA[a] ** TS),
                            in1=ps[5 + half][rows64(a), :].rearrange("p (b n) -> p b n", n=DVR),
                            op0=ALU.mult, op1=ALU.add)
                    last.then_inc(ev("ret_state_new"), 1)
                dve.wait_ge(ev("ret_r"), 1)
                for a in range(HR):
                    link(nc.vector.scalar_tensor_tensor(out=ro[:, a, :], in0=ro[:, a, :], scalar=even("ret_norm"),
                                                        in1=ro_r[a], op0=ALU.mult, op1=ALU.mult))
                nc.vector.tensor_tensor(mix[:, 4:8, :], ro[:], sgr[:], ALU.mult).then_inc(ev("ret_done"), 1)

                def prompt_max(a):
                    dve.wait_ge(ev("prompt_scores"), a + 1)
                    if a >= 2:
                        dve.wait_ge(ev("prompt_turned"), a - 1)
                    pr, u = prob[:, a % 2, :], a % 2
                    nc.vector.scalar_tensor_tensor(out=pr, in0=ps[2 + a % 2][:, 0:3 * P], scalar=ATT_SCALE,
                                                   in1=even("mask_p"), op0=ALU.mult, op1=ALU.add)\
                      .then_inc(ev("prompt_masked"), 1)
                    dve.wait_ge(ev("prompt_masked"), a + 1)
                    nc.vector.tensor_reduce(stat[:, u, 0:1], pr[:, 0:P], AX_X, ALU.max)
                    link(nc.vector.tensor_reduce(stat[:, u, 1:2], pr[:, P:3 * P], AX_X, ALU.max))
                    nc.vector.tensor_scalar(stat[:, u, :], stat[:, u, :], -1.0, None, ALU.mult)\
                      .then_inc(ev("prompt_max"), 1)

                def prompt_norm(a):
                    dve.wait_ge(ev("prompt_exp"), a + 1)
                    pr, u = prob[:, a % 2, :], a % 2
                    link(nc.vector.reciprocal(stat[:, 2 + u, :], stat[:, 2 + u, :]))
                    nc.vector.tensor_scalar(pr[:, 0:P], pr[:, 0:P], stat[:, 2 + u, 0:1], None, ALU.mult)
                    nc.vector.tensor_scalar(pr[:, P:3 * P], pr[:, P:3 * P], stat[:, 2 + u, 1:2], None, ALU.mult)\
                      .then_inc(ev("prompt_norm"), 1)

                prompt_max(0)
                prompt_max(1)
                prompt_norm(0)
                for a in range(1, HM):
                    prompt_norm(a)
                    if a + 1 < HM:
                        prompt_max(a + 1)

                dve.wait_ge(ev("q_lat_copied"), HM)
                nc.vector.tensor_copy(q_ls[:].rearrange("p b (a t) -> p b a t", t=TS),
                                      q_lat[:, :, TP:T].rearrange("p a (b t) -> p b a t", t=TS))
                nc.vector.memset(q_rs[32:64], 0.0)
                nc.vector.memset(prob_st[:, NPAGES:NPAGES + 2, :], 0.0).then_inc(ev("turned_clear"), 1)
                for a in range(HM):
                    last = nc.vector.tensor_copy(
                        q_rs[0:ROPE].rearrange("p b (a t) -> p b a t", t=TS)[:, :, a, :],
                        qr[ROPE * (a % 4):ROPE * (a % 4 + 1), a // 4, TP:T].rearrange("p (b t) -> p b t", t=TS))
                last.then_inc(ev("sample_q"), 1)

                def sample_max(b):
                    dve.wait_ge(ev("sample_scores"), b + 1)
                    if b >= 2:
                        dve.wait_ge(ev("sample_turned"), b - 1)
                    u = b % 2
                    st, new = stat_s[:, u, :], prob_s[0:NS, u, PAST // 2:]
                    nc.vector.tensor_reduce(st[:, 0:1], ps[2 + u][:], AX_X, ALU.max)
                    link(nc.vector.tensor_tensor(new, ps[1 + 6 * u][0:NS, 0:NS], mask_s[0:NS, b, :], ALU.add))
                    nc.vector.tensor_copy(st[0:NS, 1:2], st[NS:P, 0:1])
                    link(nc.vector.tensor_reduce(st[0:NS, 2:3], new, AX_X, ALU.max))
                    link(nc.vector.tensor_reduce(st[0:NS, 3:4], st[0:NS, 0:3], AX_X, ALU.max))
                    for half in range(2):
                        last = nc.vector.tensor_scalar(st[rows64(half), 4:5], st[0:NS, 3:4], -ATT_SCALE, None, ALU.mult)
                    last.then_inc(ev("sample_max"), 1)

                def sample_inverse(b):
                    dve.wait_ge(ev("sample_exp"), b + 1)
                    st = stat_s[:, b % 2, :]
                    link(nc.vector.tensor_copy(st[0:NS, 6:7], st[NS:P, 5:6]))
                    link(nc.vector.tensor_reduce(st[0:NS, 8:9], st[0:NS, 5:8], AX_X, ALU.add))
                    link(nc.vector.reciprocal(st[0:NS, 8:9], st[0:NS, 8:9]))
                    link(nc.vector.tensor_copy(st[NS:P, 8:9], st[0:NS, 8:9]))
                    nc.vector.tensor_scalar(inverse[:, b % 2, :], ident[:], st[:, 8:9], None, ALU.mult)\
                      .then_inc(ev("sample_inverse"), 1)

                sample_max(0)
                sample_max(1)
                sample_inverse(0)
                for b in range(1, NSEQ):
                    sample_inverse(b)
                    if b + 1 < NSEQ:
                        sample_max(b + 1)
                out_residual(i)

            def odd_mixer(i):
                dve.wait_ge(ev("odd_landed"), 48)
                nc.vector.memset(dtx[:], 0.0).then_inc(ev("dt_clear"), 1)
                nc.vector.memset(xpad[:, :, 0:CONV - 1], 0.0)
                nc.vector.tensor_copy(xpad[:, :, WP:].rearrange("p f (b t) -> p f b t", t=WS)[:, :, :, 0:CONV - 1], hist[:])
                nc.vector.memset(s_pair[:], 0.0)
                link(nc.vector.memset(s_samp[:], 0.0))
                dve.wait_ge(ev("small_copied"), 1)
                nc.vector.tensor_tensor(dtx[:], dtx[:], odd("dt_bias").unsqueeze(1).to_broadcast([P, NTOK, HS]), ALU.add)\
                  .then_inc(ev("dt_biased"), 1)
                dve.wait_ge(ev("dt_exp"), 1)
                link(nc.vector.tensor_scalar(dts[:], dtu[:], 2.0, None, ALU.add))
                link(nc.vector.reciprocal(dts[:], dts[:]))
                link(nc.vector.tensor_tensor(dts[:], dts[:], dtu[:], ALU.mult))
                link(nc.vector.tensor_tensor(dtu[:], dts[:], dts[:], ALU.mult))
                link(nc.vector.tensor_scalar(dtp[:], dtu[:], 1.0 / 15, None, ALU.mult))
                for k in (13, 11, 9, 7, 5, 3):
                    link(nc.vector.scalar_tensor_tensor(out=dtp[:], in0=dtp[:], scalar=1.0 / k, in1=dtu[:],
                                                        op0=ALU.add, op1=ALU.mult))
                link(nc.vector.scalar_tensor_tensor(out=dtp[:], in0=dtp[:], scalar=1.0, in1=dts[:],
                                                    op0=ALU.add, op1=ALU.mult))
                link(nc.vector.tensor_scalar(dtx[:], dtx[:], 0.0, None, ALU.max))
                link(nc.vector.scalar_tensor_tensor(out=dt[:], in0=dtp[:], scalar=2.0, in1=dtx[:],
                                                    op0=ALU.mult, op1=ALU.add))
                link(nc.vector.scalar_tensor_tensor(out=ua[:], in0=dt[:], scalar=-1.0,
                                                    in1=e_a[:].unsqueeze(1).to_broadcast([P, NTOK, HS]),
                                                    op0=ALU.mult, op1=ALU.mult))
                dve.wait_ge(ev("gate_log"), 1)
                link(nc.vector.scalar_tensor_tensor(out=gla[:], in0=gla[:], scalar=0.0, in1=ge[:],
                                                    op0=ALU.min, op1=ALU.subtract))
                for m in range(2):
                    last = nc.vector.tensor_tensor_scan(seg[:, m, :], odd("restart"), gla[:, m, :], 0.0, ALU.mult, ALU.add)
                link(last)

                def level_diff(k):
                    half = HALVES[k]
                    w = TP if half >= TS else T
                    v = seg[:, :, 0:w].rearrange("p m (n l) -> p m n l", l=2 * half)
                    nc.vector.tensor_tensor(ge[:, :, 0:w].rearrange("p m (n l) -> p m n l", l=2 * half), v,
                                            v[:, :, :, half - 1:half].to_broadcast([P, 2, w // (2 * half), 2 * half]),
                                            ALU.subtract).then_inc(ev("level_diff"), 1)

                def level_qk(k):
                    if k:
                        dve.wait_ge(ev("level_made"), k)
                    w = TP if HALVES[k] >= TS else T
                    dve.wait_ge(ev("level_exp"), k + 1)
                    nc.vector.tensor_tensor(qe[:, :, 0:w], gq[:, :, 0:w], ge[:, :, 0:w], ALU.mult)
                    nc.vector.tensor_tensor(ke[:, :, 0:w], gk[:, :, 0:w], ge[:, :, 0:w], ALU.mult)\
                      .then_inc(ev("level_qk"), 1)

                level_diff(0)
                level_qk(0)
                for k, half in enumerate(HALVES):
                    if k + 1 < len(HALVES) and HALVES[k + 1]:
                        dve.wait_ge(ev("level_qk"), k + 1)
                        level_diff(k + 1)
                        level_qk(k + 1)
                    elif half:
                        dve.wait_ge(ev("level_made"), k + 1)
                        nc.vector.memset(q_exp[:], 0.0).then_inc(ev("level_qk"), 1)
                    dve.wait_ge(ev("level_made"), k + 1)
                    pick = levels[:, k, :].bitcast(U32)
                    for e in range(2):
                        last = nc.vector.copy_predicated(s_pair[:, e], pick.unsqueeze(1).to_broadcast([P, 4, P]),
                                                         ps[6 + e][:].rearrange("p (a n) -> p a n", n=P))
                    if half < TS:
                        pick = levels[0:NS, k, 0:NS].bitcast(U32)
                        for e in range(2):
                            last = nc.vector.copy_predicated(s_samp[0:NS, e], pick.unsqueeze(1).to_broadcast([NS, 2, NS]),
                                                             ps[3 * e][0:NS, 0:2 * NS].rearrange("p (a n) -> p a n", n=NS))
                    last.then_inc(ev("level_picked"), 1)
                dve.wait_ge(ev("level_picked"), len(HALVES))
                for w0, w1, n in ((0, TP, P), (TP, T, TS)):
                    v = seg[:, :, w0:w1].rearrange("p m (n l) -> p m n l", l=n)
                    last = nc.vector.tensor_tensor(ge[:, :, w0:w1].rearrange("p m (n l) -> p m n l", l=n),
                                                   v[:, :, :, n - 1:n].to_broadcast([P, 2, (w1 - w0) // n, n]), v, ALU.subtract)
                last.then_inc(ev("tail_diff"), 1)
                dve.wait_ge(ev("gla_exps"), 1)
                nc.vector.tensor_tensor(ke[:], gk[:], ge[:], ALU.mult).then_inc(ev("gla_tail"), 1)
                for a in range(HR):
                    r, m = rows64(a), a // 2
                    last = nc.vector.tensor_tensor(q_exp[r, a, :], gq[r, m, P:T], qe[r, m, P:T], ALU.mult)
                dve.wait_ge(ev("gla_state"), 1)
                nc.vector.tensor_copy(st1[:].rearrange("p a n -> p (a n)"), ps[0][:, 0:2 * DVR]).then_inc(ev("gla_state1"), 1)
                dve.wait_ge(ev("gla_state1"), 1)
                for m in range(2):
                    last = nc.vector.scalar_tensor_tensor(out=st2[:, m, :], in0=st1[:, m, :], scalar=qe[:, m, TP - 1:TP],
                                                          in1=ps[3][:, m * DVR:(m + 1) * DVR], op0=ALU.mult, op1=ALU.add)
                last.then_inc(ev("gla_state2"), 1)
                dve.wait_ge(ev("gla_o"), HR)
                ends = qe[:, :, TP:T].rearrange("p m (b t) -> p b m t", t=TS)[:, :, :, TS - 1:TS]
                link(nc.vector.tensor_tensor(state_g[:], state_g[:], ends.to_broadcast([P, NSEQ, 2, DVR]), ALU.mult))
                for a in range(HR):
                    dve.wait_ge(ev("gla_state_add"), a + 1)
                    for half in range(2):
                        st = state_g[rows64(a), 4 * half:4 * half + 4, a // 2, :]
                        last = nc.vector.tensor_tensor(st, st, ps[5 + half][rows64(a), :].rearrange("p (b n) -> p b n", n=DVR),
                                                       ALU.add)
                    last.then_inc(ev("gla_state_new"), 1)
                dve.wait_ge(ev("gla_r"), 1)
                for a in range(HR):
                    last = nc.vector.scalar_tensor_tensor(out=go[:, a, :], in0=go[:, a, :], scalar=odd("gla_norm"),
                                                          in1=ro_r[a], op0=ALU.mult, op1=ALU.mult)
                link(last)
                dve.wait_ge(ev("odd_in"), 8)
                nc.vector.tensor_copy(conv_state[:, :, 0, :], xpad[:, :, WP - CONV + 1:WP])
                nc.vector.tensor_copy(conv_state[:, :, 1:NC, :],
                                      xpad[:, :, WP:].rearrange("p f (b t) -> p f b t", t=WS)[:, :, :, TS:WS])\
                  .then_inc(ev("conv_state"), 1)
                nc.vector.tensor_tensor(mix3[:, 0:4, :], go[:], gr[:], ALU.mult).then_inc(ev("gla_done"), 1)

                for f in range(NXC):
                    dve.wait_ge(ev("conv_first"), f + 1)
                    for k in range(1, CONV):
                        last = nc.vector.scalar_tensor_tensor(out=acc[f % 2], in0=xpad[:, f, k:k + CONV_OUT],
                                                              scalar=conv_w[:, k, f:f + 1], in1=acc[f % 2],
                                                              op0=ALU.mult, op1=ALU.add)
                        if k < CONV - 1:
                            link(last)
                    last.then_inc(ev("conv_added"), 1)
                for t, (_, size) in enumerate(TOK):
                    dve.wait_ge(ev("xs_turned"), t + 1)
                    dve.wait_ge(ev("bn_copied"), t + 1)
                    for g in range(GROUPS):
                        last = nc.vector.tensor_tensor(
                            xdt[0:size, t, g * 512:(g + 1) * 512].rearrange("p (a n) -> p a n", n=HDIM),
                            ps[1 + g][0:size, :].rearrange("p (a n) -> p a n", n=HDIM),
                            spread(dt[0:size, t, g * 8:(g + 1) * 8], HDIM), ALU.mult)
                    last.then_inc(ev("xs_copied"), 1)
                for t, (t0, size) in enumerate(TOK):
                    upto = odd("upto") if t < 2 else odd("upto_s")[0:NS, :]
                    if t:
                        dve.wait_ge(ev("decay_made"), DECAYS[t])
                    else:
                        dve.wait_ge(ev("conv_done"), NXC)
                    nc.vector.tensor_tensor(steps_of(t)[0:size], spread(ua[0:size, t, :], size),
                                            upto.unsqueeze(1).to_broadcast([size, HS, size]), ALU.mult)\
                      .then_inc(ev("steps"), 1)
                    dve.wait_ge(ev("bc_made"), t + 1)
                    link(nc.vector.tensor_tensor(gm[0:size, :, 0:size],
                                                 ps[7][0:size, 0:2 * size].rearrange("p (a n) -> p a n", n=size),
                                                 upto.unsqueeze(1).to_broadcast([size, 2, size]), ALU.mult))
                    dve.wait_ge(ev("tails"), t + 1)
                    if t == 2:
                        link(nc.vector.tensor_copy(dec_s[:].rearrange("p b a -> p a b"),
                                                   c_exp_s.rearrange("p a (b t) -> p a b t", t=TS)[:, :, :, TS - 1]))
                    for g in range(GROUPS):
                        hs = slice(8 * g, 8 * g + 8)
                        last = nc.vector.tensor_tensor(att_of(t)[0:size, hs, :], att_of(t)[0:size, hs, :],
                                                       gm[0:size, g, 0:size].unsqueeze(1).to_broadcast([size, 8, size]), ALU.mult)
                        if t:
                            ce = sized(c_exp, t)[:, hs, :]
                            last = nc.vector.tensor_tensor(ce, ce, xc[:, NXS + GROUPS + g, t0:t0 + size].unsqueeze(1)
                                                           .to_broadcast([P, 8, size]), ALU.mult)
                    last.then_inc(ev("att_ready"), 1)
                    if t:
                        dve.wait_ge(ev("ssm_add"), t)
                    nc.vector.tensor_tensor(xdt_tail[0:size, :].rearrange("p (a n) -> p a n", n=HDIM),
                                            xdt[0:size, t, :].rearrange("p (a n) -> p a n", n=HDIM),
                                            spread(tails[0:size, :], HDIM), ALU.mult).then_inc(ev("tail_ready"), 1)
                    dve.wait_ge(ev("ssd_y"), t + 1)
                    for f in range(NXS):
                        last = nc.vector.scalar_tensor_tensor(
                            out=xc[:, f, t0:t0 + size], in0=xc[:, f, t0:t0 + size], scalar=odd("d_skip")[:, f:f + 1],
                            in1=ps[1 + f // 4][:, (f % 4) * size:(f % 4 + 1) * size], op0=ALU.mult, op1=ALU.add)
                    last.then_inc(ev("y_kept"), 1)
                    if t < 2:
                        dve.wait_ge(ev("ssm_add"), t + 1)
                        if t:
                            link(nc.vector.tensor_tensor(ssm1[:].rearrange("p (a n) -> p a n", n=HDIM),
                                                         ssm1[:].rearrange("p (a n) -> p a n", n=HDIM),
                                                         spread(dec_p[:], HDIM), ALU.mult))
                        for g in range(GROUPS):
                            part = ssm1[:, g * 512:(g + 1) * 512]
                            if t:
                                last = nc.vector.tensor_tensor(part, part, ps[3 + g][:], ALU.add)
                            else:
                                last = nc.vector.tensor_copy(part, ps[3 + g][:])
                        last.then_inc(ev("ssm1_kept"), 1)
                nc.vector.tensor_tensor(b_masked[0:NS], bn[0:NS, 2, :].unsqueeze(1).to_broadcast([NS, NSEQ, GROUPS * DSTATE]),
                                        spread(sample_of[0:NS, :], GROUPS * DSTATE), ALU.mult).then_inc(ev("b_masked"), 1)
                for b in range(NSEQ):
                    dve.wait_ge(ev("ssm_add_s"), b + 1)
                    st = ssm_of(b)
                    link(nc.vector.tensor_tensor(st.rearrange("p (a n) -> p a n", n=HDIM),
                                                 st.rearrange("p (a n) -> p a n", n=HDIM),
                                                 spread(dec_s[:, b, :], HDIM), ALU.mult))
                    for g in range(GROUPS):
                        last = nc.vector.tensor_tensor(st[:, g * 512:(g + 1) * 512], st[:, g * 512:(g + 1) * 512],
                                                       ps[3 + 2 * (b % 2) + g][:], ALU.add)
                    last.then_inc(ev("ssm_new"), 1)
                dve.wait_ge(ev("y_kept"), NTOK)
                link(nc.vector.tensor_tensor(xc[:, 0:NXS, TP:T], xc[:, 0:NXS, TP:T],
                                             ps[7][:].rearrange("p (f n) -> p f n", n=NS), ALU.add))
                link(nc.vector.tensor_tensor(xc[:, 0:NXS, :], xc[:, 0:NXS, :], zs[:], ALU.mult))
                nc.vector.tensor_tensor(ysq[:], xc[:, 0:NXS, :], xc[:, 0:NXS, :], ALU.mult).then_inc(ev("gated_sq"), 1)
                dve.wait_ge(ev("ssd_r"), 1)
                for f in range(NXS):
                    last = nc.vector.scalar_tensor_tensor(out=mix3[:, 4 + f, :], in0=xc[:, f, :],
                                                          scalar=odd("ssm_norm")[:, f:f + 1], in1=ro_r[f // 4],
                                                          op0=ALU.mult, op1=ALU.mult)
                last.then_inc(ev("mix3_ready"), 1)
                out_residual(i)

            def out_residual(i):
                tiles = KD // N_OUT[i]
                dve.wait_ge(xnew_done, KD * i)
                for k in range(KD):
                    if k % tiles == tiles - 1:
                        dve.wait_ge(w_done, OUT0[i] + k // tiles + 1)
                    else:
                        dve.wait_ge(out_tile, OUT_TILE0[i] + k // tiles * (tiles - 1) + k % tiles + 1)
                    residual(i, k, 0)

            dve.wait_ge(s_load, 32)
            prepare(0)
            for i in range(NBLK):
                if i == MIXERS[0]:
                    even_mixer(i)
                elif i == MIXERS[1]:
                    odd_mixer(i)
                else:
                    ffn(i)
                norm(i)
                if i + 1 < NBLK:
                    prepare(i + 1)


def kernel(**inputs):
    import numpy as _np
    import concourse.bacc as _bacc
    from concourse import mybir as _mybir
    from concourse.bass_utils import run_bass_kernel_spmd as _run

    a = {k: _np.asarray(v) for k, v in inputs.items()}

    def slots_of(w, width):
        *lead, k, n = w.shape
        w = w.reshape(-1, k // P, P, n // width, width)
        return _np.ascontiguousarray(w.transpose(0, 3, 2, 1, 4)).reshape(-1, P, k // P * width)

    def features(w):
        w = w.reshape(*w.shape[:-1], w.shape[-1] // P, P)
        return _np.moveaxis(w, -1, 0).reshape(P, -1)

    tokens = _np.concatenate([a["x_prompt"].reshape(TP, D), a["x_sample"].reshape(NSEQ * TS, D)])
    cond = _np.concatenate([a["c_prompt"], a["c_sample"]])
    up = _np.stack([slots_of(a["ffn_w1"].reshape(4, D, FF), 2 * P), slots_of(a["ffn_w3"].reshape(4, D, FF), 2 * P)], 2)
    arrays = {
        "xT": tokens.T.reshape(KD, P, T).transpose(1, 0, 2),
        "params": _np.concatenate([features(a["ln_g"].reshape(NBLK, D)), features(a["ln_b"].reshape(NBLK, D)),
                                   features(a["b_ada"].reshape(NBLK, 3 * D)),
                                   cond.T.reshape(KD, P, NC).transpose(1, 0, 2).reshape(P, -1)], 1),
        "w_ada": slots_of(a["w_ada"], 512),
        "w_up": up.reshape(-1, P, SLOT),
        "w_down": slots_of(a["ffn_w2"].reshape(4, FF, D), P),
    }
    add_turn = _np.zeros((P, WIDE), _np.float32)
    for c in range(NC):
        add_turn[c::32, c] = 1.0
    arrays["add_turn"] = add_turn
    uq = a["w_uq"][0].reshape(QRANK, HM, NOPE + ROPE)
    uq = _np.concatenate([uq[:, :, :NOPE].reshape(QRANK, -1), uq[:, :, NOPE:].reshape(QRANK, -1)], 1)
    given = even_constants()
    given["w_uq"] = uq.reshape(2, P, -1).transpose(1, 0, 2)
    given["w_uk"] = a["w_uk"][0].reshape(RANK, HM // 2, 2 * NOPE).transpose(2, 1, 0)
    given["w_uv"] = a["w_uv"][0].reshape(RANK, HM * VM)
    given["q_norm"], given["kv_norm"] = features(a["mla_q_norm"][0]), features(a["mla_kv_norm"][0])
    given["ret_norm"] = features(a["ret_norm"][0])
    arrays["even_consts"] = _np.concatenate([given[k].reshape(P, -1) for k in EVEN_CONSTS], 1)
    w = a["w_in_even"][0]
    w = _np.concatenate([w[:, :416], w[:, 320:416], w[:, 416:]], 1)
    arrays["w_in_even"] = slots_of(w, 512)
    arrays["w_out_even"] = slots_of(a["w_out_even"][0], 512)
    lat = a["cache_mla_latent"][0]
    rope = a["cache_mla_krope"][0].transpose(0, 2, 1)
    rope = _np.concatenate([rope, _np.zeros((rope.shape[0], P - ROPE, PAGE), rope.dtype)], 1)
    arrays["cache"] = _np.concatenate([lat.transpose(0, 2, 1), lat, rope], 2)
    arrays["pages"] = a["page_table"].reshape(1, -1)
    arrays["ident"] = _np.eye(P, dtype=_np.float32)
    arrays["sample_of"] = (_np.arange(P)[:, None] // TS == _np.arange(NSEQ)[None, :]).astype(_np.float32)

    def state(s):
        return s.reshape(NSEQ, 2, 2, DKR, DVR).transpose(2, 3, 0, 1, 4).reshape(P, NSEQ, 2, DVR)

    def state_back(s):
        s = s.reshape(2, DKR, -1, 2, DVR)
        return s.transpose(2, 3, 0, 1, 4).reshape(1, -1, HR, DKR, DVR)
    arrays["state_r"] = state(a["state_retention"][0])
    given = odd_constants()
    w = a["w_in_odd"][0]
    low, rest, dts = w[:, 1024:1040], _np.concatenate([w[:, :1024], w[:, 1040:4112]], 1), w[:, 4112:]
    arrays["w_in_odd"] = slots_of(rest, 512)
    arrays["w_out_odd"] = slots_of(a["w_out_odd"][0], 2 * P)
    given["w_small"] = _np.concatenate([low, dts], 1).reshape(KD, P, 2 * GATE_RANK).transpose(1, 0, 2)
    given["w_gate"] = _np.concatenate([a["gla_w_gate"][0], _np.zeros((P - GATE_RANK, HR * DKR), _np.float32)])
    given["b_gate"], given["gla_norm"] = features(a["gla_b_gate"][0]), features(a["gla_norm"][0])
    given["conv_w"], given["conv_b"] = features(a["ssm_conv_w"][0]), features(a["ssm_conv_b"][0])
    given["dt_bias"] = _np.broadcast_to(a["ssm_dt_bias"][0], (P, HS))
    given["a_log"] = _np.broadcast_to(a["ssm_a_log"][0], (P, HS))
    given["d_skip"] = features(_np.repeat(a["ssm_d"][0], HDIM))
    given["ssm_norm"] = features(a["ssm_norm"][0])
    arrays["odd_consts"] = _np.concatenate([given[k].reshape(P, -1) for k in ODD_CONSTS], 1)
    arrays["state_g"] = state(a["state_gla"][0])
    ssm = a["state_ssm"][0].transpose(0, 2, 1, 3).reshape(-1, PER_STATE, DSTATE, INNER)
    arrays["state_ssm"] = ssm.transpose(0, 2, 1, 3).reshape(-1, DSTATE, PER_STATE * INNER)
    arrays["conv_hist"] = a["state_conv"][0].reshape(NSEQ, CONV - 1, NXC, P).transpose(3, 2, 0, 1)
    outs = {"out_gla_p": (P, HR // 2, DVR), "out_gla_s": (P, NSEQ, HR // 2, DVR), "out_ssm_p": (P, INNER),
            "out_ssm_s": (NSEQ, P, INNER), "out_conv": (P, NXC, NC, CONV - 1), "out_lat": (P, T), "out_krope": (ROPE, T), "out_ret_p": (P, HR // 2, DVR),
            "out_ret_s": (P, NSEQ, HR // 2, DVR), "yT": (P, KD, T)}
    nc = _bacc.Bacc("TRN2", target_bir_lowering=False, num_devices=1)
    arrays = {k: _np.ascontiguousarray(v) for k, v in arrays.items()}
    dram = {k: nc.dram_tensor(f"dram_{k}", v.shape, _mybir.dt.from_np(v.dtype), kind="ExternalInput").ap()
            for k, v in arrays.items()}
    for k, shape in outs.items():
        dram[k] = nc.dram_tensor(f"dram_{k}", shape, F32, kind="ExternalOutput").ap()
    build(nc, dram)
    r = _run(nc, [{f"dram_{k}": v for k, v in arrays.items()}], core_ids=[0]).results[0]
    def tokens_back(v):
        v = v.T
        return v[:TP][None], v[TP:].reshape(NSEQ, TS, -1)

    y_p, y_s = tokens_back(r["dram_yT"].transpose(1, 0, 2).reshape(D, T))
    lat_p, lat_s = tokens_back(r["dram_out_lat"])
    kr_p, kr_s = tokens_back(r["dram_out_krope"])
    conv = r["dram_out_conv"].transpose(2, 3, 1, 0).reshape(1, NC, CONV - 1, NXC * P)
    ssm_p = r["dram_out_ssm_p"].reshape(1, 1, DSTATE, HS, HDIM).transpose(0, 1, 3, 2, 4)
    ssm_s = r["dram_out_ssm_s"].reshape(1, NSEQ, DSTATE, HS, HDIM).transpose(0, 1, 3, 2, 4)
    return (y_p, y_s, lat_p[None], lat_s[None], kr_p[None], kr_s[None],
            state_back(r["dram_out_ret_p"]), state_back(r["dram_out_ret_s"]),
            state_back(r["dram_out_gla_p"]), state_back(r["dram_out_gla_s"]), ssm_p, ssm_s, conv[:, :1], conv[:, 1:])
```
